# Optimizing a Trainium2 kernel written in Bass

```python
import jax, jax.numpy as jnp
from jax import lax
import numpy as np

D_MODEL = 1024
BATCH = 1
SEQ = 256
DEPTH = 2

D_POOL = D_MODEL // 2
POOL_WINDOWS = (2, 4, 8, 16)
N_POOL_GROUPS = len(POOL_WINDOWS)
POOL_GROUP = D_POOL // N_POOL_GROUPS
D_ATTN = D_MODEL // 2
HEAD_DIM = 64
N_HEADS = D_ATTN // HEAD_DIM
DILATED_PATTERNS = ((128, 1), (512, 4), (2048, 16))
Q_BLOCK = 128
D_IN = D_POOL + 3 * D_ATTN
D_FF = 2816
N_EXPERTS = 8
TOP_K = 2
D_FF_EXPERT = 3584
EPS = 1e-6
N_DENSE = (DEPTH + 1) // 2
N_MOE = DEPTH // 2


def rmsnorm(x, g):
    xf = x.astype(jnp.float32)
    y = xf * lax.rsqrt(jnp.mean(xf * xf, axis=-1, keepdims=True) + EPS)
    return (y * g.astype(jnp.float32)).astype(x.dtype)

def pool_mixer(u, w_pool, pool_scale):
    B, S, _ = u.shape
    uf = u.astype(jnp.float32)
    c = jnp.concatenate([jnp.zeros((B, 1, D_POOL), jnp.float32), jnp.cumsum(uf, axis=1)], axis=1)
    t = jnp.arange(S)
    diffs = []
    for gi, w in enumerate(POOL_WINDOWS):
        sl = slice(gi * POOL_GROUP, (gi + 1) * POOL_GROUP)
        cg = c[..., sl]
        lo = jnp.maximum(t + 1 - w, 0)
        win_sum = cg[:, 1:] - cg[:, lo]
        cnt = (t + 1 - lo).astype(jnp.float32)[None, :, None]
        diffs.append(win_sum / cnt - uf[..., sl])
    d = jnp.stack(diffs, axis=2).astype(u.dtype)
    z = jnp.einsum('bsgc,gce->bsge', d, w_pool).reshape(B, S, D_POOL)
    return rmsnorm(z, pool_scale)

def dilated_attention(q, k, v):
    B, H, S, Dh = q.shape
    nb = S // Q_BLOCK
    scale = HEAD_DIM ** -0.5
    qb = q.reshape(B, H, nb, Q_BLOCK, Dh).transpose(2, 0, 1, 3, 4)

    def block(args):
        bi, qblk = args
        pos = bi * Q_BLOCK + jnp.arange(Q_BLOCK)
        outs, lses = [], []
        for window, dil in DILATED_PATTERNS:
            n_keys = window // dil + 1
            kidx = pos[:, None] - dil * jnp.arange(n_keys)[None, :]
            valid = kidx >= 0
            kidx = jnp.maximum(kidx, 0)
            kg = k[:, :, kidx]
            vg = v[:, :, kidx]
            s = jnp.einsum('bhqd,bhqjd->bhqj', qblk, kg).astype(jnp.float32) * scale
            s = jnp.where(valid[None, None], s, -jnp.inf)
            m = jnp.max(s, axis=-1, keepdims=True)
            p = jnp.exp(s - m)
            den = jnp.sum(p, axis=-1, keepdims=True)
            o = jnp.einsum('bhqj,bhqjd->bhqd', p, vg.astype(jnp.float32)) / den
            outs.append(o)
            lses.append(m + jnp.log(den))
        wts = jax.nn.softmax(jnp.concatenate(lses, axis=-1), axis=-1)
        o = jnp.einsum('bhqp,pbhqd->bhqd', wts, jnp.stack(outs, axis=0))
        return o.astype(q.dtype)

    ob = lax.map(block, (jnp.arange(nb), qb))
    return ob.transpose(1, 2, 0, 3, 4).reshape(B, H, S, Dh)

def hybrid_mixer(h, w_in, w_pool, pool_scale, attn_gain, w_out):
    B, S, _ = h.shape
    proj = h @ w_in
    u = proj[..., :D_POOL]
    q, k, v = jnp.split(proj[..., D_POOL:], 3, axis=-1)
    to_heads = lambda t: t.reshape(B, S, N_HEADS, HEAD_DIM).transpose(0, 2, 1, 3)
    y_a = pool_mixer(u, w_pool, pool_scale)
    o = dilated_attention(to_heads(q), to_heads(k), to_heads(v))
    y_b = rmsnorm(o.transpose(0, 2, 1, 3).reshape(B, S, D_ATTN), attn_gain)
    return jnp.concatenate([y_a, y_b], axis=-1) @ w_out

def swiglu(h, wg, wu, wd):
    return (jax.nn.silu(h @ wg) * (h @ wu)) @ wd

def moe_swiglu(h, w_router, wg, wu, wd):
    B, S, D = h.shape
    xt = h.reshape(-1, D)
    logits = (xt @ w_router).astype(jnp.float32)
    top_v, top_i = lax.top_k(logits, TOP_K)
    gates = jax.nn.softmax(top_v, axis=-1)
    gate = jnp.sum(jax.nn.one_hot(top_i, N_EXPERTS, dtype=jnp.float32) * gates[..., None], axis=1)
    y = jnp.zeros_like(xt)
    for e in range(N_EXPERTS):
        y = y + gate[:, e:e + 1].astype(xt.dtype) * swiglu(xt, wg[e], wu[e], wd[e])
    return y.reshape(B, S, D)

def first_inputs(seed: int = 0) -> dict:
    key = jax.random.key(seed)
    ks = jax.random.split(key, 20)
    f32 = jnp.float32
    nrm = lambda k, shape, fan_in: jax.random.normal(k, shape, f32) * (fan_in ** -0.5)
    gain = lambda k, shape: 1.0 + 0.05 * jax.random.normal(k, shape, f32)
    return {
        "x": jax.random.normal(ks[0], (BATCH, SEQ, D_MODEL), f32),
        "norm_mix": gain(ks[1], (DEPTH, D_MODEL)),
        "w_in": nrm(ks[2], (DEPTH, D_MODEL, D_IN), D_MODEL),
        "w_pool": nrm(ks[3], (DEPTH, N_POOL_GROUPS, POOL_GROUP, POOL_GROUP), POOL_GROUP),
        "pool_scale": gain(ks[4], (DEPTH, D_POOL)),
        "attn_gain": gain(ks[5], (DEPTH, D_ATTN)),
        "w_out": nrm(ks[6], (DEPTH, D_MODEL, D_MODEL), D_MODEL),
        "norm_ffn": gain(ks[7], (DEPTH, D_MODEL)),
        "ffn_wg": nrm(ks[8], (N_DENSE, D_MODEL, D_FF), D_MODEL),
        "ffn_wu": nrm(ks[9], (N_DENSE, D_MODEL, D_FF), D_MODEL),
        "ffn_wd": nrm(ks[10], (N_DENSE, D_FF, D_MODEL), D_FF),
        "w_router": nrm(ks[11], (N_MOE, D_MODEL, N_EXPERTS), D_MODEL),
        "moe_wg": nrm(ks[12], (N_MOE, N_EXPERTS, D_MODEL, D_FF_EXPERT), D_MODEL),
        "moe_wu": nrm(ks[13], (N_MOE, N_EXPERTS, D_MODEL, D_FF_EXPERT), D_MODEL),
        "moe_wd": nrm(ks[14], (N_MOE, N_EXPERTS, D_FF_EXPERT, D_MODEL), D_FF_EXPERT),
        "final_norm": gain(ks[15], (D_MODEL,)),
    }

def first_block(x, norm_mix, w_in, w_pool, pool_scale, attn_gain, w_out, norm_ffn,
              ffn_wg, ffn_wu, ffn_wd, w_router, moe_wg, moe_wu, moe_wd, final_norm):
    for l in range(DEPTH):
        h = rmsnorm(x, norm_mix[l])
        x = x + hybrid_mixer(h, w_in[l], w_pool[l], pool_scale[l], attn_gain[l], w_out[l])
        h = rmsnorm(x, norm_ffn[l])
        if l % 2 == 0:
            i = l // 2
            x = x + swiglu(h, ffn_wg[i], ffn_wu[i], ffn_wd[i])
        else:
            i = l // 2
            x = x + moe_swiglu(h, w_router[i], moe_wg[i], moe_wu[i], moe_wd[i])
    return rmsnorm(x, final_norm)


D_MIX = D_MODEL
N_HEADS_A = 4
N_HEADS_B = 4
N_HEADS_C = D_MIX // HEAD_DIM - N_HEADS_A - N_HEADS_B
ROPE_DIM = HEAD_DIM // 4
ROPE_THETA = 500000.0
MOBA_BLOCK = 256
MOBA_TOPK = 3
DSA_TOPK = 256
IDX_HEADS = 8
IDX_DIM = 64
N_MOD = 9
RMS_EPS = 1e-6
NEG = -1e30


SPLIT_SIZES = (N_HEADS_A * HEAD_DIM, N_HEADS_A * HEAD_DIM, N_HEADS_A * HEAD_DIM,
               N_HEADS_B * HEAD_DIM, N_HEADS_B * HEAD_DIM, N_HEADS_B * HEAD_DIM,
               IDX_HEADS * IDX_DIM, IDX_DIM, IDX_HEADS,
               N_HEADS_C * HEAD_DIM, N_HEADS_C * HEAD_DIM, N_HEADS_C * HEAD_DIM)
D_IN_2 = sum(SPLIT_SIZES)

def _rms(x):
    xf = x.astype(jnp.float32)
    return (xf * lax.rsqrt(jnp.mean(xf * xf, axis=-1, keepdims=True) + RMS_EPS))

def rmsnorm_2(x, g):
    return (_rms(x) * g.astype(jnp.float32)).astype(x.dtype)

def modulate(h, shift, scale):
    return h * (1 + scale) + shift

def swiglu_2(h, w1, w3, w2):
    return (jax.nn.silu(h @ w1) * (h @ w3)) @ w2

def rope_tables(seq):
    pos = jnp.arange(seq, dtype=jnp.float32)
    inv = ROPE_THETA ** (-jnp.arange(0, ROPE_DIM, 2, dtype=jnp.float32) / ROPE_DIM)
    ang = pos[:, None] * inv[None, :]
    return jnp.cos(ang), jnp.sin(ang)

def apply_partial_rope(x, cos, sin):
    half = ROPE_DIM // 2
    xf = x.astype(jnp.float32)
    x1, x2 = xf[..., :half], xf[..., half:ROPE_DIM]
    c, s = cos[None, :, None, :], sin[None, :, None, :]
    out = jnp.concatenate([x1 * c - x2 * s, x2 * c + x1 * s, xf[..., ROPE_DIM:]], axis=-1)
    return out.astype(x.dtype)

def _chunk(a, n):
    return jnp.moveaxis(a.reshape(a.shape[0], n, Q_BLOCK, *a.shape[2:]), 1, 0)

def _unchunk(a):
    a = jnp.moveaxis(a, 0, 1)
    return a.reshape(a.shape[0], a.shape[1] * a.shape[2], *a.shape[3:])

def moba_attention(q, k, v):
    B, S, H, d = q.shape
    nb = -(-S // MOBA_BLOCK)
    pad = nb * MOBA_BLOCK - S
    kp = jnp.pad(k, ((0, 0), (0, pad), (0, 0), (0, 0)))
    vp = jnp.pad(v, ((0, 0), (0, pad), (0, 0), (0, 0)))
    kb = kp.reshape(B, nb, MOBA_BLOCK, H, d)
    vb = vp.reshape(B, nb, MOBA_BLOCK, H, d)
    kmean = jnp.mean(kb.astype(jnp.float32), axis=2)
    kbt = jnp.transpose(kb, (0, 3, 1, 2, 4))
    vbt = jnp.transpose(vb, (0, 3, 1, 2, 4))
    n_sel = min(MOBA_TOPK, max(nb - 1, 1))
    scale = HEAD_DIM ** -0.5
    nq = S // Q_BLOCK
    gather_blocks = jax.vmap(jax.vmap(lambda blk, ii: blk[ii]))

    def one_block(args):
        qi, ci = args
        t = ci * Q_BLOCK + jnp.arange(Q_BLOCK)
        cur = (ci * Q_BLOCK) // MOBA_BLOCK
        gate = jnp.einsum('bqhd,bnhd->bqhn', qi.astype(jnp.float32), kmean)
        gate = jnp.where(jnp.arange(nb) < cur, gate, NEG)
        _, idx = lax.top_k(gate, n_sel)
        valid = jnp.transpose(idx < cur, (0, 2, 1, 3))
        idx_t = jnp.transpose(idx, (0, 2, 1, 3))
        ksel = gather_blocks(kbt, idx_t)
        vsel = gather_blocks(vbt, idx_t)
        qh = jnp.transpose(qi, (0, 2, 1, 3))
        s_past = jnp.einsum('bhqd,bhqnkd->bhqnk', qh, ksel).astype(jnp.float32) * scale
        s_past = jnp.where(valid[..., None], s_past, NEG)
        kown = lax.dynamic_slice_in_dim(kp, cur * MOBA_BLOCK, MOBA_BLOCK, axis=1)
        vown = lax.dynamic_slice_in_dim(vp, cur * MOBA_BLOCK, MOBA_BLOCK, axis=1)
        s_own = jnp.einsum('bhqd,bkhd->bhqk', qh, kown).astype(jnp.float32) * scale
        kpos = cur * MOBA_BLOCK + jnp.arange(MOBA_BLOCK)
        s_own = jnp.where(kpos[None, :] <= t[:, None], s_own, NEG)
        n_past = n_sel * MOBA_BLOCK
        s = jnp.concatenate([s_past.reshape(B, H, Q_BLOCK, n_past), s_own], axis=-1)
        p = jax.nn.softmax(s, axis=-1).astype(v.dtype)
        p_past = p[..., :n_past].reshape(B, H, Q_BLOCK, n_sel, MOBA_BLOCK)
        p_own = p[..., n_past:]
        return (jnp.einsum('bhqnk,bhqnkd->bqhd', p_past, vsel)
                + jnp.einsum('bhqk,bkhd->bqhd', p_own, vown))

    out = lax.map(one_block, (_chunk(q, nq), jnp.arange(nq)))
    return _unchunk(out)

def dsa_attention(q, k, v, q_idx, k_idx, w_idx):
    B, S, H, d = q.shape
    topk = min(DSA_TOPK, S // 4)
    scale = HEAD_DIM ** -0.5
    nq = S // Q_BLOCK
    kf = k.reshape(B, S, H * d)
    vf = v.reshape(B, S, H * d)
    kix = k_idx.astype(jnp.float32)
    gather_rows = jax.vmap(lambda rows, ii: rows[ii])

    def one_block(args):
        qb, qib, wib, ci = args
        t = ci * Q_BLOCK + jnp.arange(Q_BLOCK)
        logits = jnp.einsum('bqjd,bsd->bqjs', qib.astype(jnp.float32), kix)
        score = jnp.einsum('bqj,bqjs->bqs', wib.astype(jnp.float32), jax.nn.relu(logits))
        score = jnp.where(jnp.arange(S)[None, :] <= t[:, None], score, NEG)
        _, sel = lax.top_k(score, topk)
        valid = sel <= t[None, :, None]
        ksel = gather_rows(kf, sel).reshape(B, Q_BLOCK, topk, H, d)
        vsel = gather_rows(vf, sel).reshape(B, Q_BLOCK, topk, H, d)
        s = jnp.einsum('bqhd,bqkhd->bhqk', qb, ksel).astype(jnp.float32) * scale
        s = jnp.where(valid[:, None, :, :], s, NEG)
        p = jax.nn.softmax(s, axis=-1).astype(v.dtype)
        return jnp.einsum('bhqk,bqkhd->bqhd', p, vsel)

    out = lax.map(one_block, (_chunk(q, nq), _chunk(q_idx, nq), _chunk(w_idx, nq), jnp.arange(nq)))
    return _unchunk(out)

def stick_breaking_attention(q, k, v):
    B, S, H, d = q.shape
    scale = HEAD_DIM ** -0.5
    nq = S // Q_BLOCK
    kpos = jnp.arange(S)

    def one_block(args):
        qb, ci = args
        t = ci * Q_BLOCK + jnp.arange(Q_BLOCK)
        z = jnp.einsum('bqhd,bshd->bhqs', qb, k).astype(jnp.float32) * scale
        strict = kpos[None, :] < t[:, None]
        log_beta = jax.nn.log_sigmoid(z)
        log_1m = jnp.where(strict, jax.nn.log_sigmoid(-z), 0.0)
        after = lax.cumsum(log_1m, axis=3, reverse=True) - log_1m
        a = jnp.where(strict, jnp.exp(log_beta + after), 0.0).astype(v.dtype)
        return jnp.einsum('bhqs,bshd->bqhd', a, v)

    out = lax.map(one_block, (_chunk(q, nq), jnp.arange(nq)))
    return _unchunk(out)

def second_inputs(seed: int = 0) -> dict:
    key = jax.random.key(seed)
    ks = jax.random.split(key, 12)
    f32 = jnp.float32
    x = jax.random.normal(ks[0], (BATCH, SEQ, D_MODEL), f32)
    c = jax.random.normal(ks[1], (BATCH, D_MODEL), f32)
    w_ada = jax.random.normal(ks[2], (DEPTH, D_MODEL, N_MOD * D_MODEL), f32) * D_MODEL ** -0.5
    b_ada = 0.01 * jax.random.normal(ks[3], (DEPTH, N_MOD * D_MODEL), f32)
    norm_g = 1.0 + 0.02 * jax.random.normal(ks[4], (DEPTH, 3, D_MODEL), f32)
    w_in = jax.random.normal(ks[5], (DEPTH, D_MODEL, D_IN_2), f32) * D_MODEL ** -0.5
    qk_g = 1.0 + 0.02 * jax.random.normal(ks[6], (DEPTH, 4, HEAD_DIM), f32)
    out_g = 1.0 + 0.02 * jax.random.normal(ks[7], (DEPTH, D_MIX), f32)
    w_out = jax.random.normal(ks[8], (DEPTH, D_MIX, D_MODEL), f32) * D_MIX ** -0.5
    ffn_w1 = jax.random.normal(ks[9], (DEPTH, 2, D_MODEL, D_FF), f32) * D_MODEL ** -0.5
    ffn_w3 = jax.random.normal(ks[10], (DEPTH, 2, D_MODEL, D_FF), f32) * D_MODEL ** -0.5
    ffn_w2 = jax.random.normal(ks[11], (DEPTH, 2, D_FF, D_MODEL), f32) * D_FF ** -0.5
    return {"x": x, "c": c, "w_ada": w_ada, "b_ada": b_ada, "norm_g": norm_g, "w_in": w_in,
            "qk_g": qk_g, "out_g": out_g, "w_out": w_out, "ffn_w1": ffn_w1,
            "ffn_w3": ffn_w3, "ffn_w2": ffn_w2}

def second_block(x, c, w_ada, b_ada, norm_g, w_in, qk_g, out_g, w_out, ffn_w1, ffn_w3, ffn_w2):
    B, S, _ = x.shape
    cos, sin = rope_tables(S)
    split_points = [int(p) for p in np.cumsum(SPLIT_SIZES)[:-1]]
    silu_c = jax.nn.silu(c)
    for layer in range(DEPTH):
        mod = silu_c @ w_ada[layer] + b_ada[layer]
        sh1, sc1, g1, sh2, sc2, g2, sh3, sc3, g3 = [m[:, None, :] for m in jnp.split(mod, N_MOD, axis=-1)]

        h = modulate(rmsnorm_2(x, norm_g[layer, 0]), sh1, sc1)
        x = x + 0.5 * g1 * swiglu_2(h, ffn_w1[layer, 0], ffn_w3[layer, 0], ffn_w2[layer, 0])

        h = modulate(rmsnorm_2(x, norm_g[layer, 1]), sh2, sc2)
        proj = h @ w_in[layer]
        (qa, ka, va, qb, kb, vb, qi, ki, wi, qc, kc, vc) = jnp.split(proj, split_points, axis=-1)
        heads = lambda t, n: t.reshape(B, S, n, HEAD_DIM)
        qa = apply_partial_rope(rmsnorm_2(heads(qa, N_HEADS_A), qk_g[layer, 0]), cos, sin)
        ka = apply_partial_rope(rmsnorm_2(heads(ka, N_HEADS_A), qk_g[layer, 1]), cos, sin)
        qb = apply_partial_rope(rmsnorm_2(heads(qb, N_HEADS_B), qk_g[layer, 2]), cos, sin)
        kb = apply_partial_rope(rmsnorm_2(heads(kb, N_HEADS_B), qk_g[layer, 3]), cos, sin)
        qi = apply_partial_rope(qi.reshape(B, S, IDX_HEADS, IDX_DIM), cos, sin)
        ki = apply_partial_rope(ki[:, :, None, :], cos, sin)[:, :, 0, :]

        oa = moba_attention(qa, ka, heads(va, N_HEADS_A))
        ob = dsa_attention(qb, kb, heads(vb, N_HEADS_B), qi, ki, wi)
        oc = stick_breaking_attention(heads(qc, N_HEADS_C), heads(kc, N_HEADS_C), heads(vc, N_HEADS_C))

        o = jnp.concatenate([oa, ob, oc], axis=2)
        o = (_rms(o).reshape(B, S, D_MIX) * out_g[layer].astype(jnp.float32)).astype(x.dtype)
        x = x + g2 * (o @ w_out[layer])

        h = modulate(rmsnorm_2(x, norm_g[layer, 2]), sh3, sc3)
        x = x + 0.5 * g3 * swiglu_2(h, ffn_w1[layer, 1], ffn_w3[layer, 1], ffn_w2[layer, 1])
    return x


def setup_inputs(seed=0):
    out = dict(first_inputs(seed))
    for name, value in second_inputs(seed + 1).items():
        if name != "x":
            out[name + "_2"] = value
    return out


def reference(
    x, norm_mix, w_in, w_pool, pool_scale, attn_gain, w_out, norm_ffn, ffn_wg, ffn_wu, ffn_wd,
    w_router, moe_wg, moe_wu, moe_wd, final_norm, c_2, w_ada_2, b_ada_2, norm_g_2, w_in_2,
    qk_g_2, out_g_2, w_out_2, ffn_w1_2, ffn_w3_2, ffn_w2_2,
):
    x = first_block(
        x, norm_mix, w_in, w_pool, pool_scale, attn_gain, w_out, norm_ffn, ffn_wg, ffn_wu,
        ffn_wd, w_router, moe_wg, moe_wu, moe_wd, final_norm,
    )
    return second_block(
        x, c_2, w_ada_2, b_ada_2, norm_g_2, w_in_2, qk_g_2, out_g_2, w_out_2, ffn_w1_2,
        ffn_w3_2, ffn_w2_2,
    )


_drawn_inputs = setup_inputs


def setup_inputs(seed=0):
    import zlib

    import numpy as np

    out = dict(_drawn_inputs(seed))
    spreads = {}
    factors = {'b_ada_2': 2.671, 'norm_g_2': 2.771, 'qk_g_2': 8.0, 'out_g_2': 4.263}
    for name, (base, spread) in spreads.items():
        noise = np.random.default_rng([zlib.crc32(name.encode()), seed]).standard_normal(out[name].shape)
        drawn = base * np.exp(spread * noise) if base else spread * noise
        out[name] = __import__('jax').numpy.asarray(drawn.astype(out[name].dtype))
    for name, factor in factors.items():
        out[name] = (out[name] * factor).astype(out[name].dtype)
    return out
```

```python
from contextlib import ExitStack

import concourse.bass as bass
import numpy as np
from concourse import mybir

P = 128
T = 256
D = 1024
KB = D // P
TT = T // P
D_FF = 2816
D_FFX = 3584
NE = 8
TILE = 3072
FB = TILE // KB // P
COLS = FB * P
HD = 64
N_MOD = 9
EPS = 1e-6
NEG = -1e30
TAKEN = -3e38
TOPK = min(256, T // 4)
MODB = N_MOD * KB
CAP = 96

NS = 4
IN1_F, IN1_V = 4, (384, 128)
IN2_F, IN2_V = 7, (384, 384, 264)
IN1 = IN1_F + len(IN1_V)
IN2 = IN2_F + len(IN2_V)
OUTP = -(-KB // FB)
FF = D_FF // P
FX = D_FFX // P
ADA = MODB // FB
STREAM = [IN1, OUTP, FF, IN1, OUTP, NE * FX] + [FF, IN2, OUTP, FF] * 2
STARTS = [sum(STREAM[:i]) for i in range(len(STREAM) + 1)]
N_TILES = STARTS[-1]
IN_STAGE = (0, 3, 7, 11)
FFN_STAGE = (2, 5, 6, 9, 10, 13)
Y_STAGE = (1, 2, 4, 5, 6, 8, 9, 10, 12, 13)

CONST = {}
_at = 0
for _n, _w in (("ident", P), ("headones", P), ("rot", P), ("after", P), ("cmask0", P), ("cmask1", T),
               ("mult0", P), ("mult1", T), ("strict", T + P), ("cos", T), ("sin", T),
               ("invcnt", 4 * T), ("iota", NE), ("slots", CAP)):
    CONST[_n] = (_at, _w)
    _at += _w
N_CONST = _at
VEC = {}
_at = 0
for _n, _w in (("norm_mix", 2 * KB), ("norm_ffn", 2 * KB), ("final", KB), ("cat_g", 2 * KB),
               ("norm_g", 6 * KB), ("out_g", 2 * KB), ("qk_g", 8), ("b_ada", 2 * MODB), ("c", KB)):
    VEC[_n] = (_at, _w)
    _at += _w
N_VEC = _at


def build(nc, x_in, wstream, astream, wpool, wrouter, vectors, consts, out):
    fp32 = mybir.dt.float32
    ALU = mybir.AluOpType
    ACT = mybir.ActivationFunctionType
    AX = mybir.AxisListType.X
    ctx = ExitStack()
    with ctx:
        def sb(name, shape):
            return ctx.enter_context(nc.sbuf_tensor(name, shape, fp32))

        def sem(name):
            return ctx.enter_context(nc.semaphore(name))

        ring = sb("ring", [P, NS, TILE])
        ada = sb("ada", [P, 2, TILE])
        xT = sb("xT", [P, KB, T])
        hT = sb("hT", [P, KB, T])
        sq = sb("sq", [P, KB, T])
        proj = sb("proj", [P, 21, T])
        branch = sb("branch", [P, 3 * 4 * (16 + T)])
        upad, *win = (branch[:, i * 4 * (16 + T):(i + 1) * 4 * (16 + T)]
                      .rearrange("p (g t) -> p g t", g=4) for i in range(3))
        vtok = sb("vtok", [P, TT, 1032])
        cat = sb("cat", [P, KB, T])
        rstd = sb("rstd", [P, KB, T])
        var = sb("var", [P, KB, T])
        sm = sb("sm", [P, 4, T])
        pT = sb("pT", [P, 4, TT, P])
        small = sb("small", [P, 64])
        score = sb("score", [P, T])
        relu_l = sb("relu_l", [P, 2, T])
        selmask = sb("selmask", [P, TT, T])
        top8 = sb("top8", [P, 8])
        st_l = hT[:, 0:6, :].rearrange("p k t -> p (k t)").rearrange("p (b i t) -> p b i t", b=2, i=2)
        st_d = branch[:, 0:2 * 4 * (T + P)].rearrange("p (b i t) -> p b i t", b=2, i=4)
        sg = sb("sg", [P, 2, T])
        hid = sb("hid", [P, 2, T])
        gates = proj[:, 0:NE, :]
        place = proj[:, 8:14, :].rearrange("p k t -> p (k t)").rearrange("p (e t c) -> p e t c", e=NE, t=TT)
        gplace = proj[:, 14:20, :].rearrange("p k t -> p (k t)").rearrange("p (e t c) -> p e t c", e=NE, t=TT)
        scatter = cat[0:CAP, :, :]
        htok = vtok[:, :, 0:D]
        he = branch[:, 0:KB * CAP].rearrange("p (k c) -> p k c", k=KB)
        ye = branch[:, KB * CAP:2 * KB * CAP].rearrange("p (k c) -> p k c", k=KB)
        yt = branch[0:CAP, 2 * KB * CAP:2 * KB * CAP + D]
        rt = sb("rt", [P, 12, TT, NE])
        diag = sb("diag", [P, 2, P])
        wide = ctx.enter_context(nc.sbuf_tensor("wide", [P, NE], mybir.dt.int32))
        zeros = sb("zeros", [1, 512])
        acc = sb("acc", [P, 2, COLS])
        mod = sb("mod", [P, 2, MODB])
        gs = sb("gs", [P, 6, KB])
        qkg = sb("qkg", [P, 8])
        hg = sb("hg", [P, 6, KB])
        silu_c = sb("silu_c", [P, KB])
        ones = sb("ones", [P, P])
        cst = sb("cst", [P, N_CONST])
        vec = sb("vec", [P, N_VEC])
        wp = sb("wp", [P, 8, P])
        wr = sb("wr", [P, KB, NE])

        def C(name):
            a, w = CONST[name]
            return cst[:, a:a + w]

        def V(name, i=0, n=None):
            a, w = VEC[name]
            return vec[:, a + i:a + i + (n or 1)]

        ps = ctx.enter_context(nc.psum_tensor("ps", [P, 8, 512], fp32))
        Y = ps[:, 0:4, :].rearrange("p b (h t) -> p (b h) t", h=2)
        SS = ps[:, 6, :]

        tile_in = [sem(f"tile_in{s}") for s in range(NS)]
        tile_used = sem("tile_used")
        ada_in = [sem(f"ada_in{s}") for s in range(2)]
        ada_used = sem("ada_used")
        loaded = sem("loaded")
        stored = sem("stored")
        const_set = sem("const_set")
        x_ready = sem("x_ready")
        sq_ready = sem("sq_ready")
        ss_ready = sem("ss_ready")
        var_ready = sem("var_ready")
        std_ready = sem("std_ready")
        normed = sem("normed")
        h_ready = sem("h_ready")
        gu_ready = sem("gu_ready")
        sg_ready = sem("sg_ready")
        hid_ready = sem("hid_ready")
        in_ready = sem("in_ready")
        in_copied = sem("in_copied")
        d_ready = sem("d_ready")
        z_ready = sem("z_ready")
        z_copied = sem("z_copied")
        s_ready = sem("s_ready")
        s_used = sem("s_used")
        max_ready = sem("max_ready")
        sub_ready = sem("sub_ready")
        exp_ready = sem("exp_ready")
        rden_ready = sem("rden_ready")
        p_ready = sem("p_ready")
        pt_ready = sem("pt_ready")
        pt_copied = sem("pt_copied")
        o_ready = sem("o_ready")
        o_copied = sem("o_copied")
        csq_ready = sem("csq_ready")
        css_ready = sem("css_ready")
        cvar_ready = sem("cvar_ready")
        cstd_ready = sem("cstd_ready")
        cat_ready = sem("cat_ready")
        logit_ready = sem("logit_ready")
        route_exp_in = sem("route_exp_in")
        route_exp = sem("route_exp")
        diag_ready = sem("diag_ready")
        gate_ready = sem("gate_ready")
        mask_ready = sem("mask_ready")
        pos_ready = sem("pos_ready")
        wide_ready = sem("wide_ready")
        place_ready = sem("place_ready")
        ht_ready = sem("ht_ready")
        ht_copied = sem("ht_copied")
        gp_ready = sem("gp_ready")
        gp_copied = sem("gp_copied")
        he_gathered = sem("he_gathered")
        he_ready = sem("he_ready")
        ye_ready = sem("ye_ready")
        yt_ready = sem("yt_ready")
        yt_copied = sem("yt_copied")
        gate_copied = sem("gate_copied")
        silu_c_ready = sem("silu_c_ready")
        acc_ready = sem("acc_ready")
        mod_ready = sem("mod_ready")
        acc_step = sem("acc_step")
        hid_raw = sem("hid_raw")
        moe_done = sem("moe_done")
        mod_done = sem("mod_done")
        qsq_ready = sem("qsq_ready")
        qss_ready = sem("qss_ready")
        qvar_ready = sem("qvar_ready")
        qstd_ready = sem("qstd_ready")
        qk_ready = sem("qk_ready")
        rot_ready = sem("rot_ready")
        cos_ready = sem("cos_ready")
        rope_ready = sem("rope_ready")
        il_ready = sem("il_ready")
        ir_ready = sem("ir_ready")
        ir_used = sem("ir_used")
        sel_ready = sem("sel_ready")
        zt_ready = sem("zt_ready")
        zt_used = sem("zt_used")
        l_ready = sem("l_ready")
        sp_ready = sem("sp_ready")
        spm_ready = sem("spm_ready")
        af_ready = sem("af_ready")
        arg_ready = sem("arg_ready")
        a_exp = sem("a_exp")
        a_ready = sem("a_ready")
        co_ready = sem("co_ready")
        co_copied = sem("co_copied")
        chain = {e: sem(f"chain_{e}") for e in ("dve", "act", "pool")}
        counts = {"dve": 0, "act": 0, "pool": 0}

        def after(engine, name, instruction):
            counts[name] += 1
            instruction.then_inc(chain[name], 1)
            engine.wait_ge(chain[name], counts[name])


        def chunks_before(f):
            return [0, FF, FF + NE * FX, 2 * FF + NE * FX, 3 * FF + NE * FX, 4 * FF + NE * FX][f]

        def chunk_loop(n, first):
            lead = first + (n - first) % NS
            return lead, (n - lead) // NS

        def in_units(m):
            f, v = (IN1_F * FB, len(IN1_V) * TT) if m < 2 else (IN2_F * FB, len(IN2_V) * TT)
            return f, v

        UNITS_BEFORE = [0]
        for m in range(4):
            UNITS_BEFORE.append(UNITS_BEFORE[-1] + sum(in_units(m)))

        def unit_tile(m, u):
            feats, _ = in_units(m)
            if u < feats:
                return STARTS[IN_STAGE[m]] + u // FB, u % FB == FB - 1
            v = u - feats
            return STARTS[IN_STAGE[m]] + feats // FB + v // TT, v % TT == TT - 1

        not_last = {}
        n_ready = 0
        for m in range(4):
            for u in range(sum(in_units(m))):
                n_ready += not unit_tile(m, u)[1]
                not_last[m, u] = n_ready

        def wait_unit(engine, m, u):
            i, last = unit_tile(m, u)
            if last:
                engine.wait_ge(tile_used, i + 1)
            else:
                engine.wait_ge(in_ready, not_last[m, u])

        block = ctx.enter_context(nc.Block())

        @block.sync
        def _(sp):
            for dst, src in ((vec[:, :], vectors), (xT[:, :, :], x_in), (cst[:, :], consts),
                             (wp[:, :, :], wpool), (wr[:, :, :], wrouter)):
                sp.dma_start(dst, src).then_inc(loaded, 16)

            def load(s, i):
                sp.dma_start(ring[:, s, :], wstream[i]).then_inc(tile_in[s], 16)

            for s in range(NS):
                load(s, s)
            rounds = N_TILES // NS
            with nc.sync.Fori(1, rounds) as r:
                for s in range(NS):
                    sp.wait_ge(tile_used, r * NS + (s - NS + 1))
                    sp.dma_start(ring[:, s, :], wstream[bass.ds(r * NS + s, 1), :, :]
                                 .rearrange("a p n -> p (a n)")).then_inc(tile_in[s], 16)
            for i in range(rounds * NS, N_TILES):
                sp.wait_ge(tile_used, i - NS + 1)
                load(i % NS, i)
            sp.wait_ge(x_ready, KB * 11)
            sp.dma_start(out, xT[:, :, :]).then_inc(stored, 16)
            sp.wait_ge(stored, 16)

        @block.gpsimd
        def _(pool):
            nc.gpsimd.memset(ones[:, :], 1.0).then_inc(const_set, 1)
            nc.gpsimd.memset(win[0][:, :, 0:16], 0.0).then_inc(const_set, 1)
            nc.gpsimd.memset(win[1][:, :, 0:16], 0.0).then_inc(const_set, 1)
            nc.gpsimd.memset(upad[:, :, 0:16], 0.0).then_inc(const_set, 1)
            nc.gpsimd.memset(zeros[:, :], 0.0).then_inc(const_set, 1)
            pool.wait_ge(const_set, 5)
            pool.wait_ge(loaded, 16 * 5)

            def load_ada(s, i):
                pool.dma_start(ada[:, s, :], astream[i]).then_inc(ada_in[s], 16)

            def ada_stream():
                for s in range(2):
                    load_ada(s, s)
                with nc.gpsimd.Fori(1, ADA) as r:
                    for s in range(2):
                        pool.wait_ge(ada_used, r * 2 + (s - 1))
                        pool.dma_start(ada[:, s, :], astream[bass.ds(r * 2 + s, 1), :, :]
                                       .rearrange("a p n -> p (a n)")).then_inc(ada_in[s], 16)

            def windows(m):
                pool.wait_ge(in_copied, UNITS_BEFORE[m] + 4)
                src = upad
                for i, step in enumerate((1, 2, 4, 8)):
                    dst = win[i % 2]
                    after(pool, "pool", nc.gpsimd.tensor_tensor(
                        dst[:, i:4, 16:16 + T], src[:, i:4, 16:16 + T],
                        src[:, i:4, 16 - step:16 - step + T], ALU.add))
                    after(pool, "pool", nc.gpsimd.tensor_tensor(
                        sq[:, i, :], dst[:, i, 16:16 + T],
                        C("invcnt")[:, i * T:(i + 1) * T], ALU.mult))
                    src = dst
                nc.gpsimd.tensor_tensor(sq[:, 0:4, :], sq[:, 0:4, :], upad[:, :, 16:16 + T],
                                        ALU.subtract).then_inc(d_ready, 1)

            def softmax_unit(u, tt):
                nk = P * (tt + 1)
                pool.wait_ge(max_ready, u + 1)
                nc.gpsimd.tensor_tensor(sm[:, :, 0:nk], sm[:, :, 0:nk],
                                        small[:, 0:4].unsqueeze(2).broadcast_to([P, 4, nk]),
                                        ALU.subtract).then_inc(sub_ready, 1)
                pool.wait_ge(rden_ready, u + 1)
                nc.gpsimd.tensor_tensor(sm[:, :, 0:nk], sm[:, :, 0:nk],
                                        small[:, 8:12].unsqueeze(2).broadcast_to([P, 4, nk]),
                                        ALU.mult).then_inc(p_ready, 1)

            def ropes(m):
                n = 13 * (m - 2)
                for b in range(13):
                    pool.wait_ge(rot_ready, n + b + 1)
                    nc.gpsimd.tensor_tensor(proj[:, b, :], proj[:, b, :], C("cos"), ALU.mult)\
                        .then_inc(cos_ready, 1)

            def sticks(m):
                n = 8 * (m - 2)
                for h in range(9):
                    if h < 8:
                        pool.wait_ge(sp_ready, n + h + 1)
                        nc.gpsimd.tensor_tensor(st_d[:, h % 2, 2, :], st_d[:, h % 2, 0, :],
                                                C("strict"), ALU.mult).then_inc(spm_ready, 1)
                    if h > 0:
                        g = h - 1
                        pool.wait_ge(a_exp, n + g + 1)
                        nc.gpsimd.tensor_tensor(st_d[:, g % 2, 3, :], st_d[:, g % 2, 3, :],
                                                C("strict"), ALU.mult).then_inc(a_ready, 1)

            for m in range(2):
                windows(m)
                for u in range(4):
                    softmax_unit(4 * m + u, u % 2)
                if m == 0:
                    ada_stream()
            for m in range(2, 4):
                ropes(m)
                for u in range(4):
                    softmax_unit(4 * m + u, u % 2)
                sticks(m)

        @block.scalar
        def _(act):
            act.wait_ge(loaded, 16 * 5)
            act.wait_ge(const_set, 5)

            def norm(n):
                if n:
                    act.wait_ge(x_ready, KB * n)
                for i in range(4):
                    nc.scalar.activation(sq[:, 2 * i:2 * i + 2, :], xT[:, 2 * i:2 * i + 2, :],
                                         ACT.Square).then_inc(sq_ready, 1)
                act.wait_ge(var_ready, n + 1)
                nc.scalar.activation(rstd[:, 0, :], var[:, 0, :], ACT.Sqrt).then_inc(std_ready, 1)
                if n >= 5:
                    for k in range(KB):
                        act.wait_ge(normed, KB * (n - 5) + k + 1)
                        nc.scalar.activation(hT[:, k, :], sq[:, k, :], ACT.Identity,
                                             bias=mod[:, (n - 5) // 3, 3 * ((n - 5) % 3) * KB + k:
                                                      3 * ((n - 5) % 3) * KB + k + 1])\
                            .then_inc(h_ready, 1)

            def in_copies(m):
                feats, _ = in_units(m)
                u = UNITS_BEFORE[m]
                for b in range(feats):
                    wait_unit(act, m, b)
                    src = ps[:, u % 4, 0:T]
                    if m < 2 and b < 4:
                        dst, scale = upad[:, b, 16:16 + T], 1.0
                    else:
                        isq = (4 <= b < 8) if m < 2 else (13 <= b < 17)
                        dst, scale = proj[:, b, :], (HD ** -0.5 if isq else 1.0)
                    nc.scalar.activation(dst, src, ACT.Copy, scale=scale).then_inc(in_copied, 1)
                    u += 1
                at = 0
                for w in (IN1_V if m < 2 else IN2_V):
                    for tt in range(TT):
                        wait_unit(act, m, u - UNITS_BEFORE[m])
                        nc.scalar.activation(vtok[:, tt, at:at + w], ps[:, u % 4, 0:w], ACT.Copy)\
                            .then_inc(in_copied, 1)
                        u += 1
                    at += w

            def softmax_unit(u, tt, block0):
                nk = P * (tt + 1)
                act.wait_ge(sub_ready, u + 1)
                nc.scalar.activation(sm[:, :, 0:nk], sm[:, :, 0:nk], ACT.Exp).then_inc(exp_ready, 1)
                act.wait_ge(pt_ready, u + 1)
                if u:
                    act.wait_ge(o_ready, u)
                nc.scalar.activation(
                    pT[:, :, 0:tt + 1, :],
                    ps[:, 2:4, :].rearrange("p b (h k t) -> p (b h) k t", h=2, k=TT)[:, :, 0:tt + 1, :],
                    ACT.Copy).then_inc(pt_copied, 1)
                act.wait_ge(o_ready, u + 1)
                nc.scalar.activation(
                    cat[:, block0:block0 + 2, tt * P:(tt + 1) * P],
                    ps[:, 4 + u % 2, 0:T].rearrange("p (b t) -> p b t", b=2), ACT.Copy)\
                    .then_inc(o_copied, 1)

            def cat_norm(m):
                act.wait_ge(o_copied, 4 * (m + 1))
                if m >= 2:
                    act.wait_ge(co_copied, 4 * (m - 1))
                else:
                    act.wait_ge(z_copied, 2 * (m + 1))
                nc.scalar.activation(sq[:, :, :], cat[:, :, :], ACT.Square).then_inc(csq_ready, 1)
                act.wait_ge(cvar_ready, m + 1)
                n = 2 if m < 2 else KB
                nc.scalar.activation(rstd[:, 0:n, :], var[:, 0:n, :], ACT.Sqrt).then_inc(cstd_ready, 1)

            def mixer1(m):
                in_copies(m)
                for i in range(2):
                    act.wait_ge(z_ready, 2 * m + i + 1)
                    nc.scalar.activation(cat[:, 2 * i:2 * i + 2, :],
                                         ps[:, 6 + i, :].rearrange("p (b t) -> p b t", b=2),
                                         ACT.Copy).then_inc(z_copied, 1)
                for u in range(4):
                    softmax_unit(4 * m + u, u % 2, 4 + 2 * (u // 2))
                cat_norm(m)

            def mixer2(m):
                in_copies(m)
                act.wait_ge(in_copied, UNITS_BEFORE[m] + 8)
                nc.scalar.activation(sq[:, :, :], proj[:, 0:8, :], ACT.Square).then_inc(qsq_ready, 1)
                act.wait_ge(qvar_ready, m - 1)
                nc.scalar.activation(rstd[:, :, :], var[:, :, :], ACT.Sqrt).then_inc(qstd_ready, 1)
                for i in range(16):
                    n = 16 * (m - 2) + i
                    nk = P * (i // 8 + 1)
                    act.wait_ge(il_ready, n + 1)
                    if n >= 2:
                        act.wait_ge(ir_used, n - 1)
                    nc.scalar.activation(relu_l[:, n % 2, 0:nk], ps[:, 6 + n % 2, 0:nk], ACT.Relu)\
                        .then_inc(ir_ready, 1)
                for u in range(4):
                    softmax_unit(4 * m + u, u % 2, 2 * (u // 2))
                for h in range(9):
                    n = 8 * (m - 2) + h
                    if h < 8:
                        act.wait_ge(zt_ready, n + 1)
                        if n >= 2:
                            act.wait_ge(sp_ready, n - 1)
                        z = ps[:, n % 2, 0:T + P]
                        after(act, "act", nc.scalar.activation(st_l[:, n % 2, 0, :], z, ACT.Abs))
                        after(act, "act", nc.scalar.activation(st_l[:, n % 2, 0, :], st_l[:, n % 2, 0, :],
                                                               ACT.Exp, scale=-1.0))
                        nc.scalar.activation(st_l[:, n % 2, 1, :], st_l[:, n % 2, 0, :], ACT.Ln,
                                             bias=1.0).then_inc(l_ready, 1)
                    if h > 0:
                        g = n - 1
                        act.wait_ge(arg_ready, g + 1)
                        if g >= 2:
                            act.wait_ge(co_ready, g - 1)
                        nc.scalar.activation(st_d[:, g % 2, 3, :], st_d[:, g % 2, 1, :], ACT.Exp,
                                             scale=-1.0).then_inc(a_exp, 1)
                        if g % 2 and h >= 3:
                            copy_sticks(m, (h - 1) // 2 - 1)
                copy_sticks(m, 3)
                cat_norm(m)

            def copy_sticks(m, pair):
                act.wait_ge(co_ready, 8 * (m - 2) + 2 * pair + 2)
                nc.scalar.activation(cat[:, 4 + pair, :], ps[:, 4 + pair % 2, 0:T], ACT.Copy)\
                    .then_inc(co_copied, 1)

            def ffn(f, n):
                base = chunks_before(f)

                def chunk(b, c):
                    act.wait_ge(gu_ready, c + 1)
                    act.wait_ge(hid_ready, c - 1)
                    nc.scalar.activation(sg[:, b, :], ps[:, 4 + b, 0:T], ACT.Silu).then_inc(sg_ready, 1)

                def first(b, c):
                    act.wait_ge(gu_ready, c + 1)
                    if c >= 2:
                        act.wait_ge(hid_ready, c - 1)
                    nc.scalar.activation(sg[:, b, :], ps[:, 4 + b, 0:T], ACT.Silu).then_inc(sg_ready, 1)

                lead, rounds = chunk_loop(n, 2)
                for c in range(lead):
                    first(c % 2, base + c)
                with nc.scalar.Fori(0, rounds) as r:
                    for j in range(NS):
                        chunk((lead + j) % 2, r * NS + (base + lead + j))

            def moe():
                base = chunks_before(1)

                def chunk(b, c, width):
                    act.wait_ge(gu_ready, c + 1)
                    act.wait_ge(hid_ready, c - 1)
                    nc.scalar.activation(sg[:, b, 0:width], ps[:, 4 + b, 0:width], ACT.Silu)\
                        .then_inc(sg_ready, 1)

                act.wait_ge(wide_ready, 1)
                with nc.scalar.Fori(0, NE) as e:
                    is_wide = nc.scalar.value_load(wide[0:1, bass.ds(e, 1)], min_val=0, max_val=1)
                    with nc.scalar.If(is_wide == 1):
                        with nc.scalar.Fori(0, FX // NS) as r:
                            for j in range(NS):
                                chunk(j % 2, e * FX + r * NS + (base + j), T)
                        act.sem_inc(he_ready, 1)
                        act.sem_inc(ye_ready, 1)
                    with nc.scalar.Else():
                        act.wait_ge(he_gathered, e + 1)
                        nc.scalar.activation(
                            he.rearrange("p (h k) c -> p h (k c)", h=2), ps[:, 6:8, 0:4 * CAP], ACT.Copy)\
                            .then_inc(he_ready, 1)
                        with nc.scalar.Fori(0, FX // NS) as r:
                            for j in range(NS):
                                chunk(j % 2, e * FX + r * NS + (base + j), CAP)
                        act.wait_ge(tile_used, e * FX + (STARTS[5] + FX))
                        nc.scalar.activation(
                            ye.rearrange("p (h k) c -> p h (k c)", h=2), ps[:, 6:8, 0:4 * CAP], ACT.Copy)\
                            .then_inc(ye_ready, 1)

            nc.scalar.activation(silu_c[:, :], V("c", 0, KB), ACT.Silu).then_inc(silu_c_ready, 1)
            norm(0)
            mixer1(0)
            norm(1)
            ffn(0, FF)
            norm(2)
            mixer1(1)
            norm(3)
            act.wait_ge(route_exp_in, 1)
            nc.scalar.activation(rt[:, 8, :, 0:1], rt[:, 7, :, 0:1], ACT.Exp).then_inc(route_exp, 1)
            for i in range(4):
                act.wait_ge(ht_ready, i + 1)
                nc.scalar.activation(htok[:, i // 2, (i % 2) * 512:(i % 2 + 1) * 512], ps[:, 4 + i % 2, :],
                                     ACT.Copy).then_inc(ht_copied, 1)
            for i in range(4):
                act.wait_ge(gp_ready, i + 1)
                nc.scalar.activation(scatter[:, 2 * i:2 * i + 2, :],
                                     ps[0:CAP, 4 + i % 2, :].rearrange("p (e t) -> p e t", e=2),
                                     ACT.Copy).then_inc(gp_copied, 1)
            moe()
            norm(4)
            for l in range(2):
                norm(5 + 3 * l)
                ffn(2 + 2 * l, FF)
                norm(6 + 3 * l)
                mixer2(2 + l)
                norm(7 + 3 * l)
                ffn(3 + 2 * l, FF)

        @block.vector
        def _(dve):
            dve.wait_ge(loaded, 16 * 5)
            dve.wait_ge(const_set, 5)

            def mean_eps(dst, src, inv, signal):
                nc.vector.tensor_scalar(dst, src, inv, EPS, ALU.mult, ALU.add).then_inc(signal, 1)

            def norm(n):
                dve.wait_ge(ss_ready, n + 1)
                mean_eps(var[:, 0, :], SS[:, 0:T], 1.0 / D, var_ready)
                dve.wait_ge(std_ready, n + 1)
                after(dve, "dve", nc.vector.reciprocal(rstd[:, 1, :], rstd[:, 0, :]))
                for k in range(KB):
                    if n < 4:
                        g = V("norm_ffn" if n % 2 else "norm_mix", (n // 2) * KB + k)
                        nc.vector.scalar_tensor_tensor(hT[:, k, :], xT[:, k, :], g, rstd[:, 1, :],
                                                       ALU.mult, ALU.mult).then_inc(h_ready, 1)
                    elif n == 4:
                        nc.vector.scalar_tensor_tensor(xT[:, k, :], xT[:, k, :], V("final", k),
                                                       rstd[:, 1, :], ALU.mult, ALU.mult)\
                            .then_inc(x_ready, 1)
                    else:
                        nc.vector.scalar_tensor_tensor(sq[:, k, :], xT[:, k, :],
                                                       gs[:, n - 5, k:k + 1], rstd[:, 1, :],
                                                       ALU.mult, ALU.mult).then_inc(normed, 1)

            def residual(r, gate=None):
                dve.wait_ge(tile_used, STARTS[Y_STAGE[r] + 1])
                if r == 3:
                    dve.wait_ge(moe_done, 1)
                for k in range(KB):
                    if gate is None:
                        ins = nc.vector.tensor_tensor(xT[:, k, :], xT[:, k, :], Y[:, k, :], ALU.add)
                    else:
                        ins = nc.vector.scalar_tensor_tensor(xT[:, k, :], Y[:, k, :],
                                                             hg[:, gate, k:k + 1], xT[:, k, :],
                                                             ALU.mult, ALU.add)
                    ins.then_inc(x_ready, 1)

            def softmax_unit(u, tt, mask, mult):
                nk = P * (tt + 1)
                s_ps = ps[:, 0:2, :].rearrange("p b (h t) -> p (b h) t", h=2)[:, :, 0:nk]
                dve.wait_ge(s_ready, u + 1)
                if u:
                    dve.wait_ge(pt_ready, u)
                ins = nc.vector.tensor_tensor(sm[:, :, 0:nk], s_ps,
                                              mask.unsqueeze(1).broadcast_to([P, 4, nk]), ALU.add)
                ins.then_inc(s_used, 1)
                dve.wait_ge(s_used, u + 1)
                nc.vector.tensor_reduce(small[:, 0:4], sm[:, :, 0:nk], AX, ALU.max)\
                    .then_inc(max_ready, 1)
                dve.wait_ge(exp_ready, u + 1)
                if mult is not None:
                    after(dve, "dve", nc.vector.tensor_tensor(
                        sm[:, :, 0:nk], sm[:, :, 0:nk], mult.unsqueeze(1).broadcast_to([P, 4, nk]),
                        ALU.mult))
                after(dve, "dve", nc.vector.tensor_reduce(small[:, 4:8], sm[:, :, 0:nk], AX, ALU.add))
                nc.vector.reciprocal(small[:, 8:12], small[:, 4:8]).then_inc(rden_ready, 1)

            def cat_norm(m):
                n = 2 if m < 2 else KB
                dve.wait_ge(css_ready, m + 1)
                src = SS.rearrange("p (b t) -> p b t", b=2) if m < 2 else Y
                mean_eps(var[:, 0:n, :], src, 1.0 / (512 if m < 2 else HD), cvar_ready)
                dve.wait_ge(cstd_ready, m + 1)
                after(dve, "dve", nc.vector.reciprocal(var[:, 0:n, :], rstd[:, 0:n, :]))
                for k in range(KB):
                    g = V("cat_g", m * KB + k) if m < 2 else V("out_g", (m - 2) * KB + k)
                    nc.vector.scalar_tensor_tensor(cat[:, k, :], cat[:, k, :], g,
                                                   var[:, k // 4 if m < 2 else k, :],
                                                   ALU.mult, ALU.mult).then_inc(cat_ready, 1)

            def mixer1(m):
                for u in range(4):
                    tt = u % 2
                    softmax_unit(4 * m + u, tt, C(f"cmask{tt}"), C(f"mult{tt}"))
                cat_norm(m)

            def mixer2(m):
                l = m - 2
                dve.wait_ge(qss_ready, l + 1)
                mean_eps(var[:, :, :], Y, 1.0 / HD, qvar_ready)
                dve.wait_ge(qstd_ready, l + 1)
                after(dve, "dve", nc.vector.reciprocal(var[:, :, :], rstd[:, :, :]))
                for b in range(8):
                    nc.vector.scalar_tensor_tensor(proj[:, b, :], proj[:, b, :],
                                                   qkg[:, 4 * l + b // 2:4 * l + b // 2 + 1],
                                                   var[:, b, :], ALU.mult, ALU.mult)\
                        .then_inc(qk_ready, 1)
                for b in range(13):
                    n = 13 * l + b
                    dve.wait_ge(rot_ready, n + 1)
                    if n >= 2:
                        dve.wait_ge(rope_ready, n - 1)
                    after(dve, "dve", nc.vector.tensor_tensor(relu_l[:, n % 2, :], ps[:, n % 2, 0:T],
                                                              C("sin"), ALU.mult))
                    dve.wait_ge(cos_ready, n + 1)
                    nc.vector.tensor_tensor(proj[:, b, :], proj[:, b, :], relu_l[:, n % 2, :], ALU.add)\
                        .then_inc(rope_ready, 1)
                dve.wait_ge(in_copied, UNITS_BEFORE[m + 1])
                for tt in range(TT):
                    nk = P * (tt + 1)
                    for j in range(8):
                        n = 16 * l + 8 * tt + j
                        dve.wait_ge(ir_ready, n + 1)
                        w = vtok[:, tt, 1024 + j:1025 + j]
                        if j == 0:
                            ins = nc.vector.scalar_tensor_tensor(score[:, 0:nk], relu_l[:, n % 2, 0:nk],
                                                                 w, C(f"cmask{tt}"), ALU.mult, ALU.add)
                        else:
                            ins = nc.vector.scalar_tensor_tensor(score[:, 0:nk], relu_l[:, n % 2, 0:nk],
                                                                 w, score[:, 0:nk], ALU.mult, ALU.add)
                        ins.then_inc(ir_used, 1)
                        dve.wait_ge(ir_used, n + 1)
                    for i in range(TOPK // 8):
                        after(dve, "dve", nc.vector.max(top8[:, :], score[:, 0:nk]))
                        after(dve, "dve", nc.vector.match_replace(score[:, 0:nk], top8[:, :],
                                                                  score[:, 0:nk], TAKEN))
                    after(dve, "dve", nc.vector.tensor_scalar(score[:, 0:nk], score[:, 0:nk], 2 * NEG * 1e7,
                                                              -NEG, ALU.is_le, ALU.mult))
                    nc.vector.scalar_tensor_tensor(selmask[:, tt, 0:nk], score[:, 0:nk], NEG,
                                                   C(f"cmask{tt}"), ALU.add, ALU.add)\
                        .then_inc(sel_ready, 1)
                    dve.wait_ge(sel_ready, 2 * l + tt + 1)
                for u in range(4):
                    tt = u % 2
                    mask = C(f"cmask{tt}") if u < 2 else selmask[:, tt, 0:P * (tt + 1)]
                    softmax_unit(4 * m + u, tt, mask, None)
                for h in range(9):
                    n = 8 * l + h
                    if h < 8:
                        dve.wait_ge(l_ready, n + 1)
                        if n >= 2:
                            dve.wait_ge(spm_ready, n - 1)
                            dve.wait_ge(a_exp, n - 1)
                        z = ps[:, n % 2, 0:T + P]
                        after(dve, "dve", nc.vector.scalar_tensor_tensor(
                            st_d[:, n % 2, 0, :], z, 0.0, st_l[:, n % 2, 1, :], ALU.max, ALU.add))
                        nc.vector.tensor_tensor(st_d[:, n % 2, 1, :], st_d[:, n % 2, 0, :], z,
                                                ALU.subtract).then_inc(sp_ready, 1)
                    if h > 0:
                        g = n - 1
                        dve.wait_ge(af_ready, g + 1)
                        dve.wait_ge(sp_ready, g + 1)
                        nc.vector.tensor_tensor(st_d[:, g % 2, 1, :], st_d[:, g % 2, 1, :],
                                                ps[:, 2 + g % 2, 0:T + P], ALU.add)\
                            .then_inc(arg_ready, 1)
                cat_norm(m)

            def ffn(f, n):
                base = chunks_before(f)

                def chunk(b, c, lead=False):
                    dve.wait_ge(sg_ready, c + 1)
                    if not lead or (isinstance(c, int) and c >= 2):
                        dve.wait_ge(tile_used, c + (STARTS[FFN_STAGE[f]] - base - 1))
                    nc.vector.tensor_tensor(hid[:, b, :], sg[:, b, :], ps[:, 4 + b, T:2 * T],
                                            ALU.mult).then_inc(hid_ready, 1)

                lead, rounds = chunk_loop(n, 2)
                for c in range(lead):
                    chunk(c % 2, base + c, lead=True)
                with nc.vector.Fori(0, rounds) as r:
                    for j in range(NS):
                        chunk((lead + j) % 2, r * NS + (base + lead + j))

            def moe():
                base = chunks_before(1)

                def chunk(b, c, width, gate):
                    dve.wait_ge(sg_ready, c + 1)
                    dve.wait_ge(tile_used, c + (STARTS[5] - base - 1))
                    ins = nc.vector.tensor_tensor(hid[:, b, 0:width], sg[:, b, 0:width],
                                                  ps[:, 4 + b, width:2 * width], ALU.mult)
                    if gate is not None:
                        ins.then_inc(hid_raw, 1)
                        dve.wait_ge(hid_raw, c + (1 - base))
                        ins = nc.vector.tensor_tensor(hid[:, b, :], hid[:, b, :], gate, ALU.mult)
                    ins.then_inc(hid_ready, 1)

                with nc.vector.Fori(0, NE) as e:
                    is_wide = nc.vector.value_load(wide[0:1, bass.ds(e, 1)], min_val=0, max_val=1)
                    with nc.vector.If(is_wide == 1):
                        with nc.vector.Fori(0, FX // NS) as r:
                            for j in range(NS):
                                chunk(j % 2, e * FX + r * NS + (base + j), T,
                                      gates[:, bass.ds(e, 1), :].rearrange("p a t -> p (a t)"))
                        dve.sem_inc(yt_copied, 1)
                    with nc.vector.Else():
                        with nc.vector.Fori(0, FX // NS) as r:
                            for j in range(NS):
                                chunk(j % 2, e * FX + r * NS + (base + j), CAP, None)
                        dve.sem_inc(hid_raw, FX)
                        dve.wait_ge(yt_ready, e + 1)
                        nc.vector.tensor_copy(yt.rearrange("p (h n) -> p h n", h=2), ps[0:CAP, 4:6, :])\
                            .then_inc(yt_copied, 1)

            def ada_all():
                with nc.vector.Fori(0, ADA) as r:
                    for s in range(2):
                        i = r * 2 + s
                        dve.wait_ge(ada_in[s], r * 16 + 16)
                        dve.wait_ge(mod_ready, r * 2 + s)
                        for k in range(KB):
                            src = ada[:, s, k * COLS:(k + 1) * COLS]
                            c = silu_c[:, k:k + 1]
                            if k == 0:
                                ins = nc.vector.tensor_scalar(acc[:, s, :], src, c, None, ALU.mult)
                            else:
                                ins = nc.vector.scalar_tensor_tensor(acc[:, s, :], src, c, acc[:, s, :],
                                                                     ALU.mult, ALU.add)
                            ins.then_inc(acc_step, 1)
                            dve.wait_ge(acc_step, r * 16 + (8 * s + k + 1))
                        dve.sem_inc(ada_used, 1)
                        dve.sem_inc(acc_ready, 1)

            def router():
                dve.wait_ge(logit_ready, 1)
                lg, t0, t1, oh1, oh2 = (rt[:, i, :, :] for i in range(5))
                m1, m2 = rt[:, 5, :, 0:1], rt[:, 6, :, 0:1]
                d, e2, g1, g2 = (rt[:, i, :, 0:1] for i in (7, 8, 9, 10))
                idx = rt[:, 11, :, 0:1]
                iota = C("iota").unsqueeze(1).broadcast_to([P, TT, NE])

                def bc(a):
                    return a.broadcast_to([P, TT, NE])

                def tt_(o, a, b, op):
                    after(dve, "dve", nc.vector.tensor_tensor(o, a, b, op))

                def first_max(mx, onehot):
                    after(dve, "dve", nc.vector.tensor_reduce(mx, lg, AX, ALU.max))
                    tt_(t0, lg, bc(mx), ALU.is_lt)
                    after(dve, "dve", nc.vector.tensor_scalar(t0, t0, 1000.0, None, ALU.mult))
                    tt_(t0, t0, iota, ALU.add)
                    after(dve, "dve", nc.vector.tensor_reduce(idx, t0, AX, ALU.min))
                    tt_(onehot, iota, bc(idx), ALU.is_equal)

                after(dve, "dve", nc.vector.tensor_copy(
                    lg, ps[:, 6, 0:TT * NE].rearrange("p (t e) -> p t e", t=TT)))
                first_max(m1, oh1)
                after(dve, "dve", nc.vector.tensor_scalar(t1, oh1, TAKEN, None, ALU.mult))
                tt_(lg, lg, t1, ALU.add)
                first_max(m2, oh2)
                nc.vector.tensor_tensor(d, m2, m1, ALU.subtract).then_inc(route_exp_in, 1)
                dve.wait_ge(route_exp, 1)
                after(dve, "dve", nc.vector.tensor_scalar(t0[:, :, 0:1], e2, 1.0, None, ALU.add))
                after(dve, "dve", nc.vector.reciprocal(g1, t0[:, :, 0:1]))
                tt_(g2, e2, g1, ALU.mult)
                nc.vector.tensor_tensor(lg, oh1, oh2, ALU.add).then_inc(mask_ready, 1)
                tt_(oh1, oh1, bc(g1), ALU.mult)
                tt_(oh2, oh2, bc(g2), ALU.mult)
                tt_(oh1, oh1, oh2, ALU.add)
                dve.wait_ge(mask_ready, 1)
                dve.wait_ge(pos_ready, 1)
                nc.vector.tensor_scalar(wide[:, :], ps[:, 7, TT * NE:(TT + 1) * NE], CAP + 0.5, None,
                                        ALU.is_gt).then_inc(wide_ready, 1)
                after(dve, "dve", nc.vector.tensor_copy(
                    t0, ps[:, 7, 0:TT * NE].rearrange("p (t e) -> p t e", t=TT)))
                for e in range(NE):
                    for tt in range(TT):
                        nc.vector.tensor_scalar(place[:, e, tt, :], C("slots"), rt[:, 1, tt, e:e + 1],
                                                rt[:, 0, tt, e:e + 1], ALU.is_equal, ALU.mult)\
                            .then_inc(place_ready, 1)
                        nc.vector.tensor_scalar(gplace[:, e, tt, :], C("slots"), rt[:, 1, tt, e:e + 1],
                                                rt[:, 3, tt, e:e + 1], ALU.is_equal, ALU.mult)\
                            .then_inc(place_ready, 1)
                for i in range(TT * NE):
                    e, tt = divmod(i, TT)
                    if i >= 2:
                        dve.wait_ge(gate_ready, i - 1)
                    nc.vector.tensor_scalar(diag[:, i % 2, :], C("ident"), rt[:, 3, tt, e:e + 1], None,
                                            ALU.mult).then_inc(diag_ready, 1)
                for b in range(4):
                    dve.wait_ge(gate_ready, 4 * b + 4)
                    after(dve, "dve", nc.vector.tensor_copy(
                        gates[:, 2 * b:2 * b + 2, :],
                        ps[:, b, :].rearrange("p (e t) -> p e t", e=2)))
                dve.sem_inc(gate_copied, 1)

            def modulation():
                dve.wait_ge(mod_ready, 2 * ADA)
                after(dve, "dve", nc.vector.tensor_tensor(
                    mod[:, :, :], ps[:, 7, 0:2 * MODB].rearrange("p (l b) -> p l b", l=2),
                    V("b_ada", 0, 2 * MODB).rearrange("p (l b) -> p l b", l=2), ALU.add))
                for n in range(6):
                    l, j = divmod(n, 3)
                    scale = mod[:, l, (3 * j + 1) * KB:(3 * j + 2) * KB]
                    after(dve, "dve", nc.vector.scalar_tensor_tensor(
                        gs[:, n, :], scale, 1.0, V("norm_g", n * KB, KB), ALU.add, ALU.mult))
                    after(dve, "dve", nc.vector.tensor_scalar(
                        hg[:, n, :], mod[:, l, (3 * j + 2) * KB:(3 * j + 3) * KB],
                        1.0 if j == 1 else 0.5, None, ALU.mult))
                for i in range(8):
                    after(dve, "dve", nc.vector.tensor_scalar(
                        qkg[:, i:i + 1], V("qk_g", i), HD ** -0.5 if i % 2 == 0 else 1.0, None, ALU.mult))
                dve.sem_inc(mod_done, 1)

            dve.wait_ge(silu_c_ready, 1)
            norm(0)
            mixer1(0)
            residual(0)
            ada_all()
            modulation()
            norm(1)
            ffn(0, FF)
            residual(1)
            norm(2)
            mixer1(1)
            residual(2)
            norm(3)
            router()
            moe()
            residual(3)
            norm(4)
            for l in range(2):
                norm(5 + 3 * l)
                ffn(2 + 2 * l, FF)
                residual(4 + 3 * l, 3 * l)
                norm(6 + 3 * l)
                mixer2(2 + l)
                residual(5 + 3 * l, 3 * l + 1)
                norm(7 + 3 * l)
                ffn(3 + 2 * l, FF)
                residual(6 + 3 * l, 3 * l + 2)

        @block.tensor
        def _(pe):
            mm = nc.tensor.matmul
            pe.wait_ge(loaded, 16 * 5)
            pe.wait_ge(const_set, 5)
            tile = [0]

            def take():
                i = tile[0]
                tile[0] += 1
                pe.wait_ge(tile_in[i % NS], 16 * (i // NS + 1))
                return ring[:, i % NS, :]

            def norm(n):
                for k in range(KB):
                    if k % 2 == 0:
                        pe.wait_ge(sq_ready, 4 * n + k // 2 + 1)
                    ins = mm(SS[:, 0:T], ones[:, :], sq[:, k, :], start=k == 0, stop=k == KB - 1)
                ins.then_inc(ss_ready, 1)

            h_norms = [0, 1, 2, 3, 5, 6, 7, 8, 9, 10]

            def wait_h(n, k):
                pe.wait_ge(h_ready, KB * h_norms.index(n) + k + 1)

            def inproj(m, n):
                u = UNITS_BEFORE[m]
                for i in range(IN1_F if m < 2 else IN2_F):
                    w = take().rearrange("p (k f) -> p k f", k=KB)
                    for b in range(FB):
                        if u >= 4:
                            pe.wait_ge(in_copied, u - 3)
                        for k in range(KB):
                            if i == 0 and b == 0:
                                wait_h(n, k)
                            ins = mm(ps[:, u % 4, 0:T], w[:, k, b * P:(b + 1) * P], hT[:, k, :],
                                     start=k == 0, stop=k == KB - 1)
                        last = unit_tile(m, u - UNITS_BEFORE[m])[1]
                        ins.then_inc(tile_used if last else in_ready, 1)
                        u += 1
                for cols in (IN1_V if m < 2 else IN2_V):
                    w = take().rearrange("p (k f) -> p k f", k=KB)
                    for tt in range(TT):
                        pe.wait_ge(in_copied, u - 3)
                        for k in range(KB):
                            ins = mm(ps[:, u % 4, 0:cols], hT[:, k, tt * P:(tt + 1) * P], w[:, k, 0:cols],
                                     start=k == 0, stop=k == KB - 1)
                        last = unit_tile(m, u - UNITS_BEFORE[m])[1]
                        ins.then_inc(tile_used if last else in_ready, 1)
                        u += 1

            def outproj(m):
                for i in range(OUTP):
                    w = take().rearrange("p (k f) -> p k f", k=KB)
                    for b in range(min(FB, KB - i * FB)):
                        for k in range(KB):
                            if i == 0 and b == 0:
                                pe.wait_ge(cat_ready, KB * m + k + 1)
                            ins = mm(Y[:, i * FB + b, :], w[:, k, b * P:(b + 1) * P], cat[:, k, :],
                                     start=k == 0, stop=k == KB - 1)
                    ins.then_inc(tile_used, 1)

            def scores(u, tt, qb, kb):
                nk = P * (tt + 1)
                if u:
                    pe.wait_ge(s_used, u)
                for h in range(4):
                    r = (h % 2) * HD
                    ins = mm(ps[:, h % 2, (h // 2) * T:(h // 2) * T + nk],
                             proj[r:r + HD, qb + h // 2, tt * P:(tt + 1) * P],
                             proj[r:r + HD, kb + h // 2, 0:nk], start=True, stop=True)
                ins.then_inc(s_ready, 1)

            def values(u, tt, v0):
                pe.wait_ge(p_ready, u + 1)
                for i in range(4):
                    for kt in range(tt + 1):
                        at = (i % 2) * T + kt * P
                        ins = nc.tensor.transpose(ps[:, 2 + i // 2, at:at + P],
                                                  sm[:, i, kt * P:(kt + 1) * P], C("ident"))
                ins.then_inc(pt_ready, 1)
                pe.wait_ge(pt_copied, u + 1)
                if u >= 2:
                    pe.wait_ge(o_copied, u - 1)
                for h in range(4):
                    r = (h % 2) * HD
                    for kt in range(tt + 1):
                        ins = mm(ps[r:r + HD, 4 + u % 2, (h // 2) * P:(h // 2 + 1) * P],
                                 vtok[:, kt, v0 + h * HD:v0 + (h + 1) * HD], pT[:, 2 * (h % 2) + h // 2, kt, :],
                                 start=kt == 0, stop=kt == tt)
                ins.then_inc(o_ready, 1)

            def mixer1(m, n):
                inproj(m, n)
                pe.wait_ge(in_copied, UNITS_BEFORE[m + 1])
                scores(4 * m, 0, 4, 8)
                pe.wait_ge(d_ready, m + 1)
                for g in range(4):
                    ins = mm(ps[:, 6 + g // 2, (g % 2) * T:(g % 2 + 1) * T], wp[:, 4 * m + g, :],
                             sq[:, g, :], start=True, stop=True)
                    if g % 2:
                        ins.then_inc(z_ready, 1)
                for u in range(4):
                    if u < 3:
                        scores(4 * m + u + 1, (u + 1) % 2, 4 + 2 * ((u + 1) // 2), 8 + 2 * ((u + 1) // 2))
                    values(4 * m + u, u % 2, 256 * (u // 2))
                pe.wait_ge(csq_ready, m + 1)
                for k in range(KB):
                    ins = mm(SS[:, (k // 4) * T:(k // 4 + 1) * T], ones[:, :], sq[:, k, :],
                             start=k % 4 == 0, stop=k % 4 == 3)
                ins.then_inc(css_ready, 1)
                outproj(m)

            def mixer2(m, n):
                l = m - 2
                inproj(m, n)
                pe.wait_ge(qsq_ready, l + 1)
                pe.wait_ge(in_copied, UNITS_BEFORE[m + 1])
                for b in range(8):
                    ins = mm(Y[:, b, :], C("headones"), sq[:, b, :], start=True, stop=True)
                ins.then_inc(qss_ready, 1)
                for b in range(13):
                    i = 13 * l + b
                    pe.wait_ge(qk_ready, 8 * l + min(b + 1, 8))
                    if i >= 2:
                        pe.wait_ge(rope_ready, i - 1)
                    if b < 2:
                        pe.wait_ge(qvar_ready, l + 1)
                    mm(ps[:, i % 2, 0:T], C("rot"), proj[:, b, :], start=True, stop=True)\
                        .then_inc(rot_ready, 1)
                pe.wait_ge(rope_ready, 13 * (l + 1))
                for i in range(16):
                    nn = 16 * l + i
                    tt, j = divmod(i, 8)
                    r = (j % 2) * HD
                    if nn >= 2:
                        pe.wait_ge(ir_ready, nn - 1)
                    mm(ps[:, 6 + nn % 2, 0:P * (tt + 1)], proj[r:r + HD, 8 + j // 2, tt * P:(tt + 1) * P],
                       proj[r:r + HD, 12, 0:P * (tt + 1)], start=True, stop=True).then_inc(il_ready, 1)
                scores(4 * m, 0, 0, 2)
                for u in range(4):
                    if u < 3:
                        q0 = 4 * ((u + 1) // 2)
                        scores(4 * m + u + 1, (u + 1) % 2, q0, q0 + 2)
                    values(4 * m + u, u % 2, 256 * (u // 2))

                def logits(h):
                    nn = 8 * l + h
                    r, b = (h % 2) * HD, h // 2
                    if h >= 2:
                        pe.wait_ge(sp_ready, nn - 1)
                    elif h == 0:
                        pe.wait_ge(s_used, 4 * (m + 1))
                    z = ps[:, nn % 2, :]
                    mm(z[:, 0:T], proj[r:r + HD, 17 + b, 0:P], proj[r:r + HD, 13 + b, :],
                       start=True, stop=True)
                    mm(z[:, T:T + P], proj[r:r + HD, 17 + b, P:T], proj[r:r + HD, 13 + b, P:T],
                       start=True, stop=True).then_inc(zt_ready, 1)

                def weigh(h):
                    nn = 8 * l + h
                    r, b = (h % 2) * HD, h // 2
                    pe.wait_ge(a_ready, nn + 1)
                    if h % 2 == 0:
                        if b >= 2:
                            pe.wait_ge(co_copied, 4 * l + b - 1)
                        else:
                            pe.wait_ge(o_copied, 4 * (m + 1))
                    o = ps[r:r + HD, 4 + b % 2, :]
                    v0 = 512 + h * HD
                    mm(o[:, 0:T], vtok[:, 0, v0:v0 + HD], st_d[:, nn % 2, 3, 0:T], start=True, stop=False)
                    mm(o[:, P:T], vtok[:, 1, v0:v0 + HD], st_d[:, nn % 2, 3, T:T + P], start=False,
                       stop=True).then_inc(co_ready, 1)

                logits(0)
                for h in range(9):
                    nn = 8 * l + h
                    if h < 7:
                        logits(h + 1)
                    if h < 8:
                        pe.wait_ge(spm_ready, nn + 1)
                        if h >= 2:
                            pe.wait_ge(arg_ready, nn - 1)
                        elif h == 0:
                            pe.wait_ge(pt_copied, 4 * (m + 1))
                        a = ps[:, 2 + nn % 2, :]
                        spm = st_d[:, nn % 2, 2, :]
                        mm(a[:, 0:T], C("after"), spm[:, 0:T], start=True, stop=False)
                        mm(a[:, P:T], ones[:, :], spm[:, T:T + P], start=False, stop=True)
                        mm(a[:, T:T + P], C("after"), spm[:, T:T + P], start=True, stop=True)\
                            .then_inc(af_ready, 1)
                    if h > 0:
                        weigh(h - 1)
                pe.wait_ge(csq_ready, m + 1)
                for k in range(KB):
                    ins = mm(Y[:, k, :], C("headones"), sq[:, k, :], start=True, stop=True)
                ins.then_inc(css_ready, 1)
                pe.wait_ge(cvar_ready, m + 1)
                outproj(m)

            def ffn(f, n, norm_n):
                base = chunks_before(f)
                t0 = tile[0]

                def up(s, c, n_in, first=False, wait_bank=True):
                    pe.wait_ge(tile_in[s], n_in)
                    w = ring[:, s, 0:2 * KB * P].rearrange("p (g k f) -> p g k f", g=2, k=KB)
                    b = s_parity[0] = (s - t0) % 2
                    if wait_bank:
                        pe.wait_ge(hid_ready, c - 1)
                    for g in range(2):
                        for k in range(KB):
                            if first and g == 0:
                                wait_h(norm_n, k)
                            ins = mm(ps[:, 4 + b, g * T:(g + 1) * T], w[:, g, k, :], hT[:, k, :],
                                     start=k == 0, stop=k == KB - 1)
                    ins.then_inc(gu_ready, 1)

                def down(s, c, first=False, last=False):
                    pe.wait_ge(hid_ready, c + 1)
                    w = ring[:, s, 2 * KB * P:].rearrange("p (d f) -> p d f", d=KB)
                    b = (s - t0) % 2
                    for d in range(KB):
                        ins = mm(Y[:, d, :], w[:, d, :], hid[:, b, :], start=first and d % 2 == 0,
                                 stop=last, skip_group_check=True)
                    ins.then_inc(tile_used, 1)

                s_parity = [0]
                lead, rounds = chunk_loop(n, 2)
                for c in range(lead):
                    i = t0 + c
                    up(i % NS, base + c, 16 * (i // NS + 1), first=c == 0, wait_bank=base + c >= 2)
                    if c:
                        down((i - 1) % NS, base + c - 1, first=c == 1)
                with nc.tensor.Fori(0, rounds) as r:
                    for j in range(NS):
                        i = t0 + lead + j
                        up(i % NS, r * NS + (base + lead + j), r * 16 + 16 * (i // NS + 1))
                        down((i - 1) % NS, r * NS + (base + lead + j - 1))
                down((t0 + n - 1) % NS, base + n - 1, last=True)
                tile[0] = t0 + n

            def ada_all():
                with nc.tensor.Fori(0, ADA) as r:
                    for s in range(2):
                        pe.wait_ge(acc_ready, r * 2 + (s + 1))
                        for b in range(FB):
                            ins = mm(ps[:, 7, bass.ds(r * (2 * FB) + (s * FB + b), 1)],
                                     acc[:, s, b * P:(b + 1) * P], ones[:, 0:1], start=True, stop=True)
                        ins.then_inc(mod_ready, 1)

            def router():
                for tt in range(TT):
                    for k in range(KB):
                        if tt == 0:
                            wait_h(3, k)
                        ins = mm(ps[:, 6, tt * NE:(tt + 1) * NE], hT[:, k, tt * P:(tt + 1) * P],
                                 wr[:, k, :], start=k == 0, stop=k == KB - 1)
                ins.then_inc(logit_ready, 1)
                for i in range(4):
                    if i >= 2:
                        pe.wait_ge(ht_copied, i - 1)
                    for j in range(4):
                        ins = nc.tensor.transpose(ps[:, 4 + i % 2, j * P:(j + 1) * P],
                                                  hT[:, 4 * (i % 2) + j, (i // 2) * P:(i // 2 + 1) * P],
                                                  C("ident"))
                    ins.then_inc(ht_ready, 1)
                pe.wait_ge(mask_ready, 1)
                m0, m1 = rt[:, 0, 0, :], rt[:, 0, 1, :]
                before = C("strict")[:, 0:P]
                mm(ps[:, 7, 0:NE], before, m0, start=True, stop=True)
                mm(ps[:, 7, NE:2 * NE], before, m1, start=True, stop=False)
                mm(ps[:, 7, NE:2 * NE], ones[:, :], m0, start=False, stop=True)
                mm(ps[:, 7, 2 * NE:3 * NE], ones[:, :], m0, start=True, stop=False)
                mm(ps[:, 7, 2 * NE:3 * NE], ones[:, :], m1, start=False, stop=True).then_inc(pos_ready, 1)
                for i in range(4):
                    pe.wait_ge(ht_copied, min(4, 3 + i))
                    if i >= 2:
                        pe.wait_ge(gp_copied, i - 1)
                    for j in range(4):
                        e, tt = 2 * i + j // 2, j % 2
                        pe.wait_ge(place_ready, 4 * e + 2 * tt + 2)
                        ins = nc.tensor.transpose(ps[0:CAP, 4 + i % 2, j * P:(j + 1) * P],
                                                  gplace[:, e, tt, :], C("ident"))
                    ins.then_inc(gp_ready, 1)
                for i in range(TT * NE):
                    e, tt = divmod(i, TT)
                    pe.wait_ge(diag_ready, i + 1)
                    at = (e % 2) * T + tt * P
                    mm(ps[:, e // 2, at:at + P], ones[:, :], diag[:, i % 2, :], start=True, stop=True)\
                        .then_inc(gate_ready, 1)
                pe.wait_ge(gate_copied, 1)
                pe.wait_ge(gp_copied, 4)

            def moe():
                base = chunks_before(1)
                t0 = STARTS[5]
                assert FX % NS == 0

                def up(s, c, n_in, act_in, width):
                    pe.wait_ge(tile_in[s], n_in)
                    w = ring[:, s, 0:2 * KB * P].rearrange("p (g k f) -> p g k f", g=2, k=KB)
                    b = (s - t0) % 2
                    pe.wait_ge(hid_ready, c - 1)
                    for g in range(2):
                        for k in range(KB):
                            ins = mm(ps[:, 4 + b, g * width:(g + 1) * width], w[:, g, k, :], act_in[:, k, :],
                                     start=k == 0, stop=k == KB - 1)
                    ins.then_inc(gu_ready, 1)

                def down(s, c, wide_path, first=False):
                    pe.wait_ge(hid_ready, c + 1)
                    w = ring[:, s, 2 * KB * P:].rearrange("p (d f) -> p d f", d=KB)
                    b = (s - t0) % 2
                    for d in range(KB):
                        if wide_path:
                            ins = mm(Y[:, d, :], w[:, d, :], hid[:, b, :], start=False, stop=False,
                                     skip_group_check=True)
                        else:
                            ins = mm(ps[:, 6 + d // 4, (d % 4) * CAP:(d % 4 + 1) * CAP], w[:, d, :],
                                     hid[:, b, 0:CAP], start=first and d % 4 == 0, stop=False,
                                     skip_group_check=True)
                    ins.then_inc(tile_used, 1)

                def expert(e, wide_path):
                    act_in, width = (hT, T) if wide_path else (he, CAP)

                    def at(c):
                        i = t0 + c
                        return i % NS, e * FX + (base + c), e * (16 * FX // NS) + 16 * (i // NS + 1)

                    lead = NS
                    for c in range(lead):
                        s, n, n_in = at(c)
                        up(s, n, n_in, act_in, width)
                        if c:
                            s, n, _ = at(c - 1)
                            down(s, n, wide_path, first=c == 1)
                    with nc.tensor.Fori(0, FX // NS - 1) as r:
                        for j in range(NS):
                            s, n, n_in = at(lead + j)
                            up(s, r * NS + n, r * 16 + n_in, act_in, width)
                            s, n, _ = at(lead + j - 1)
                            down(s, r * NS + n, wide_path)
                    s, n, _ = at(FX - 1)
                    down(s, n, wide_path)

                for b in range(4):
                    mm(ps[:, b, :], ones[0:1, :], zeros[0:1, :], start=True, stop=False,
                       skip_group_check=True)
                pe.wait_ge(wide_ready, 1)
                with nc.tensor.Fori(0, NE) as e:
                    is_wide = nc.tensor.value_load(wide[0:1, bass.ds(e, 1)], min_val=0, max_val=1)
                    with nc.tensor.If(is_wide == 1):
                        expert(e, True)
                        nc.tensor.sem_inc(he_gathered, 1)
                        nc.tensor.sem_inc(yt_ready, 1)
                    with nc.tensor.Else():
                        for k in range(KB):
                            for tt in range(TT):
                                ins = mm(ps[:, 6 + k // 4, (k % 4) * CAP:(k % 4 + 1) * CAP],
                                         htok[:, tt, k * P:(k + 1) * P],
                                         place[:, bass.ds(e, 1), tt, :].rearrange("p a c -> p (a c)"),
                                         start=tt == 0, stop=tt == TT - 1)
                        ins.then_inc(he_gathered, 1)
                        pe.wait_ge(he_ready, e + 1)
                        expert(e, False)
                        pe.wait_ge(ye_ready, e + 1)
                        for d in range(KB):
                            ins = nc.tensor.transpose(ps[0:CAP, 4 + d // 4, (d % 4) * P:(d % 4 + 1) * P],
                                                      ye[:, d, :], C("ident"))
                        ins.then_inc(yt_ready, 1)
                        pe.wait_ge(yt_copied, e + 1)
                        for d in range(KB):
                            mm(Y[:, d, :], yt[:, d * P:(d + 1) * P],
                               scatter[:, bass.ds(e, 1), :].rearrange("p a t -> p (a t)"),
                               start=False, stop=False, skip_group_check=True)
                mm(Y[:, 0, :], ones[0:1, :], zeros[0:1, 0:T], start=False, stop=True,
                   skip_group_check=True).then_inc(moe_done, 1)

            norm(0)
            mixer1(0, 0)
            ada_all()
            norm(1)
            ffn(0, FF, 1)
            norm(2)
            mixer1(1, 2)
            norm(3)
            router()
            moe()
            tile[0] = STARTS[6]
            norm(4)
            for l in range(2):
                norm(5 + 3 * l)
                ffn(2 + 2 * l, FF, 5 + 3 * l)
                norm(6 + 3 * l)
                mixer2(2 + l, 6 + 3 * l)
                norm(7 + 3 * l)
                ffn(3 + 2 * l, FF, 7 + 3 * l)


def _proj_tiles(w):
    f = w.shape[1]
    n = -(-f // COLS)
    w = np.pad(w, ((0, 0), (0, n * COLS - f)))
    return w.reshape(KB, P, n, COLS).transpose(2, 1, 0, 3).reshape(n, P, TILE)


def _ffn_tiles(wg, wu, wd):
    n = wg.shape[1] // P
    g = wg.reshape(KB, P, n, P).transpose(2, 1, 0, 3).reshape(n, P, D)
    u = wu.reshape(KB, P, n, P).transpose(2, 1, 0, 3).reshape(n, P, D)
    return np.concatenate([g, u, wd.reshape(n, P, D)], axis=2)


def _col(v):
    return np.asarray(v).reshape(-1, P).T


def _constants():
    c = np.zeros((P, N_CONST), np.float32)

    def put(name, a):
        at, w = CONST[name]
        c[:, at:at + w] = a.reshape(P, w)

    i = np.arange(P)
    t = np.arange(T)
    put("ident", np.eye(P))
    put("headones", (i[:, None] // HD == i[None, :] // HD).astype(np.float32))
    rot = np.zeros((P, P))
    for h in range(0, P, HD):
        for a in range(8):
            rot[h + a + 8, h + a] = -1.0
            rot[h + a, h + a + 8] = 1.0
    put("rot", rot)
    put("after", (i[:, None] > i[None, :]).astype(np.float32))
    for tt in range(TT):
        q = tt * P + i[:, None]
        k = np.arange(P * (tt + 1))[None, :]
        d = q - k
        put(f"cmask{tt}", np.where(d >= 0, 0.0, NEG))
        put(f"mult{tt}", sum(((d >= 0) & (d <= w) & (d % s == 0)).astype(np.float32)
                             for w, s in ((128, 1), (512, 4), (2048, 16))))
    put("strict", np.concatenate([(i[:, None] < t[None, :]), (P + i[:, None] < t[None, P:])], axis=1)
        .astype(np.float32))
    inv = np.float32(500000.0) ** (-np.arange(0, 16, 2, dtype=np.float32) / np.float32(16))
    ang = t.astype(np.float32)[:, None] * inv.astype(np.float32)[None, :]
    cos, sin = np.ones((P, T), np.float32), np.zeros((P, T), np.float32)
    for h in range(0, P, HD):
        for a in range(16):
            cos[h + a], sin[h + a] = np.cos(ang[:, a % 8]), np.sin(ang[:, a % 8])
    put("cos", cos)
    put("sin", sin)
    put("invcnt", np.broadcast_to(np.concatenate([1.0 / np.minimum(t + 1, w) for w in (2, 4, 8, 16)]),
                                  (P, 4 * T)))
    put("iota", np.broadcast_to(np.arange(NE), (P, NE)))
    put("slots", np.broadcast_to(np.arange(CAP), (P, CAP)))
    return c


def kernel(**inputs):
    import concourse.bacc as bacc
    from concourse.bass_utils import run_bass_kernel_spmd

    a = {k: np.asarray(v) for k, v in inputs.items()}

    stream = np.empty((N_TILES, P, TILE), np.float32)
    at = 0

    def add(tiles):
        nonlocal at
        stream[at:at + len(tiles)] = tiles
        at += len(tiles)

    for l in range(2):
        add(_proj_tiles(a["w_in"][l]))
        add(_proj_tiles(a["w_out"][l]))
        if l == 0:
            add(_ffn_tiles(a["ffn_wg"][0], a["ffn_wu"][0], a["ffn_wd"][0]))
        else:
            for e in range(NE):
                add(_ffn_tiles(a["moe_wg"][0, e], a["moe_wu"][0, e], a["moe_wd"][0, e]))
    for l in range(2):
        w = a["w_in_2"][l]
        qa, ka, va, qb, kb, vb, qi, ki, wi, qc, kc, vc = np.split(
            w, np.cumsum([256, 256, 256, 256, 256, 256, 512, 64, 8, 512, 512]), axis=1)
        w = np.concatenate([qa, ka, qb, kb, qi, ki, ki, qc, kc, va, vb, vc, wi], axis=1)
        f = (a["ffn_w1_2"][l], a["ffn_w3_2"][l], a["ffn_w2_2"][l])
        add(_ffn_tiles(*(x[0] for x in f)))
        add(_proj_tiles(w))
        add(_proj_tiles(a["w_out_2"][l]))
        add(_ffn_tiles(*(x[1] for x in f)))
    assert at == N_TILES
    astream = np.concatenate([_proj_tiles(a["w_ada_2"][l]) for l in range(2)])

    cat_g = np.concatenate([np.concatenate([a["pool_scale"][l], a["attn_gain"][l]]) for l in range(2)])
    qk = np.concatenate([np.tile(a["qk_g_2"], (1, 1, 2)).reshape(-1)])
    vectors = np.concatenate([_col(v) for v in (
        a["norm_mix"], a["norm_ffn"], a["final_norm"], cat_g, a["norm_g_2"], a["out_g_2"], qk,
        a["b_ada_2"], a["c_2"])], axis=1)
    host = {
        "x_in": a["x"][0].T.reshape(KB, P, T).transpose(1, 0, 2),
        "wstream": stream,
        "astream": astream,
        "wpool": a["w_pool"].reshape(8, P, P).transpose(1, 0, 2),
        "wrouter": a["w_router"][0].reshape(KB, P, NE).transpose(1, 0, 2),
        "vectors": vectors,
        "consts": _constants(),
    }
    host = {k: np.ascontiguousarray(v) for k, v in host.items()}
    nc = bacc.Bacc("TRN2", target_bir_lowering=False, num_devices=1)
    args = {k: nc.dram_tensor(k, v.shape, mybir.dt.float32, kind="ExternalInput").ap()
            for k, v in host.items()}
    out = nc.dram_tensor("out", (P, KB, T), mybir.dt.float32, kind="ExternalOutput").ap()
    build(nc, out=out, **args)
    r = run_bass_kernel_spmd(nc, [host], core_ids=[0])
    y = r.results[0]["out"]
    return y.transpose(1, 0, 2).reshape(1, D, T).transpose(0, 2, 1)
```

```python
from contextlib import ExitStack

import concourse.bass as bass
import numpy as np
from concourse import mybir

P = 128
T = 256
D = 1024
KB = D // P
TT = T // P
D_FF = 2816
D_FFX = 3584
NE = 8
TILE = 3072
FB = TILE // KB // P
COLS = FB * P
HD = 64
N_MOD = 9
EPS = 1e-6
NEG = -1e30
TAKEN = -3e38
TOPK = min(256, T // 4)
MODB = N_MOD * KB
CAP = 96

NS = 4
IN1_F, IN1_V = 4, (384, 128)
IN2_F, IN2_V = 7, (384, 384, 264)
IN1 = IN1_F + len(IN1_V)
IN2 = IN2_F + len(IN2_V)
OUTP = -(-KB // FB)
FF = D_FF // P
FX = D_FFX // P
ADA = MODB // FB
ADA_X = 2 * ADA // NE
STREAM = [IN1, OUTP, FF, IN1, OUTP, NE * FX] + [FF, IN2, OUTP, FF] * 2
STARTS = [sum(STREAM[:i]) for i in range(len(STREAM) + 1)]
N_TILES = STARTS[-1]
IN_STAGE = (0, 3, 7, 11)
FFN_STAGE = (2, 5, 6, 9, 10, 13)
MOE_STAGE = 5
SPLITS = [STARTS[i] - (STREAM[MOE_STAGE] if i > MOE_STAGE else 0) for i in range(len(STREAM) + 1)]
SPLIT_INPUTS = ["n0", "c0", "n1", "n2", "c1", "n5", "n6", "c2", "n7", "n8", "n9", "c3", "n10"]
Y_STAGE = (1, 2, 4, 5, 6, 8, 9, 10, 12, 13)

CONST = {}
_at = 0
for _n, _w in (("ident", P), ("headones", P), ("rot", P), ("after", P), ("cmask0", P), ("cmask1", T),
               ("mult0", P), ("mult1", T), ("strict", T + P), ("cos", T), ("sin", T),
               ("invcnt", 4 * 16), ("iota", NE), ("slots", CAP)):
    CONST[_n] = (_at, _w)
    _at += _w
N_CONST = _at
VEC = {}
_at = 0
for _n, _w in (("norm_mix", 2 * KB), ("norm_ffn", 2 * KB), ("final", KB), ("cat_g", 2 * KB),
               ("norm_g", 6 * KB), ("out_g", 2 * KB), ("qk_g", 8), ("b_ada", 2 * MODB), ("c", KB)):
    VEC[_n] = (_at, _w)
    _at += _w
N_VEC = _at


def build(nc, x_in, wstream, astream, wpool, wrouter, vectors, consts, out):
    fp32 = mybir.dt.float32
    fp32r = mybir.dt.float32r
    ALU = mybir.AluOpType
    ACT = mybir.ActivationFunctionType
    AX = mybir.AxisListType.X
    ctx = ExitStack()
    with ctx:
        def sb(name, shape, dtype=fp32):
            return ctx.enter_context(nc.sbuf_tensor(name, shape, dtype))

        def sem(name):
            return ctx.enter_context(nc.semaphore(name))

        first_byte = -(-nc.sbuf_base // 32) * 32
        w_parts = sb("w_parts", [P, 2, 2, TILE], fp32r)
        moe_room = nc.alloc_sbuf_tensor_at("moe_room", [P, 4 * TILE], fp32, offset=first_byte)
        w_hi, w_lo = w_parts[:, 0], w_parts[:, 1]
        ring = sb("ring", [P, NS, TILE])
        xT = sb("xT", [P, KB, T])
        hT = sb("hT", [P, KB, T])
        cat = hT
        a_hi = sb("a_hi", [P, KB, T], fp32r)
        a_lo = sb("a_lo", [P, KB, T], fp32r)
        sq = sb("sq", [P, KB, T])
        proj = sb("proj", [P, 21, T])
        branch = sb("branch", [P, 3 * 4 * (16 + T)])
        upad, *win = (branch[:, i * 4 * (16 + T):(i + 1) * 4 * (16 + T)]
                      .rearrange("p (g t) -> p g t", g=4) for i in range(3))
        vtok = sb("vtok", [P, TT, 1032])
        sm = sb("sm", [P, 4, T])
        pT = sb("pT", [P, 4, TT, P])
        small = sb("small", [P, 64])
        score = branch[:, 0:T]
        relu_l = branch[:, T:3 * T].rearrange("p (b t) -> p b t", b=2)
        selmask = sb("selmask", [P, TT, T])
        top8 = sb("top8", [P, 8])
        st_l = sq[:, 0:6, :].rearrange("p k t -> p (k t)").rearrange("p (b i t) -> p b i t", b=2, i=2)
        st_d = branch[:, 0:2 * 4 * (T + P)].rearrange("p (b i t) -> p b i t", b=2, i=4)
        norm_s = pT[:, 0:2, :, :].rearrange("p a k t -> p a (k t)")
        sg, hid = sm[:, 0:2, :], sm[:, 2:4, :]
        hid_hi = sb("hid_hi", [P, 2, T], fp32r)
        hid_lo = sb("hid_lo", [P, 2, T], fp32r)
        gates = proj[:, 0:NE, :]
        ada = moe_room[:, 0:2 * TILE].rearrange("p (s n) -> p s n", s=2)
        place, gplace = (moe_room[:, 2 * TILE + i * NE * TT * CAP:2 * TILE + (i + 1) * NE * TT * CAP]
                         .rearrange("p (e t c) -> p e t c", e=NE, t=TT) for i in range(2))
        at = 2 * TILE + 2 * NE * TT * CAP
        scatter = moe_room[0:CAP, at:at + NE * T].rearrange("p (e t) -> p e t", e=NE)
        at += NE * T
        acc = moe_room[:, at:at + 2 * COLS].rearrange("p (b f) -> p b f", b=2)
        htok = vtok[:, :, 0:D]
        he = branch[:, 0:KB * CAP].rearrange("p (k c) -> p k c", k=KB)
        ye = branch[:, KB * CAP:2 * KB * CAP].rearrange("p (k c) -> p k c", k=KB)
        yt = branch[0:CAP, 2 * KB * CAP:2 * KB * CAP + D]
        rt = sb("rt", [P, 12, TT, NE])
        diag = proj[:, NE, :].rearrange("p (b t) -> p b t", b=2)
        wide = ctx.enter_context(nc.sbuf_tensor("wide", [P, NE], mybir.dt.int32))
        zeros = sb("zeros", [1, T])
        mod = sb("mod", [P, 2, MODB])
        gs = sb("gs", [P, 6, KB])
        qkg = sb("qkg", [P, 8])
        hg = sb("hg", [P, 6, KB])
        silu_c = sb("silu_c", [P, KB])
        ones = sb("ones", [P, P])
        cst = sb("cst", [P, N_CONST])
        vec = sb("vec", [P, N_VEC])
        wp = proj[:, 16:20, :].rearrange("p (g h) (i f) -> p (g h i) f", g=4, i=2)
        wr = sb("wr", [P, KB, NE])

        def C(name):
            a, w = CONST[name]
            return cst[:, a:a + w]

        def V(name, i=0, n=None):
            a, w = VEC[name]
            return vec[:, a + i:a + i + (n or 1)]

        ps = ctx.enter_context(nc.psum_tensor("ps", [P, 8, 512], fp32))
        Y = ps[:, 0:4, :].rearrange("p b (h t) -> p (b h) t", h=2)
        SS = ps[:, 6, :]

        MOD_AT = 4 * CAP

        tile_in = [sem(f"tile_in{s}") for s in range(NS)]
        tile_used = sem("tile_used")
        hi_ready = sem("hi_ready")
        split_ready = sem("split_ready")
        split_used = sem("split_used")
        ah_ready = sem("ah_ready")
        as_ready = sem("as_ready")
        ada_in = [sem(f"ada_in{s}") for s in range(2)]
        ada_used = sem("ada_used")
        loaded = sem("loaded")
        stored = sem("stored")
        const_set = sem("const_set")
        x_ready = sem("x_ready")
        sq_ready = sem("sq_ready")
        ss_ready = sem("ss_ready")
        var_ready = sem("var_ready")
        std_ready = sem("std_ready")
        normed = sem("normed")
        h_ready = sem("h_ready")
        gu_ready = sem("gu_ready")
        sg_ready = sem("sg_ready")
        hid_ready = sem("hid_ready")
        in_ready = sem("in_ready")
        in_copied = sem("in_copied")
        d_ready = sem("d_ready")
        z_ready = sem("z_ready")
        z_copied = sem("z_copied")
        s_ready = sem("s_ready")
        s_used = sem("s_used")
        max_ready = sem("max_ready")
        sub_ready = sem("sub_ready")
        exp_ready = sem("exp_ready")
        rden_ready = sem("rden_ready")
        p_ready = sem("p_ready")
        pt_ready = sem("pt_ready")
        pt_copied = sem("pt_copied")
        o_ready = sem("o_ready")
        o_copied = sem("o_copied")
        csq_ready = sem("csq_ready")
        css_ready = sem("css_ready")
        cvar_ready = sem("cvar_ready")
        cstd_ready = sem("cstd_ready")
        cat_ready = sem("cat_ready")
        logit_ready = sem("logit_ready")
        route_exp_in = sem("route_exp_in")
        route_exp = sem("route_exp")
        diag_ready = sem("diag_ready")
        gate_ready = sem("gate_ready")
        mask_ready = sem("mask_ready")
        pos_ready = sem("pos_ready")
        wide_ready = sem("wide_ready")
        place_ready = sem("place_ready")
        ht_ready = sem("ht_ready")
        ht_copied = sem("ht_copied")
        gp_ready = sem("gp_ready")
        gp_copied = sem("gp_copied")
        he_gathered = sem("he_gathered")
        he_ready = sem("he_ready")
        ye_ready = sem("ye_ready")
        yt_ready = sem("yt_ready")
        yt_copied = sem("yt_copied")
        gate_copied = sem("gate_copied")
        silu_c_ready = sem("silu_c_ready")
        acc_ready = sem("acc_ready")
        mod_ready = sem("mod_ready")
        acc_step = sem("acc_step")
        hid_raw = sem("hid_raw")
        hid_top = sem("hid_top")
        moe_done = sem("moe_done")
        mod_done = sem("mod_done")
        qsq_ready = sem("qsq_ready")
        qss_ready = sem("qss_ready")
        qvar_ready = sem("qvar_ready")
        qstd_ready = sem("qstd_ready")
        qk_ready = sem("qk_ready")
        rot_ready = sem("rot_ready")
        cos_ready = sem("cos_ready")
        rope_ready = sem("rope_ready")
        il_ready = sem("il_ready")
        ir_ready = sem("ir_ready")
        ir_used = sem("ir_used")
        sel_ready = sem("sel_ready")
        zt_ready = sem("zt_ready")
        zt_used = sem("zt_used")
        l_ready = sem("l_ready")
        sp_ready = sem("sp_ready")
        spm_ready = sem("spm_ready")
        af_ready = sem("af_ready")
        arg_ready = sem("arg_ready")
        a_exp = sem("a_exp")
        a_ready = sem("a_ready")
        co_ready = sem("co_ready")
        co_copied = sem("co_copied")
        chain = {e: sem(f"chain_{e}") for e in ("dve", "act", "pool")}
        counts = {"dve": 0, "act": 0, "pool": 0}

        def after(engine, name, instruction):
            counts[name] += 1
            instruction.then_inc(chain[name], 1)
            engine.wait_ge(chain[name], counts[name])


        h_norms = [0, 1, 2, 3, 5, 6, 7, 8, 9, 10]
        q0_ffn = [0, None, FF, 2 * FF, 3 * FF, 4 * FF]

        def chunks_before(f):
            return [0, FF, FF + NE * FX, 2 * FF + NE * FX, 3 * FF + NE * FX, 4 * FF + NE * FX][f]

        UP = 2 * KB * P

        def ffn_loop(n):
            lead = 2 + (n - 3) % NS
            return lead, (n - 1 - lead) // NS

        def in_units(m):
            f, v = (IN1_F * FB, len(IN1_V) * TT) if m < 2 else (IN2_F * FB, len(IN2_V) * TT)
            return f, v

        UNITS_BEFORE = [0]
        for m in range(4):
            UNITS_BEFORE.append(UNITS_BEFORE[-1] + sum(in_units(m)))

        def up_part(c):
            return 2 * c - 1 if c else 0

        def down_part(c, n):
            return 2 * n - 1 if c == n - 1 else 2 * c + 2

        def unit_tile(m, u):
            feats, _ = in_units(m)
            if u < feats:
                return SPLITS[IN_STAGE[m]] + u // FB, u % FB == FB - 1
            v = u - feats
            return SPLITS[IN_STAGE[m]] + feats // FB + v // TT, v % TT == TT - 1

        not_last = {}
        n_ready = 0
        for m in range(4):
            for u in range(sum(in_units(m))):
                n_ready += not unit_tile(m, u)[1]
                not_last[m, u] = n_ready

        def wait_unit(engine, m, u):
            i, last = unit_tile(m, u)
            if last:
                engine.wait_ge(split_used, i + 1)
            else:
                engine.wait_ge(in_ready, not_last[m, u])

        block = ctx.enter_context(nc.Block())

        @block.sync
        def _(sp):
            for dst, src in ((vec[:, :], vectors), (xT[:, :, :], x_in), (cst[:, :], consts),
                             (wp[:, :, :], wpool), (wr[:, :, :], wrouter)):
                sp.dma_start(dst, src).then_inc(loaded, 16)

            def load(s, i):
                sp.dma_start(ring[:, s, :], wstream[i]).then_inc(tile_in[s], 16)

            for s in range(NS):
                load(s, s)
            rounds = N_TILES // NS
            with nc.sync.Fori(1, rounds) as r:
                for s in range(NS):
                    sp.wait_ge(tile_used, r * NS + (s - NS + 1))
                    sp.dma_start(ring[:, s, :], wstream[bass.ds(r * NS + s, 1), :, :]
                                 .rearrange("a p n -> p (a n)")).then_inc(tile_in[s], 16)
            for i in range(rounds * NS, N_TILES):
                sp.wait_ge(tile_used, i - NS + 1)
                load(i % NS, i)
            sp.wait_ge(x_ready, KB * 11)
            sp.dma_start(out, xT[:, :, :]).then_inc(stored, 16)
            sp.wait_ge(stored, 16)

        @block.gpsimd
        def _(pool):
            nc.gpsimd.memset(ones[:, :], 1.0).then_inc(const_set, 1)
            nc.gpsimd.memset(win[0][:, :, 0:16], 0.0).then_inc(const_set, 1)
            nc.gpsimd.memset(win[1][:, :, 0:16], 0.0).then_inc(const_set, 1)
            nc.gpsimd.memset(upad[:, :, 0:16], 0.0).then_inc(const_set, 1)
            nc.gpsimd.memset(zeros[:, :], 0.0).then_inc(const_set, 1)
            pool.wait_ge(const_set, 5)
            pool.wait_ge(loaded, 16 * 5)

            def load_ada(s, i):
                pool.dma_start(ada[:, s, :], astream[i]).then_inc(ada_in[s], 16)

            def ada_stream():
                pool.wait_ge(place_ready, 2 * NE * TT)
                for s in range(2):
                    load_ada(s, s)
                with nc.gpsimd.Fori(1, ADA) as r:
                    for s in range(2):
                        pool.wait_ge(ada_used, r * 2 + (s - 1))
                        pool.dma_start(ada[:, s, :], astream[bass.ds(r * 2 + s, 1), :, :]
                                       .rearrange("a p n -> p (a n)")).then_inc(ada_in[s], 16)

            def windows(m):
                pool.wait_ge(in_copied, UNITS_BEFORE[m] + 4)
                src = upad
                for i, step in enumerate((1, 2, 4, 8)):
                    dst = win[i % 2]
                    after(pool, "pool", nc.gpsimd.tensor_tensor(
                        dst[:, i:4, 16:16 + T], src[:, i:4, 16:16 + T],
                        src[:, i:4, 16 - step:16 - step + T], ALU.add))
                    after(pool, "pool", nc.gpsimd.tensor_scalar(
                        sq[:, i, 16:T], dst[:, i, 32:16 + T], 0.5 / step, None, ALU.mult))
                    after(pool, "pool", nc.gpsimd.tensor_tensor(
                        sq[:, i, 0:16], dst[:, i, 16:32], C("invcnt")[:, i * 16:(i + 1) * 16], ALU.mult))
                    src = dst
                nc.gpsimd.tensor_tensor(sq[:, 0:4, :], sq[:, 0:4, :], upad[:, :, 16:16 + T],
                                        ALU.subtract).then_inc(d_ready, 1)

            def softmax_unit(u, tt):
                nk = P * (tt + 1)
                pool.wait_ge(max_ready, u + 1)
                nc.gpsimd.tensor_tensor(sm[:, :, 0:nk], sm[:, :, 0:nk],
                                        small[:, 0:4].unsqueeze(2).broadcast_to([P, 4, nk]),
                                        ALU.subtract).then_inc(sub_ready, 1)
                pool.wait_ge(rden_ready, u + 1)
                nc.gpsimd.tensor_tensor(sm[:, :, 0:nk], sm[:, :, 0:nk],
                                        small[:, 8:12].unsqueeze(2).broadcast_to([P, 4, nk]),
                                        ALU.mult).then_inc(p_ready, 1)

            def ropes(m):
                n = 13 * (m - 2)
                for b in range(13):
                    pool.wait_ge(rot_ready, n + b + 1)
                    nc.gpsimd.tensor_tensor(proj[:, b, :], proj[:, b, :], C("cos"), ALU.mult)\
                        .then_inc(cos_ready, 1)

            def sticks(m):
                n = 8 * (m - 2)
                for h in range(9):
                    if h < 8:
                        pool.wait_ge(sp_ready, n + h + 1)
                        nc.gpsimd.tensor_tensor(st_d[:, h % 2, 2, :], st_d[:, h % 2, 0, :],
                                                C("strict"), ALU.mult).then_inc(spm_ready, 1)
                    if h > 0:
                        g = h - 1
                        pool.wait_ge(a_exp, n + g + 1)
                        nc.gpsimd.tensor_tensor(st_d[:, g % 2, 3, :], st_d[:, g % 2, 3, :],
                                                C("strict"), ALU.mult).then_inc(a_ready, 1)

            for m in range(2):
                windows(m)
                for u in range(4):
                    softmax_unit(4 * m + u, u % 2)
            ada_stream()
            for m in range(2, 4):
                ropes(m)
                for u in range(4):
                    softmax_unit(4 * m + u, u % 2)
                sticks(m)

        @block.scalar
        def _(act):
            act.wait_ge(loaded, 16 * 5)
            act.wait_ge(const_set, 5)

            def norm(n, meanwhile=None):
                if n:
                    act.wait_ge(x_ready, KB * n)
                for i in range(4):
                    nc.scalar.activation(sq[:, 2 * i:2 * i + 2, :], xT[:, 2 * i:2 * i + 2, :],
                                         ACT.Square).then_inc(sq_ready, 1)
                if meanwhile:
                    meanwhile()
                act.wait_ge(var_ready, n + 1)
                nc.scalar.activation(norm_s[:, 0, :], norm_s[:, 0, :], ACT.Sqrt).then_inc(std_ready, 1)
                if n < 5:
                    if n < 3:
                        split_input(f"n{n}", hT, h_ready, KB * n)
                else:
                    for k in range(KB):
                        act.wait_ge(normed, KB * (n - 5) + k + 1)
                        shift = mod[:, (n - 5) // 3, 3 * ((n - 5) % 3) * KB + k:
                                    3 * ((n - 5) % 3) * KB + k + 1]
                        nc.scalar.activation(hT[:, k, :], sq[:, k, :], ACT.Identity, bias=shift)\
                            .then_inc(h_ready, 1)
                        nc.scalar.activation(a_hi[:, k, :], sq[:, k, :], ACT.Identity, bias=shift)\
                            .then_inc(ah_ready, 1)

            def split_input(name, src, ready, before):
                for k in range(KB):
                    act.wait_ge(ready, before + k + 1)
                    nc.scalar.activation(a_hi[:, k, :], src[:, k, :], ACT.Copy).then_inc(ah_ready, 1)

            def hi(stage, i, a, b):
                act.wait_ge(tile_in[(STARTS[stage] + i) % NS], 16 * ((STARTS[stage] + i) // NS + 1))
                q = SPLITS[stage] + i
                nc.scalar.activation(w_hi[:, q % 2, a:b], ring[:, (STARTS[stage] + i) % NS, a:b], ACT.Copy)\
                    .then_inc(hi_ready, 1)

            def hi_tile(stage, i):
                if i < STREAM[stage]:
                    q = SPLITS[stage] + i
                    if q >= 2:
                        act.wait_ge(split_used, q - 1)
                    for h in range(2):
                        hi(stage, i, h * TILE // 2, (h + 1) * TILE // 2)

            def hi_outproj(stage):
                for i in range(2, OUTP):
                    hi_tile(stage, i)

            def in_copies(m):
                feats, _ = in_units(m)
                u = UNITS_BEFORE[m]
                stage = IN_STAGE[m]
                for b in range(feats):
                    wait_unit(act, m, b)
                    src = ps[:, u % 4, 0:T]
                    if m < 2 and b < 4:
                        dst, scale = upad[:, b, 16:16 + T], 1.0
                    else:
                        isq = (4 <= b < 8) if m < 2 else (13 <= b < 17)
                        dst, scale = proj[:, b, :], (HD ** -0.5 if isq else 1.0)
                    nc.scalar.activation(dst, src, ACT.Copy, scale=scale).then_inc(in_copied, 1)
                    u += 1
                    if b % FB == FB - 1:
                        hi_tile(stage, b // FB + 2)
                at = 0
                for w in (IN1_V if m < 2 else IN2_V):
                    for tt in range(TT):
                        wait_unit(act, m, u - UNITS_BEFORE[m])
                        nc.scalar.activation(vtok[:, tt, at:at + w], ps[:, u % 4, 0:w], ACT.Copy)\
                            .then_inc(in_copied, 1)
                        u += 1
                    at += w
                    hi_tile(stage, unit_tile(m, u - 1 - UNITS_BEFORE[m])[0] - SPLITS[stage] + 2)
                for i in range(2):
                    hi_tile(stage + 1, i)

            def softmax_unit(u, tt, block0):
                nk = P * (tt + 1)
                act.wait_ge(sub_ready, u + 1)
                nc.scalar.activation(sm[:, :, 0:nk], sm[:, :, 0:nk], ACT.Exp).then_inc(exp_ready, 1)
                act.wait_ge(pt_ready, u + 1)
                if u:
                    act.wait_ge(o_ready, u)
                nc.scalar.activation(
                    pT[:, :, 0:tt + 1, :],
                    ps[:, 2:4, :].rearrange("p b (h k t) -> p (b h) k t", h=2, k=TT)[:, :, 0:tt + 1, :],
                    ACT.Copy).then_inc(pt_copied, 1)
                act.wait_ge(o_ready, u + 1)
                nc.scalar.activation(
                    cat[:, block0:block0 + 2, tt * P:(tt + 1) * P],
                    ps[:, 4 + u % 2, 0:T].rearrange("p (b t) -> p b t", b=2), ACT.Copy)\
                    .then_inc(o_copied, 1)

            def cat_norm(m):
                act.wait_ge(o_copied, 4 * (m + 1))
                if m >= 2:
                    act.wait_ge(co_copied, 4 * (m - 1))
                else:
                    act.wait_ge(z_copied, 2 * (m + 1))
                nc.scalar.activation(sq[:, :, :], cat[:, :, :], ACT.Square).then_inc(csq_ready, 1)
                act.wait_ge(cvar_ready, m + 1)
                n = 2 if m < 2 else KB
                nc.scalar.activation(sq[:, 0:n, :], sq[:, 0:n, :], ACT.Sqrt).then_inc(cstd_ready, 1)
                split_input(f"c{m}", cat, cat_ready, KB * m)
                hi_outproj(IN_STAGE[m] + 1)

            def mixer1(m):
                in_copies(m)
                for i in range(2):
                    act.wait_ge(z_ready, 2 * m + i + 1)
                    nc.scalar.activation(cat[:, 2 * i:2 * i + 2, :],
                                         ps[:, 6 + i, :].rearrange("p (b t) -> p b t", b=2),
                                         ACT.Copy).then_inc(z_copied, 1)
                for u in range(4):
                    softmax_unit(4 * m + u, u % 2, 4 + 2 * (u // 2))
                cat_norm(m)

            def mixer2(m):
                in_copies(m)
                act.wait_ge(in_copied, UNITS_BEFORE[m] + 8)
                nc.scalar.activation(sq[:, :, :], proj[:, 0:8, :], ACT.Square).then_inc(qsq_ready, 1)
                act.wait_ge(qvar_ready, m - 1)
                nc.scalar.activation(sq[:, :, :], sq[:, :, :], ACT.Sqrt).then_inc(qstd_ready, 1)
                for i in range(16):
                    n = 16 * (m - 2) + i
                    nk = P * (i // 8 + 1)
                    act.wait_ge(il_ready, n + 1)
                    if n >= 2:
                        act.wait_ge(ir_used, n - 1)
                    nc.scalar.activation(relu_l[:, n % 2, 0:nk], ps[:, 6 + n % 2, 0:nk], ACT.Relu)\
                        .then_inc(ir_ready, 1)
                for u in range(4):
                    softmax_unit(4 * m + u, u % 2, 2 * (u // 2))
                for h in range(9):
                    n = 8 * (m - 2) + h
                    if h < 8:
                        act.wait_ge(zt_ready, n + 1)
                        if n >= 2:
                            act.wait_ge(sp_ready, n - 1)
                        z = ps[:, n % 2, 0:T + P]
                        after(act, "act", nc.scalar.activation(st_l[:, n % 2, 0, :], z, ACT.Abs))
                        after(act, "act", nc.scalar.activation(st_l[:, n % 2, 0, :], st_l[:, n % 2, 0, :],
                                                               ACT.Exp, scale=-1.0))
                        nc.scalar.activation(st_l[:, n % 2, 1, :], st_l[:, n % 2, 0, :], ACT.Ln,
                                             bias=1.0).then_inc(l_ready, 1)
                    if h > 0:
                        g = n - 1
                        act.wait_ge(arg_ready, g + 1)
                        if g >= 2:
                            act.wait_ge(co_ready, g - 1)
                        nc.scalar.activation(st_d[:, g % 2, 3, :], st_d[:, g % 2, 1, :], ACT.Exp,
                                             scale=-1.0).then_inc(a_exp, 1)
                        if g % 2 and h >= 3:
                            copy_sticks(m, (h - 1) // 2 - 1)
                copy_sticks(m, 3)
                cat_norm(m)

            def copy_sticks(m, pair):
                act.wait_ge(co_ready, 8 * (m - 2) + 2 * pair + 2)
                nc.scalar.activation(cat[:, 4 + pair, :], ps[:, 4 + pair % 2, 0:T], ACT.Copy)\
                    .then_inc(co_copied, 1)

            def hi_first(f):
                stage = FFN_STAGE[f]
                for c in range(2):
                    act.wait_ge(split_used, SPLITS[stage] + c - 1)
                    hi(stage, c, 0, UP)

            def ffn(f, n):
                base, stage = chunks_before(f), FFN_STAGE[f]
                q0, i0 = SPLITS[stage], STARTS[stage]

                def chunk(c, r=0, last=False):
                    s, nx = (i0 + c) % NS, (i0 + c + 1) % NS
                    rt_ = 16 // NS
                    if c and not last:
                        act.wait_ge(gu_ready, r + (base + c))
                        act.wait_ge(tile_in[nx], r * rt_ + 16 * ((i0 + c + 1) // NS + 1))
                        nc.scalar.activation(w_hi[:, (q0 + c + 1) % 2, 0:UP], ring[:, nx, 0:UP], ACT.Copy)\
                            .then_inc(hi_ready, 1)
                    act.wait_ge(split_used, r + (q0 + c - 1))
                    act.wait_ge(tile_in[s], r * rt_ + 16 * ((i0 + c) // NS + 1))
                    nc.scalar.activation(w_hi[:, (q0 + c) % 2, UP:TILE], ring[:, s, UP:TILE], ACT.Copy)\
                        .then_inc(hi_ready, 1)
                    act.wait_ge(gu_ready, r + (base + c + 1))
                    if base + c >= 2:
                        act.wait_ge(hid_ready, r + (base + c - 1))
                    nc.scalar.activation(sg[:, c % 2, :], ps[:, 4 + c % 2, 0:T], ACT.Silu)\
                        .then_inc(sg_ready, 1)

                lead, rounds = ffn_loop(n)
                for c in range(lead):
                    chunk(c)
                with nc.scalar.Fori(0, rounds) as r:
                    for j in range(NS):
                        chunk(lead + j, r * NS)
                chunk(n - 1, last=True)

            def moe():
                base = chunks_before(1)

                def chunk(b, c, width):
                    act.wait_ge(gu_ready, c + 1)
                    act.wait_ge(hid_ready, c - 1)
                    nc.scalar.activation(sg[:, b, 0:width], ps[:, 4 + b, 0:width], ACT.Silu)\
                        .then_inc(sg_ready, 1)

                act.wait_ge(wide_ready, 1)
                with nc.scalar.Fori(0, NE) as e:
                    is_wide = nc.scalar.value_load(wide[0:1, bass.ds(e, 1)], min_val=0, max_val=1)
                    with nc.scalar.If(is_wide == 1):
                        with nc.scalar.Fori(0, FX // NS) as r:
                            for j in range(NS):
                                chunk(j % 2, e * FX + r * NS + (base + j), T)
                        act.sem_inc(he_ready, 1)
                        act.sem_inc(ye_ready, 1)
                    with nc.scalar.Else():
                        act.wait_ge(he_gathered, e + 1)
                        nc.scalar.activation(
                            he.rearrange("p (h k) c -> p h (k c)", h=2), ps[:, 6:8, 0:4 * CAP], ACT.Copy)\
                            .then_inc(he_ready, 1)
                        with nc.scalar.Fori(0, FX // NS) as r:
                            for j in range(NS):
                                chunk(j % 2, e * FX + r * NS + (base + j), CAP)
                        act.wait_ge(tile_used, e * FX + (STARTS[5] + FX))
                        nc.scalar.activation(
                            ye.rearrange("p (h k) c -> p h (k c)", h=2), ps[:, 6:8, 0:4 * CAP], ACT.Copy)\
                            .then_inc(ye_ready, 1)

            nc.scalar.activation(silu_c[:, :], V("c", 0, KB), ACT.Silu).then_inc(silu_c_ready, 1)
            def tiles_first(stage):
                return lambda: [hi_tile(stage, i) for i in range(2)]

            norm(0, tiles_first(0))
            mixer1(0)
            norm(1, lambda: hi_first(0))
            ffn(0, FF)
            norm(2, tiles_first(IN_STAGE[1]))
            mixer1(1)
            norm(3)
            act.wait_ge(route_exp_in, 1)
            nc.scalar.activation(rt[:, 8, :, 0:1], rt[:, 7, :, 0:1], ACT.Exp).then_inc(route_exp, 1)
            for i in range(4):
                act.wait_ge(ht_ready, i + 1)
                nc.scalar.activation(htok[:, i // 2, (i % 2) * 512:(i % 2 + 1) * 512], ps[:, 4 + i % 2, :],
                                     ACT.Copy).then_inc(ht_copied, 1)
            for i in range(4):
                act.wait_ge(gp_ready, i + 1)
                nc.scalar.activation(scatter[:, 2 * i:2 * i + 2, :],
                                     ps[0:CAP, 4 + i % 2, :].rearrange("p (e t) -> p e t", e=2),
                                     ACT.Copy).then_inc(gp_copied, 1)
            moe()
            act.wait_ge(mod_done, 1)
            act.wait_ge(moe_done, 1)
            norm(4, lambda: hi_first(2))
            for l in range(2):
                norm(5 + 3 * l, (lambda: hi_first(4)) if l else None)
                ffn(2 + 2 * l, FF)
                norm(6 + 3 * l, tiles_first(IN_STAGE[2 + l]))
                mixer2(2 + l)
                norm(7 + 3 * l, lambda: hi_first(3 + 2 * l))
                ffn(3 + 2 * l, FF)

        @block.vector
        def _(dve):
            dve.wait_ge(loaded, 16 * 5)
            dve.wait_ge(const_set, 5)

            def mean_eps(dst, src, inv, signal):
                nc.vector.tensor_scalar(dst, src, inv, EPS, ALU.mult, ALU.add).then_inc(signal, 1)

            def norm(n, meanwhile=None):
                if meanwhile:
                    meanwhile()
                dve.wait_ge(ss_ready, n + 1)
                mean_eps(norm_s[:, 0, :], SS[:, 0:T], 1.0 / D, var_ready)
                dve.wait_ge(std_ready, n + 1)
                after(dve, "dve", nc.vector.reciprocal(norm_s[:, 1, :], norm_s[:, 0, :]))
                for k in range(KB):
                    if n < 4:
                        g = V("norm_ffn" if n % 2 else "norm_mix", (n // 2) * KB + k)
                        nc.vector.scalar_tensor_tensor(hT[:, k, :], xT[:, k, :], g, norm_s[:, 1, :],
                                                       ALU.mult, ALU.mult).then_inc(h_ready, 1)
                    elif n == 4:
                        nc.vector.scalar_tensor_tensor(xT[:, k, :], xT[:, k, :], V("final", k),
                                                       norm_s[:, 1, :], ALU.mult, ALU.mult)\
                            .then_inc(x_ready, 1)
                    else:
                        nc.vector.scalar_tensor_tensor(sq[:, k, :], xT[:, k, :],
                                                       gs[:, n - 5, k:k + 1], norm_s[:, 1, :],
                                                       ALU.mult, ALU.mult).then_inc(normed, 1)
                if n not in (3, 4):
                    split_input(f"n{n}", hT)

            def split_input(name, src):
                e = SPLIT_INPUTS.index(name)
                for k in range(KB):
                    dve.wait_ge(ah_ready, KB * e + k + 1)
                    if name[0] == "n":
                        dve.wait_ge(h_ready, KB * h_norms.index(int(name[1:])) + k + 1)
                    else:
                        dve.wait_ge(cat_ready, KB * int(name[1:]) + k + 1)
                    nc.vector.tensor_tensor(a_lo[:, k, :], src[:, k, :], a_hi[:, k, :], ALU.subtract)\
                        .then_inc(as_ready, 1)

            def lo(stage, i, a, b, n, free):
                dve.wait_ge(hi_ready, n + 1)
                q = (SPLITS[stage] + i) % 2
                nc.vector.tensor_tensor(w_lo[:, q, a:b], ring[:, (STARTS[stage] + i) % NS, a:b],
                                        w_hi[:, q, a:b], ALU.subtract).then_inc(split_ready, 1)
                if free:
                    dve.wait_ge(split_ready, n + 1)
                    dve.sem_inc(tile_used, 1)

            def lo_tiles(stage, tiles):
                for i in tiles:
                    for h in range(2):
                        lo(stage, i, h * TILE // 2, (h + 1) * TILE // 2, 2 * (SPLITS[stage] + i) + h, h == 1)

            def lo_first(f):
                stage = FFN_STAGE[f]
                for c in range(2):
                    lo(stage, c, 0, UP, 2 * SPLITS[stage] + up_part(c), False)

            def residual(r, gate=None):
                if r != 3:
                    dve.wait_ge(split_used, SPLITS[Y_STAGE[r] + 1])
                if r == 3:
                    dve.wait_ge(moe_done, 1)
                for k in range(KB):
                    if gate is None:
                        ins = nc.vector.tensor_tensor(xT[:, k, :], xT[:, k, :], Y[:, k, :], ALU.add)
                    else:
                        ins = nc.vector.scalar_tensor_tensor(xT[:, k, :], Y[:, k, :],
                                                             hg[:, gate, k:k + 1], xT[:, k, :],
                                                             ALU.mult, ALU.add)
                    ins.then_inc(x_ready, 1)

            def softmax_unit(u, tt, mask, mult):
                nk = P * (tt + 1)
                s_ps = ps[:, 0:2, :].rearrange("p b (h t) -> p (b h) t", h=2)[:, :, 0:nk]
                dve.wait_ge(s_ready, u + 1)
                if u:
                    dve.wait_ge(pt_ready, u)
                ins = nc.vector.tensor_tensor(sm[:, :, 0:nk], s_ps,
                                              mask.unsqueeze(1).broadcast_to([P, 4, nk]), ALU.add)
                ins.then_inc(s_used, 1)
                dve.wait_ge(s_used, u + 1)
                nc.vector.tensor_reduce(small[:, 0:4], sm[:, :, 0:nk], AX, ALU.max)\
                    .then_inc(max_ready, 1)
                dve.wait_ge(exp_ready, u + 1)
                if mult is not None:
                    after(dve, "dve", nc.vector.tensor_tensor(
                        sm[:, :, 0:nk], sm[:, :, 0:nk], mult.unsqueeze(1).broadcast_to([P, 4, nk]),
                        ALU.mult))
                after(dve, "dve", nc.vector.tensor_reduce(small[:, 4:8], sm[:, :, 0:nk], AX, ALU.add))
                nc.vector.reciprocal(small[:, 8:12], small[:, 4:8]).then_inc(rden_ready, 1)

            def cat_norm(m):
                n = 2 if m < 2 else KB
                dve.wait_ge(css_ready, m + 1)
                src = SS.rearrange("p (b t) -> p b t", b=2) if m < 2 else Y
                mean_eps(sq[:, 0:n, :], src, 1.0 / (512 if m < 2 else HD), cvar_ready)
                dve.wait_ge(cstd_ready, m + 1)
                after(dve, "dve", nc.vector.reciprocal(sq[:, 0:n, :], sq[:, 0:n, :]))
                for k in range(KB):
                    g = V("cat_g", m * KB + k) if m < 2 else V("out_g", (m - 2) * KB + k)
                    nc.vector.scalar_tensor_tensor(cat[:, k, :], cat[:, k, :], g,
                                                   sq[:, k // 4 if m < 2 else k, :],
                                                   ALU.mult, ALU.mult).then_inc(cat_ready, 1)
                split_input(f"c{m}", cat)
                lo_tiles(IN_STAGE[m] + 1, range(2, OUTP))

            def in_splits(m):
                lo_tiles(IN_STAGE[m], range(2, STREAM[IN_STAGE[m]]))
                lo_tiles(IN_STAGE[m] + 1, range(2))

            def mixer1(m):
                in_splits(m)
                for u in range(4):
                    tt = u % 2
                    softmax_unit(4 * m + u, tt, C(f"cmask{tt}"), C(f"mult{tt}"))
                cat_norm(m)

            def mixer2(m):
                l = m - 2
                in_splits(m)
                dve.wait_ge(qss_ready, l + 1)
                mean_eps(sq[:, :, :], Y, 1.0 / HD, qvar_ready)
                dve.wait_ge(qstd_ready, l + 1)
                after(dve, "dve", nc.vector.reciprocal(sq[:, :, :], sq[:, :, :]))
                for b in range(8):
                    nc.vector.scalar_tensor_tensor(proj[:, b, :], proj[:, b, :],
                                                   qkg[:, 4 * l + b // 2:4 * l + b // 2 + 1],
                                                   sq[:, b, :], ALU.mult, ALU.mult)\
                        .then_inc(qk_ready, 1)
                for b in range(13):
                    n = 13 * l + b
                    dve.wait_ge(rot_ready, n + 1)
                    if n >= 2:
                        dve.wait_ge(rope_ready, n - 1)
                    after(dve, "dve", nc.vector.tensor_tensor(relu_l[:, n % 2, :], ps[:, n % 2, 0:T],
                                                              C("sin"), ALU.mult))
                    dve.wait_ge(cos_ready, n + 1)
                    nc.vector.tensor_tensor(proj[:, b, :], proj[:, b, :], relu_l[:, n % 2, :], ALU.add)\
                        .then_inc(rope_ready, 1)
                dve.wait_ge(in_copied, UNITS_BEFORE[m + 1])
                for tt in range(TT):
                    nk = P * (tt + 1)
                    for j in range(8):
                        n = 16 * l + 8 * tt + j
                        dve.wait_ge(ir_ready, n + 1)
                        w = vtok[:, tt, 1024 + j:1025 + j]
                        if j == 0:
                            ins = nc.vector.scalar_tensor_tensor(score[:, 0:nk], relu_l[:, n % 2, 0:nk],
                                                                 w, C(f"cmask{tt}"), ALU.mult, ALU.add)
                        else:
                            ins = nc.vector.scalar_tensor_tensor(score[:, 0:nk], relu_l[:, n % 2, 0:nk],
                                                                 w, score[:, 0:nk], ALU.mult, ALU.add)
                        ins.then_inc(ir_used, 1)
                        dve.wait_ge(ir_used, n + 1)
                    for i in range(TOPK // 8):
                        after(dve, "dve", nc.vector.max(top8[:, :], score[:, 0:nk]))
                        after(dve, "dve", nc.vector.match_replace(score[:, 0:nk], top8[:, :],
                                                                  score[:, 0:nk], TAKEN))
                    after(dve, "dve", nc.vector.tensor_scalar(score[:, 0:nk], score[:, 0:nk], 2 * NEG * 1e7,
                                                              -NEG, ALU.is_le, ALU.mult))
                    nc.vector.scalar_tensor_tensor(selmask[:, tt, 0:nk], score[:, 0:nk], NEG,
                                                   C(f"cmask{tt}"), ALU.add, ALU.add)\
                        .then_inc(sel_ready, 1)
                    dve.wait_ge(sel_ready, 2 * l + tt + 1)
                for u in range(4):
                    tt = u % 2
                    mask = C(f"cmask{tt}") if u < 2 else selmask[:, tt, 0:P * (tt + 1)]
                    softmax_unit(4 * m + u, tt, mask, None)
                for h in range(9):
                    n = 8 * l + h
                    if h < 8:
                        dve.wait_ge(l_ready, n + 1)
                        if n >= 2:
                            dve.wait_ge(spm_ready, n - 1)
                            dve.wait_ge(a_exp, n - 1)
                        z = ps[:, n % 2, 0:T + P]
                        after(dve, "dve", nc.vector.scalar_tensor_tensor(
                            st_d[:, n % 2, 0, :], z, 0.0, st_l[:, n % 2, 1, :], ALU.max, ALU.add))
                        nc.vector.tensor_tensor(st_d[:, n % 2, 1, :], st_d[:, n % 2, 0, :], z,
                                                ALU.subtract).then_inc(sp_ready, 1)
                    if h > 0:
                        g = n - 1
                        dve.wait_ge(af_ready, g + 1)
                        dve.wait_ge(sp_ready, g + 1)
                        nc.vector.tensor_tensor(st_d[:, g % 2, 1, :], st_d[:, g % 2, 1, :],
                                                ps[:, 2 + g % 2, 0:T + P], ALU.add)\
                            .then_inc(arg_ready, 1)
                cat_norm(m)

            def ffn(f, n):
                base, stage = chunks_before(f), FFN_STAGE[f]
                q0, i0 = SPLITS[stage], STARTS[stage]

                def chunk(c, r=0, last=False):
                    b = c % 2
                    if c and not last:
                        n_part = 2 * q0 + up_part(c + 1)
                        dve.wait_ge(hi_ready, r * 2 + (n_part + 1))
                        nc.vector.tensor_tensor(w_lo[:, (q0 + c + 1) % 2, 0:UP],
                                                ring[:, (i0 + c + 1) % NS, 0:UP],
                                                w_hi[:, (q0 + c + 1) % 2, 0:UP], ALU.subtract)\
                            .then_inc(split_ready, 1)
                    n_part = 2 * q0 + down_part(c, n)
                    dve.wait_ge(hi_ready, r * 2 + (n_part + 1))
                    nc.vector.tensor_tensor(w_lo[:, (q0 + c) % 2, UP:TILE], ring[:, (i0 + c) % NS, UP:TILE],
                                            w_hi[:, (q0 + c) % 2, UP:TILE], ALU.subtract)\
                        .then_inc(split_ready, 1)
                    dve.wait_ge(split_ready, r * 2 + (n_part + 1))
                    dve.sem_inc(tile_used, 1)
                    dve.wait_ge(sg_ready, r + (base + c + 1))
                    dve.wait_ge(split_used, r + (q0 + c - 1))
                    nc.vector.tensor_tensor(hid[:, b, :], sg[:, b, :], ps[:, 4 + b, T:2 * T], ALU.mult)\
                        .then_inc(hid_raw, 1)
                    dve.wait_ge(hid_raw, r + (base + c + 1))
                    nc.vector.tensor_copy(hid_hi[:, b, :], hid[:, b, :]).then_inc(hid_top, 1)
                    dve.wait_ge(hid_top, r + (q0_ffn[f] + c + 1))
                    nc.vector.tensor_tensor(hid_lo[:, b, :], hid[:, b, :], hid_hi[:, b, :], ALU.subtract)\
                        .then_inc(hid_ready, 1)

                lead, rounds = ffn_loop(n)
                for c in range(lead):
                    chunk(c)
                with nc.vector.Fori(0, rounds) as r:
                    for j in range(NS):
                        chunk(lead + j, r * NS)
                chunk(n - 1, last=True)

            def moe():
                base = chunks_before(1)

                def chunk(b, c, width, gate):
                    dve.wait_ge(sg_ready, c + 1)
                    dve.wait_ge(tile_used, c + (STARTS[5] - base - 1))
                    ins = nc.vector.tensor_tensor(hid[:, b, 0:width], sg[:, b, 0:width],
                                                  ps[:, 4 + b, width:2 * width], ALU.mult)
                    if gate is not None:
                        ins.then_inc(hid_raw, 1)
                        dve.wait_ge(hid_raw, c + 1)
                        ins = nc.vector.tensor_tensor(hid[:, b, :], hid[:, b, :], gate, ALU.mult)
                    ins.then_inc(hid_ready, 1)

                def ada_part(e, r2, s, j):
                    i = e * ADA_X + r2 * 2 + s
                    if j == 0:
                        dve.wait_ge(ada_in[s], e * (8 * ADA_X) + r2 * 16 + 16)
                        dve.wait_ge(mod_ready, i + 1)
                    for k in (2 * j, 2 * j + 1):
                        src, c = ada[:, s, k * COLS:(k + 1) * COLS], silu_c[:, k:k + 1]
                        if k == 0:
                            ins = nc.vector.tensor_scalar(acc[:, s, :], src, c, None, ALU.mult)
                        else:
                            dve.wait_ge(acc_step, e * (8 * ADA_X) + r2 * 16 + (8 * s + k))
                            ins = nc.vector.scalar_tensor_tensor(acc[:, s, :], src, c, acc[:, s, :],
                                                                 ALU.mult, ALU.add)
                        ins.then_inc(acc_step, 1)
                    if j == NS - 1:
                        dve.wait_ge(acc_step, e * (8 * ADA_X) + r2 * 16 + (8 * s + 8))
                        dve.sem_inc(ada_used, 1)
                        dve.sem_inc(acc_ready, 1)

                def chunks(e, width, gate):
                    with nc.vector.Fori(0, ADA_X // 2) as r2:
                        for s in range(2):
                            for j in range(NS):
                                chunk(j % 2, e * FX + r2 * (2 * NS) + (base + s * NS + j), width, gate)
                                ada_part(e, r2, s, j)
                    for j in range(FX - ADA_X * NS):
                        chunk(j % 2, e * FX + (base + ADA_X * NS + j), width, gate)

                with nc.vector.Fori(0, NE) as e:
                    is_wide = nc.vector.value_load(wide[0:1, bass.ds(e, 1)], min_val=0, max_val=1)
                    with nc.vector.If(is_wide == 1):
                        chunks(e, T, gates[:, bass.ds(e, 1), :].rearrange("p a t -> p (a t)"))
                        dve.sem_inc(yt_copied, 1)
                    with nc.vector.Else():
                        chunks(e, CAP, None)
                        dve.sem_inc(hid_raw, FX)
                        dve.wait_ge(yt_ready, e + 1)
                        nc.vector.tensor_copy(yt.rearrange("p (h n) -> p h n", h=2), ps[0:CAP, 4:6, :])\
                            .then_inc(yt_copied, 1)

            def router():
                dve.wait_ge(logit_ready, 1)
                lg, t0, t1, oh1, oh2 = (rt[:, i, :, :] for i in range(5))
                m1, m2 = rt[:, 5, :, 0:1], rt[:, 6, :, 0:1]
                d, e2, g1, g2 = (rt[:, i, :, 0:1] for i in (7, 8, 9, 10))
                idx = rt[:, 11, :, 0:1]
                iota = C("iota").unsqueeze(1).broadcast_to([P, TT, NE])

                def bc(a):
                    return a.broadcast_to([P, TT, NE])

                def tt_(o, a, b, op):
                    after(dve, "dve", nc.vector.tensor_tensor(o, a, b, op))

                def first_max(mx, onehot):
                    after(dve, "dve", nc.vector.tensor_reduce(mx, lg, AX, ALU.max))
                    tt_(t0, lg, bc(mx), ALU.is_lt)
                    after(dve, "dve", nc.vector.tensor_scalar(t0, t0, 1000.0, None, ALU.mult))
                    tt_(t0, t0, iota, ALU.add)
                    after(dve, "dve", nc.vector.tensor_reduce(idx, t0, AX, ALU.min))
                    tt_(onehot, iota, bc(idx), ALU.is_equal)

                after(dve, "dve", nc.vector.tensor_copy(
                    lg, ps[:, 6, 0:TT * NE].rearrange("p (t e) -> p t e", t=TT)))
                first_max(m1, oh1)
                after(dve, "dve", nc.vector.tensor_scalar(t1, oh1, TAKEN, None, ALU.mult))
                tt_(lg, lg, t1, ALU.add)
                first_max(m2, oh2)
                nc.vector.tensor_tensor(d, m2, m1, ALU.subtract).then_inc(route_exp_in, 1)
                dve.wait_ge(route_exp, 1)
                after(dve, "dve", nc.vector.tensor_scalar(t0[:, :, 0:1], e2, 1.0, None, ALU.add))
                after(dve, "dve", nc.vector.reciprocal(g1, t0[:, :, 0:1]))
                tt_(g2, e2, g1, ALU.mult)
                nc.vector.tensor_tensor(lg, oh1, oh2, ALU.add).then_inc(mask_ready, 1)
                tt_(oh1, oh1, bc(g1), ALU.mult)
                tt_(oh2, oh2, bc(g2), ALU.mult)
                tt_(oh1, oh1, oh2, ALU.add)
                dve.wait_ge(mask_ready, 1)
                dve.wait_ge(pos_ready, 1)
                nc.vector.tensor_scalar(wide[:, :], ps[:, 7, TT * NE:(TT + 1) * NE], CAP + 0.5, None,
                                        ALU.is_gt).then_inc(wide_ready, 1)
                after(dve, "dve", nc.vector.tensor_copy(
                    t0, ps[:, 7, 0:TT * NE].rearrange("p (t e) -> p t e", t=TT)))
                for e in range(NE):
                    for tt in range(TT):
                        nc.vector.tensor_scalar(place[:, e, tt, :], C("slots"), rt[:, 1, tt, e:e + 1],
                                                rt[:, 0, tt, e:e + 1], ALU.is_equal, ALU.mult)\
                            .then_inc(place_ready, 1)
                        nc.vector.tensor_scalar(gplace[:, e, tt, :], C("slots"), rt[:, 1, tt, e:e + 1],
                                                rt[:, 3, tt, e:e + 1], ALU.is_equal, ALU.mult)\
                            .then_inc(place_ready, 1)
                for i in range(TT * NE):
                    e, tt = divmod(i, TT)
                    if i >= 2:
                        dve.wait_ge(gate_ready, i - 1)
                    nc.vector.tensor_scalar(diag[:, i % 2, :], C("ident"), rt[:, 3, tt, e:e + 1], None,
                                            ALU.mult).then_inc(diag_ready, 1)
                for b in range(4):
                    dve.wait_ge(gate_ready, 4 * b + 4)
                    after(dve, "dve", nc.vector.tensor_copy(
                        gates[:, 2 * b:2 * b + 2, :],
                        ps[:, b, :].rearrange("p (e t) -> p e t", e=2)))
                dve.sem_inc(gate_copied, 1)

            def modulation():
                dve.wait_ge(mod_ready, 2 * ADA + 2)
                after(dve, "dve", nc.vector.tensor_tensor(
                    mod[:, :, :], ps[:, 6:8, MOD_AT:MOD_AT + MODB],
                    V("b_ada", 0, 2 * MODB).rearrange("p (l b) -> p l b", l=2), ALU.add))
                for n in range(6):
                    l, j = divmod(n, 3)
                    scale = mod[:, l, (3 * j + 1) * KB:(3 * j + 2) * KB]
                    after(dve, "dve", nc.vector.scalar_tensor_tensor(
                        gs[:, n, :], scale, 1.0, V("norm_g", n * KB, KB), ALU.add, ALU.mult))
                    after(dve, "dve", nc.vector.tensor_scalar(
                        hg[:, n, :], mod[:, l, (3 * j + 2) * KB:(3 * j + 3) * KB],
                        1.0 if j == 1 else 0.5, None, ALU.mult))
                for i in range(8):
                    after(dve, "dve", nc.vector.tensor_scalar(
                        qkg[:, i:i + 1], V("qk_g", i), HD ** -0.5 if i % 2 == 0 else 1.0, None, ALU.mult))
                dve.sem_inc(mod_done, 1)

            dve.wait_ge(silu_c_ready, 1)
            def tiles_first(stage):
                return lambda: lo_tiles(stage, range(2))

            norm(0, tiles_first(0))
            mixer1(0)
            residual(0)
            norm(1, lambda: lo_first(0))
            ffn(0, FF)
            residual(1)
            norm(2, tiles_first(IN_STAGE[1]))
            mixer1(1)
            residual(2)
            norm(3)
            router()
            moe()
            modulation()
            residual(3)
            norm(4, lambda: lo_first(2))
            for l in range(2):
                norm(5 + 3 * l, (lambda: lo_first(4)) if l else None)
                ffn(2 + 2 * l, FF)
                residual(4 + 3 * l, 3 * l)
                norm(6 + 3 * l, tiles_first(IN_STAGE[2 + l]))
                mixer2(2 + l)
                residual(5 + 3 * l, 3 * l + 1)
                norm(7 + 3 * l, lambda: lo_first(3 + 2 * l))
                ffn(3 + 2 * l, FF)
                residual(6 + 3 * l, 3 * l + 2)

        @block.tensor
        def _(pe):
            mm = nc.tensor.matmul
            pe.wait_ge(loaded, 16 * 5)
            pe.wait_ge(const_set, 5)

            def mm3(o, stationary, moving, start, stop):
                mm(o, stationary[0], moving[0], start=start, stop=False, skip_group_check=True)
                mm(o, stationary[0], moving[1], start=False, stop=False, skip_group_check=True)
                return mm(o, stationary[1], moving[0], start=False, stop=stop, skip_group_check=True)

            def parts(stage, i, a, b):
                q = (SPLITS[stage] + i) % 2
                return w_hi[:, q, a:b], w_lo[:, q, a:b]

            def wait_half(stage, i, k):
                if k % (KB // 2) == 0:
                    pe.wait_ge(split_ready, 2 * (SPLITS[stage] + i) + k // (KB // 2) + 1)

            def wait_input(name, k):
                pe.wait_ge(as_ready, KB * SPLIT_INPUTS.index(name) + k + 1)

            def norm(n):
                for k in range(KB):
                    if k % 2 == 0:
                        pe.wait_ge(sq_ready, 4 * n + k // 2 + 1)
                    ins = mm(SS[:, 0:T], ones[:, :], sq[:, k, :], start=k == 0, stop=k == KB - 1)
                ins.then_inc(ss_ready, 1)

            def wait_h(n, k):
                pe.wait_ge(h_ready, KB * h_norms.index(n) + k + 1)

            def inproj(m, n):
                u = UNITS_BEFORE[m]
                stage = IN_STAGE[m]
                feats = IN1_F if m < 2 else IN2_F
                for i in range(feats):
                    for b in range(FB):
                        if u >= 4:
                            pe.wait_ge(in_copied, u - 3)
                        for k in range(KB):
                            if b == 0:
                                wait_half(stage, i, k)
                                if i == 0:
                                    wait_input(f"n{n}", k)
                            at = k * COLS + b * P
                            ins = mm3(ps[:, u % 4, 0:T], parts(stage, i, at, at + P),
                                      (a_hi[:, k, :], a_lo[:, k, :]), k == 0, k == KB - 1)
                        last = unit_tile(m, u - UNITS_BEFORE[m])[1]
                        ins.then_inc(split_used if last else in_ready, 1)
                        u += 1
                for i, cols in enumerate(IN1_V if m < 2 else IN2_V, feats):
                    for tt in range(TT):
                        pe.wait_ge(in_copied, u - 3)
                        for k in range(KB):
                            if tt == 0:
                                wait_half(stage, i, k)
                            tokens = slice(tt * P, (tt + 1) * P)
                            ins = mm3(ps[:, u % 4, 0:cols], (a_hi[:, k, tokens], a_lo[:, k, tokens]),
                                      parts(stage, i, k * COLS, k * COLS + cols), k == 0, k == KB - 1)
                        last = unit_tile(m, u - UNITS_BEFORE[m])[1]
                        ins.then_inc(split_used if last else in_ready, 1)
                        u += 1

            def outproj(m):
                stage = IN_STAGE[m] + 1
                for i in range(OUTP):
                    for b in range(min(FB, KB - i * FB)):
                        for k in range(KB):
                            if b == 0:
                                wait_half(stage, i, k)
                                if i == 0:
                                    wait_input(f"c{m}", k)
                            at = k * COLS + b * P
                            ins = mm3(Y[:, i * FB + b, :], parts(stage, i, at, at + P),
                                      (a_hi[:, k, :], a_lo[:, k, :]), k == 0, k == KB - 1)
                    ins.then_inc(split_used, 1)

            def scores(u, tt, qb, kb):
                nk = P * (tt + 1)
                if u:
                    pe.wait_ge(s_used, u)
                for h in range(4):
                    r = (h % 2) * HD
                    ins = mm(ps[:, h % 2, (h // 2) * T:(h // 2) * T + nk],
                             proj[r:r + HD, qb + h // 2, tt * P:(tt + 1) * P],
                             proj[r:r + HD, kb + h // 2, 0:nk], start=True, stop=True)
                ins.then_inc(s_ready, 1)

            def values(u, tt, v0):
                pe.wait_ge(p_ready, u + 1)
                for i in range(4):
                    for kt in range(tt + 1):
                        at = (i % 2) * T + kt * P
                        ins = nc.tensor.transpose(ps[:, 2 + i // 2, at:at + P],
                                                  sm[:, i, kt * P:(kt + 1) * P], C("ident"))
                ins.then_inc(pt_ready, 1)
                pe.wait_ge(pt_copied, u + 1)
                if u >= 2:
                    pe.wait_ge(o_copied, u - 1)
                for h in range(4):
                    r = (h % 2) * HD
                    for kt in range(tt + 1):
                        ins = mm(ps[r:r + HD, 4 + u % 2, (h // 2) * P:(h // 2 + 1) * P],
                                 vtok[:, kt, v0 + h * HD:v0 + (h + 1) * HD], pT[:, 2 * (h % 2) + h // 2, kt, :],
                                 start=kt == 0, stop=kt == tt)
                ins.then_inc(o_ready, 1)

            def mixer1(m, n):
                inproj(m, n)
                pe.wait_ge(in_copied, UNITS_BEFORE[m + 1])
                scores(4 * m, 0, 4, 8)
                pe.wait_ge(d_ready, m + 1)
                for g in range(4):
                    ins = mm(ps[:, 6 + g // 2, (g % 2) * T:(g % 2 + 1) * T], wp[:, 4 * m + g, :],
                             sq[:, g, :], start=True, stop=True)
                    if g % 2:
                        ins.then_inc(z_ready, 1)
                for u in range(4):
                    if u < 3:
                        scores(4 * m + u + 1, (u + 1) % 2, 4 + 2 * ((u + 1) // 2), 8 + 2 * ((u + 1) // 2))
                    values(4 * m + u, u % 2, 256 * (u // 2))
                pe.wait_ge(csq_ready, m + 1)
                for k in range(KB):
                    ins = mm(SS[:, (k // 4) * T:(k // 4 + 1) * T], ones[:, :], sq[:, k, :],
                             start=k % 4 == 0, stop=k % 4 == 3)
                ins.then_inc(css_ready, 1)
                outproj(m)

            def mixer2(m, n):
                l = m - 2
                inproj(m, n)
                pe.wait_ge(qsq_ready, l + 1)
                pe.wait_ge(in_copied, UNITS_BEFORE[m + 1])
                for b in range(8):
                    ins = mm(Y[:, b, :], C("headones"), sq[:, b, :], start=True, stop=True)
                ins.then_inc(qss_ready, 1)
                for b in range(13):
                    i = 13 * l + b
                    pe.wait_ge(qk_ready, 8 * l + min(b + 1, 8))
                    if i >= 2:
                        pe.wait_ge(rope_ready, i - 1)
                    if b < 2:
                        pe.wait_ge(qvar_ready, l + 1)
                    mm(ps[:, i % 2, 0:T], C("rot"), proj[:, b, :], start=True, stop=True)\
                        .then_inc(rot_ready, 1)
                pe.wait_ge(rope_ready, 13 * (l + 1))
                for i in range(16):
                    nn = 16 * l + i
                    tt, j = divmod(i, 8)
                    r = (j % 2) * HD
                    if nn >= 2:
                        pe.wait_ge(ir_ready, nn - 1)
                    mm(ps[:, 6 + nn % 2, 0:P * (tt + 1)], proj[r:r + HD, 8 + j // 2, tt * P:(tt + 1) * P],
                       proj[r:r + HD, 12, 0:P * (tt + 1)], start=True, stop=True).then_inc(il_ready, 1)
                scores(4 * m, 0, 0, 2)
                for u in range(4):
                    if u < 3:
                        q0 = 4 * ((u + 1) // 2)
                        scores(4 * m + u + 1, (u + 1) % 2, q0, q0 + 2)
                    values(4 * m + u, u % 2, 256 * (u // 2))

                def logits(h):
                    nn = 8 * l + h
                    r, b = (h % 2) * HD, h // 2
                    if h >= 2:
                        pe.wait_ge(sp_ready, nn - 1)
                    elif h == 0:
                        pe.wait_ge(s_used, 4 * (m + 1))
                    z = ps[:, nn % 2, :]
                    mm(z[:, 0:T], proj[r:r + HD, 17 + b, 0:P], proj[r:r + HD, 13 + b, :],
                       start=True, stop=True)
                    mm(z[:, T:T + P], proj[r:r + HD, 17 + b, P:T], proj[r:r + HD, 13 + b, P:T],
                       start=True, stop=True).then_inc(zt_ready, 1)

                def weigh(h):
                    nn = 8 * l + h
                    r, b = (h % 2) * HD, h // 2
                    pe.wait_ge(a_ready, nn + 1)
                    if h % 2 == 0:
                        if b >= 2:
                            pe.wait_ge(co_copied, 4 * l + b - 1)
                        else:
                            pe.wait_ge(o_copied, 4 * (m + 1))
                    o = ps[r:r + HD, 4 + b % 2, :]
                    v0 = 512 + h * HD
                    mm(o[:, 0:T], vtok[:, 0, v0:v0 + HD], st_d[:, nn % 2, 3, 0:T], start=True, stop=False)
                    mm(o[:, P:T], vtok[:, 1, v0:v0 + HD], st_d[:, nn % 2, 3, T:T + P], start=False,
                       stop=True).then_inc(co_ready, 1)

                logits(0)
                for h in range(9):
                    nn = 8 * l + h
                    if h < 7:
                        logits(h + 1)
                    if h < 8:
                        pe.wait_ge(spm_ready, nn + 1)
                        if h >= 2:
                            pe.wait_ge(arg_ready, nn - 1)
                        elif h == 0:
                            pe.wait_ge(pt_copied, 4 * (m + 1))
                        a = ps[:, 2 + nn % 2, :]
                        spm = st_d[:, nn % 2, 2, :]
                        mm(a[:, 0:T], C("after"), spm[:, 0:T], start=True, stop=False)
                        mm(a[:, P:T], ones[:, :], spm[:, T:T + P], start=False, stop=True)
                        mm(a[:, T:T + P], C("after"), spm[:, T:T + P], start=True, stop=True)\
                            .then_inc(af_ready, 1)
                    if h > 0:
                        weigh(h - 1)
                pe.wait_ge(csq_ready, m + 1)
                for k in range(KB):
                    ins = mm(Y[:, k, :], C("headones"), sq[:, k, :], start=True, stop=True)
                ins.then_inc(css_ready, 1)
                pe.wait_ge(cvar_ready, m + 1)
                outproj(m)

            def ffn(f, n, norm_n):
                base, stage = chunks_before(f), FFN_STAGE[f]
                q0 = SPLITS[stage]

                def up(c, r=0):
                    pe.wait_ge(split_ready, r * 2 + (2 * q0 + up_part(c) + 1))
                    if base + c >= 2:
                        pe.wait_ge(hid_ready, r + (base + c - 1))
                    for g in range(2):
                        for k in range(KB):
                            if c == 0 and g == 0:
                                wait_input(f"n{norm_n}", k)
                            at = (g * KB + k) * P
                            ins = mm3(ps[:, 4 + c % 2, g * T:(g + 1) * T], parts(stage, c, at, at + P),
                                      (a_hi[:, k, :], a_lo[:, k, :]), k == 0, k == KB - 1)
                    ins.then_inc(gu_ready, 1)

                def down(c, r=0):
                    pe.wait_ge(hid_ready, r + (base + c + 1))
                    pe.wait_ge(split_ready, r * 2 + (2 * q0 + down_part(c, n) + 1))
                    for d in range(KB):
                        at = UP + d * P
                        ins = mm3(Y[:, d, :], parts(stage, c, at, at + P),
                                  (hid_hi[:, c % 2, :], hid_lo[:, c % 2, :]),
                                  c == 0 and d % 2 == 0, c == n - 1)
                    ins.then_inc(split_used, 1)

                lead, rounds = ffn_loop(n)
                up(0)
                for c in range(1, lead):
                    up(c)
                    down(c - 1)
                with nc.tensor.Fori(0, rounds) as r:
                    for j in range(NS):
                        up(lead + j, r * NS)
                        down(lead + j - 1, r * NS)
                up(n - 1)
                down(n - 2)
                down(n - 1)

            def router():
                for tt in range(TT):
                    for k in range(KB):
                        if tt == 0:
                            wait_h(3, k)
                        ins = mm(ps[:, 6, tt * NE:(tt + 1) * NE], hT[:, k, tt * P:(tt + 1) * P],
                                 wr[:, k, :], start=k == 0, stop=k == KB - 1)
                ins.then_inc(logit_ready, 1)
                for i in range(4):
                    if i >= 2:
                        pe.wait_ge(ht_copied, i - 1)
                    for j in range(4):
                        ins = nc.tensor.transpose(ps[:, 4 + i % 2, j * P:(j + 1) * P],
                                                  hT[:, 4 * (i % 2) + j, (i // 2) * P:(i // 2 + 1) * P],
                                                  C("ident"))
                    ins.then_inc(ht_ready, 1)
                pe.wait_ge(mask_ready, 1)
                m0, m1 = rt[:, 0, 0, :], rt[:, 0, 1, :]
                before = C("strict")[:, 0:P]
                mm(ps[:, 7, 0:NE], before, m0, start=True, stop=True)
                mm(ps[:, 7, NE:2 * NE], before, m1, start=True, stop=False)
                mm(ps[:, 7, NE:2 * NE], ones[:, :], m0, start=False, stop=True)
                mm(ps[:, 7, 2 * NE:3 * NE], ones[:, :], m0, start=True, stop=False)
                mm(ps[:, 7, 2 * NE:3 * NE], ones[:, :], m1, start=False, stop=True).then_inc(pos_ready, 1)
                for i in range(4):
                    pe.wait_ge(ht_copied, min(4, 3 + i))
                    if i >= 2:
                        pe.wait_ge(gp_copied, i - 1)
                    for j in range(4):
                        e, tt = 2 * i + j // 2, j % 2
                        pe.wait_ge(place_ready, 4 * e + 2 * tt + 2)
                        ins = nc.tensor.transpose(ps[0:CAP, 4 + i % 2, j * P:(j + 1) * P],
                                                  gplace[:, e, tt, :], C("ident"))
                    ins.then_inc(gp_ready, 1)
                for i in range(TT * NE):
                    e, tt = divmod(i, TT)
                    pe.wait_ge(diag_ready, i + 1)
                    at = (e % 2) * T + tt * P
                    mm(ps[:, e // 2, at:at + P], ones[:, :], diag[:, i % 2, :], start=True, stop=True)\
                        .then_inc(gate_ready, 1)
                pe.wait_ge(gate_copied, 1)
                pe.wait_ge(gp_copied, 4)

            def moe():
                base = chunks_before(1)
                t0 = STARTS[5]
                assert FX % NS == 0

                def up(s, c, n_in, act_in, width):
                    pe.wait_ge(tile_in[s], n_in)
                    w = ring[:, s, 0:2 * KB * P].rearrange("p (g k f) -> p g k f", g=2, k=KB)
                    b = (s - t0) % 2
                    pe.wait_ge(hid_ready, c - 1)
                    for g in range(2):
                        for k in range(KB):
                            ins = mm(ps[:, 4 + b, g * width:(g + 1) * width], w[:, g, k, :], act_in[:, k, :],
                                     start=k == 0, stop=k == KB - 1)
                    ins.then_inc(gu_ready, 1)

                def down(s, c, wide_path, first=False):
                    pe.wait_ge(hid_ready, c + 1)
                    w = ring[:, s, 2 * KB * P:].rearrange("p (d f) -> p d f", d=KB)
                    b = (s - t0) % 2
                    for d in range(KB):
                        if wide_path:
                            ins = mm(Y[:, d, :], w[:, d, :], hid[:, b, :], start=False, stop=False,
                                     skip_group_check=True)
                        else:
                            ins = mm(ps[:, 6 + d // 4, (d % 4) * CAP:(d % 4 + 1) * CAP], w[:, d, :],
                                     hid[:, b, 0:CAP], start=first and d % 4 == 0, stop=False,
                                     skip_group_check=True)
                    ins.then_inc(tile_used, 1)

                def ada_sums(e, half, e4, r2, b):
                    pe.wait_ge(acc_ready, e * ADA_X + r2 * 2 + (b + 1))
                    for f in range(FB):
                        column = e4 * (ADA_X * FB) + r2 * (2 * FB) + (MOD_AT + b * FB + f)
                        ins = mm(ps[:, bass.ds(half + 6, 1), bass.ds(column, 1)]
                                 .rearrange("p a c -> p (a c)"),
                                 acc[:, b, f * P:(f + 1) * P], ones[:, 0:1], start=False, stop=False,
                                 skip_group_check=True)
                    ins.then_inc(mod_ready, 1)

                def expert(e, half, e4, wide_path):
                    act_in, width = (hT, T) if wide_path else (he, CAP)

                    def at(c):
                        i = t0 + c
                        return i % NS, e * FX + (base + c), e * (16 * FX // NS) + 16 * (i // NS + 1)

                    lead = NS
                    for c in range(lead):
                        s, n, n_in = at(c)
                        up(s, n, n_in, act_in, width)
                        if c:
                            s, n, _ = at(c - 1)
                            down(s, n, wide_path, first=c == 1)
                    with nc.tensor.Fori(0, ADA_X // 2) as r:
                        for j in range(2 * NS):
                            s, n, n_in = at(lead + j)
                            up(s, r * (2 * NS) + n, r * 32 + n_in, act_in, width)
                            s, n, _ = at(lead + j - 1)
                            down(s, r * (2 * NS) + n, wide_path)
                            if j % NS == NS - 1:
                                ada_sums(e, half, e4, r, j // NS)
                    s, n, _ = at(FX - 1)
                    down(s, n, wide_path)

                for d in range(KB):
                    mm(Y[:, d, :], ones[0:1, :], zeros[0:1, :], start=d % 2 == 0, stop=False,
                       skip_group_check=True)
                for b in (6, 7):
                    mm(ps[:, b, 0:2], ones[0:1, :], zeros[0:1, 0:2], start=True, stop=True)
                pe.sem_inc(mod_ready, 2)
                pe.wait_ge(wide_ready, 1)
                with nc.tensor.Fori(0, 2) as half, nc.tensor.Fori(0, NE // 2) as e4:
                    e = half * (NE // 2) + e4
                    is_wide = nc.tensor.value_load(wide[0:1, bass.ds(e, 1)], min_val=0, max_val=1)
                    with nc.tensor.If(is_wide == 1):
                        expert(e, half, e4, True)
                        nc.tensor.sem_inc(he_gathered, 1)
                        nc.tensor.sem_inc(yt_ready, 1)
                    with nc.tensor.Else():
                        for k in range(KB):
                            for tt in range(TT):
                                ins = mm(ps[:, 6 + k // 4, (k % 4) * CAP:(k % 4 + 1) * CAP],
                                         htok[:, tt, k * P:(k + 1) * P],
                                         place[:, bass.ds(e, 1), tt, :].rearrange("p a c -> p (a c)"),
                                         start=tt == 0, stop=tt == TT - 1)
                        ins.then_inc(he_gathered, 1)
                        pe.wait_ge(he_ready, e + 1)
                        expert(e, half, e4, False)
                        pe.wait_ge(ye_ready, e + 1)
                        for d in range(KB):
                            ins = nc.tensor.transpose(ps[0:CAP, 4 + d // 4, (d % 4) * P:(d % 4 + 1) * P],
                                                      ye[:, d, :], C("ident"))
                        ins.then_inc(yt_ready, 1)
                        pe.wait_ge(yt_copied, e + 1)
                        for d in range(KB):
                            mm(Y[:, d, :], yt[:, d * P:(d + 1) * P],
                               scatter[:, bass.ds(e, 1), :].rearrange("p a t -> p (a t)"),
                               start=False, stop=False, skip_group_check=True)
                mm(Y[:, 0, :], ones[0:1, :], zeros[0:1, 0:T], start=False, stop=True,
                   skip_group_check=True).then_inc(moe_done, 1)

            norm(0)
            mixer1(0, 0)
            norm(1)
            ffn(0, FF, 1)
            norm(2)
            mixer1(1, 2)
            norm(3)
            router()
            moe()
            norm(4)
            for l in range(2):
                norm(5 + 3 * l)
                ffn(2 + 2 * l, FF, 5 + 3 * l)
                norm(6 + 3 * l)
                mixer2(2 + l, 6 + 3 * l)
                norm(7 + 3 * l)
                ffn(3 + 2 * l, FF, 7 + 3 * l)


def _proj_tiles(w):
    f = w.shape[1]
    n = -(-f // COLS)
    w = np.pad(w, ((0, 0), (0, n * COLS - f)))
    return w.reshape(KB, P, n, COLS).transpose(2, 1, 0, 3).reshape(n, P, TILE)


def _ffn_tiles(wg, wu, wd):
    n = wg.shape[1] // P
    g = wg.reshape(KB, P, n, P).transpose(2, 1, 0, 3).reshape(n, P, D)
    u = wu.reshape(KB, P, n, P).transpose(2, 1, 0, 3).reshape(n, P, D)
    return np.concatenate([g, u, wd.reshape(n, P, D)], axis=2)


def _col(v):
    return np.asarray(v).reshape(-1, P).T


def _constants():
    c = np.zeros((P, N_CONST), np.float32)

    def put(name, a):
        at, w = CONST[name]
        c[:, at:at + w] = a.reshape(P, w)

    i = np.arange(P)
    t = np.arange(T)
    put("ident", np.eye(P))
    put("headones", (i[:, None] // HD == i[None, :] // HD).astype(np.float32))
    rot = np.zeros((P, P))
    for h in range(0, P, HD):
        for a in range(8):
            rot[h + a + 8, h + a] = -1.0
            rot[h + a, h + a + 8] = 1.0
    put("rot", rot)
    put("after", (i[:, None] > i[None, :]).astype(np.float32))
    for tt in range(TT):
        q = tt * P + i[:, None]
        k = np.arange(P * (tt + 1))[None, :]
        d = q - k
        put(f"cmask{tt}", np.where(d >= 0, 0.0, NEG))
        put(f"mult{tt}", sum(((d >= 0) & (d <= w) & (d % s == 0)).astype(np.float32)
                             for w, s in ((128, 1), (512, 4), (2048, 16))))
    put("strict", np.concatenate([(i[:, None] < t[None, :]), (P + i[:, None] < t[None, P:])], axis=1)
        .astype(np.float32))
    inv = np.float32(500000.0) ** (-np.arange(0, 16, 2, dtype=np.float32) / np.float32(16))
    ang = t.astype(np.float32)[:, None] * inv.astype(np.float32)[None, :]
    cos, sin = np.ones((P, T), np.float32), np.zeros((P, T), np.float32)
    for h in range(0, P, HD):
        for a in range(16):
            cos[h + a], sin[h + a] = np.cos(ang[:, a % 8]), np.sin(ang[:, a % 8])
    put("cos", cos)
    put("sin", sin)
    put("invcnt", np.broadcast_to(np.concatenate([1.0 / np.minimum(t[:16] + 1, w) for w in (2, 4, 8, 16)]),
                                  (P, 4 * 16)))
    put("iota", np.broadcast_to(np.arange(NE), (P, NE)))
    put("slots", np.broadcast_to(np.arange(CAP), (P, CAP)))
    return c


def kernel(**inputs):
    import concourse.bacc as bacc
    from concourse.bass_utils import run_bass_kernel_spmd

    a = {k: np.asarray(v) for k, v in inputs.items()}

    stream = np.empty((N_TILES, P, TILE), np.float32)
    at = 0

    def add(tiles):
        nonlocal at
        stream[at:at + len(tiles)] = tiles
        at += len(tiles)

    for l in range(2):
        add(_proj_tiles(a["w_in"][l]))
        add(_proj_tiles(a["w_out"][l]))
        if l == 0:
            add(_ffn_tiles(a["ffn_wg"][0], a["ffn_wu"][0], a["ffn_wd"][0]))
        else:
            for e in range(NE):
                add(_ffn_tiles(a["moe_wg"][0, e], a["moe_wu"][0, e], a["moe_wd"][0, e]))
    for l in range(2):
        w = a["w_in_2"][l]
        qa, ka, va, qb, kb, vb, qi, ki, wi, qc, kc, vc = np.split(
            w, np.cumsum([256, 256, 256, 256, 256, 256, 512, 64, 8, 512, 512]), axis=1)
        w = np.concatenate([qa, ka, qb, kb, qi, ki, ki, qc, kc, va, vb, vc, wi], axis=1)
        f = (a["ffn_w1_2"][l], a["ffn_w3_2"][l], a["ffn_w2_2"][l])
        add(_ffn_tiles(*(x[0] for x in f)))
        add(_proj_tiles(w))
        add(_proj_tiles(a["w_out_2"][l]))
        add(_ffn_tiles(*(x[1] for x in f)))
    assert at == N_TILES
    astream = np.concatenate([_proj_tiles(a["w_ada_2"][l]) for l in range(2)])

    cat_g = np.concatenate([np.concatenate([a["pool_scale"][l], a["attn_gain"][l]]) for l in range(2)])
    qk = np.concatenate([np.tile(a["qk_g_2"], (1, 1, 2)).reshape(-1)])
    vectors = np.concatenate([_col(v) for v in (
        a["norm_mix"], a["norm_ffn"], a["final_norm"], cat_g, a["norm_g_2"], a["out_g_2"], qk,
        a["b_ada_2"], a["c_2"])], axis=1)
    host = {
        "x_in": a["x"][0].T.reshape(KB, P, T).transpose(1, 0, 2),
        "wstream": stream,
        "astream": astream,
        "wpool": a["w_pool"].reshape(8, P, P).transpose(1, 0, 2),
        "wrouter": a["w_router"][0].reshape(KB, P, NE).transpose(1, 0, 2),
        "vectors": vectors,
        "consts": _constants(),
    }
    host = {k: np.ascontiguousarray(v) for k, v in host.items()}
    nc = bacc.Bacc("TRN2", target_bir_lowering=False, num_devices=1)
    args = {k: nc.dram_tensor(k, v.shape, mybir.dt.float32, kind="ExternalInput").ap()
            for k, v in host.items()}
    out = nc.dram_tensor("out", (P, KB, T), mybir.dt.float32, kind="ExternalOutput").ap()
    build(nc, out=out, **args)
    r = run_bass_kernel_spmd(nc, [host], core_ids=[0])
    y = r.results[0]["out"]
    return y.transpose(1, 0, 2).reshape(1, D, T).transpose(0, 2, 1)
```

```python
from contextlib import ExitStack

import concourse.bass as bass
import numpy as np
from concourse import mybir

P = 128
T = 256
D = 1024
KB = D // P
TT = T // P
D_FF = 2816
D_FFX = 3584
NE = 8
NS = 4
TILE = 3072
FB = TILE // KB // P
COLS = FB * P
HD = 64
N_MOD = 9
EPS = 1e-6
NEG = -1e30
TAKEN = -3e38
TOPK = min(256, T // 4)
MODB = N_MOD * KB
CAP = 96

PAIRS = [(b, min(2, 13 - b)) for b in range(0, 13, 2)]
IN1_F, IN1_V = 4, (384, 128)
IN2_F, IN2_V = 7, (384, 384, 264)
IN1 = IN1_F + len(IN1_V)
IN2 = IN2_F + len(IN2_V)
OUTP = -(-KB // FB)
FF = D_FF // P
FX = D_FFX // P
ADA = MODB // FB
ADA_F = 16
ADA_X = (2 * ADA - ADA_F) // NE
SPAN = (FX - NS) // ADA_X
STREAM = [IN1, OUTP, FF, IN1, OUTP, NE * FX] + [FF, IN2, OUTP, FF] * 2
STARTS = [sum(STREAM[:i]) for i in range(len(STREAM) + 1)]
N_TILES = STARTS[-1]
IN_STAGE = (0, 3, 7, 11)
FFN_STAGE = (2, 5, 6, 9, 10, 13)
MOE_STAGE = 5
SPLITS = [STARTS[i] - (STREAM[MOE_STAGE] if i > MOE_STAGE else 0) for i in range(len(STREAM) + 1)]
SPLIT_INPUTS = ["n0", "c0", "n1", "n2", "c1", "n5", "n6", "c2", "n7", "n8", "n9", "c3", "n10"]
Y_STAGE = (1, 2, 4, 5, 6, 8, 9, 10, 12, 13)

CONST = {}
_at = 0
for _n, _w in (("ident", P), ("headsel", KB * 16), ("spread", KB * P), ("rot", P), ("after", P),
               ("cmask0", P), ("cmask1", T),
               ("mult0", P), ("mult1", T), ("strict", T + P), ("cos", T), ("sin", T),
               ("invcnt", 4 * 16), ("iota", NE), ("slots", CAP)):
    CONST[_n] = (_at, _w)
    _at += _w
N_CONST = _at
VEC = {}
_at = 0
for _n, _w in (("norm_mix", 2 * KB), ("norm_ffn", 2 * KB), ("final", KB), ("cat_g", 2 * KB),
               ("norm_g", 6 * KB), ("out_g", 2 * KB), ("qk_g", 8), ("b_ada", 2 * MODB), ("c", KB)):
    VEC[_n] = (_at, _w)
    _at += _w
N_VEC = _at


def build(nc, x_in, wstream, astream, wpool, wrouter, vectors, consts, out):
    fp32 = mybir.dt.float32
    fp32r = mybir.dt.float32r
    ALU = mybir.AluOpType
    ACT = mybir.ActivationFunctionType
    AX = mybir.AxisListType.X
    ctx = ExitStack()
    with ctx:
        def sb(name, shape, dtype=fp32):
            return ctx.enter_context(nc.sbuf_tensor(name, shape, dtype))

        def sem(name):
            return ctx.enter_context(nc.semaphore(name))

        first_byte = -(-nc.sbuf_base // 32) * 32
        w_parts = sb("w_parts", [P, 2, 2, TILE], fp32r)
        moe_room = nc.alloc_sbuf_tensor_at("moe_room", [P, 4 * TILE], fp32, offset=first_byte)
        w_hi, w_lo = w_parts[:, 0], w_parts[:, 1]
        ring = sb("ring", [P, NS, TILE])
        xT = sb("xT", [P, KB, T])
        hT = sb("hT", [P, KB, T])
        cat = hT
        a_hi = sb("a_hi", [P, KB, T], fp32r)
        a_lo = sb("a_lo", [P, KB, T], fp32r)
        sq = sb("sq", [P, KB, T])
        proj = sb("proj", [P, 21, T])
        branch = sb("branch", [P, 3 * 4 * (16 + T)])
        upad, *win = (branch[:, i * 4 * (16 + T):(i + 1) * 4 * (16 + T)]
                      .rearrange("p (g t) -> p g t", g=4) for i in range(3))
        vtok = sb("vtok", [P, TT, 1032])
        sm = sb("sm", [P, 4, T])
        st_l = sq[:, 0:3, :].rearrange("p k t -> p (k t)").rearrange("p (b t) -> p b t", b=2)
        sm2 = (sm, sq[:, 4:8, :])
        pT = sb("pT", [P, 4, TT, P])
        small = sb("small", [P, 64])
        rope_t = branch[:, 0:4 * T].rearrange("p (i b t) -> p i b t", i=2, b=2)
        cat_sq = branch[:, 0:KB * T].rearrange("p (k t) -> p k t", k=KB)
        relu_l = branch[:, 0:2 * T].rearrange("p (b t) -> p b t", b=2)
        select = (sb("select0", [P, P]), sq[:, 3, :])
        top8 = sb("top8", [P, 8])
        st_d = branch[:, 0:2 * 4 * (T + P)].rearrange("p (b i t) -> p b i t", b=2, i=4)
        norm_s = pT[:, 0:2, :, :].rearrange("p a k t -> p a (k t)")
        sg, hid = sm[:, 0:2, :], sm[:, 2:4, :]
        hid_hi = sb("hid_hi", [P, 2, T], fp32r)
        hid_lo = sb("hid_lo", [P, 2, T], fp32r)
        gates = proj[:, 0:NE, :]
        ada = moe_room[:, 0:2 * TILE].rearrange("p (s n) -> p s n", s=2)
        place, gplace = (moe_room[:, 2 * TILE + i * NE * TT * CAP:2 * TILE + (i + 1) * NE * TT * CAP]
                         .rearrange("p (e t c) -> p e t c", e=NE, t=TT) for i in range(2))
        at = 2 * TILE + 2 * NE * TT * CAP
        scatter = moe_room[0:CAP, at:at + NE * T].rearrange("p (e t) -> p e t", e=NE)
        at += NE * T
        acc = moe_room[:, at:at + 2 * COLS].rearrange("p (b f) -> p b f", b=2)
        ada_f = proj[:, 0:TILE // T, :].rearrange("p k t -> p (k t)").rearrange("p (h n) -> p h n", h=2)
        acc_f = sq[:, 0:5, :].rearrange("p k t -> p (k t)")[:, 0:3 * COLS].rearrange("p (b f) -> p b f", b=3)
        place_next = moe_room[:, 2 * TILE:2 * TILE + (NE + 1) * TT * CAP].rearrange(
            "p (e t c) -> p e t c", e=NE + 1, t=TT)
        htok = vtok[:, :, 0:D]
        he = branch[:, 0:KB * CAP].rearrange("p (k c) -> p k c", k=KB)
        ye = branch[0:CAP, KB * CAP:KB * CAP + D]
        wd_hi, wd_lo = (a.rearrange("p (b d) t -> p b (d t)", b=2) for a in (a_hi, a_lo))
        rt = sb("rt", [P, 12, TT, NE])
        diag = proj[:, NE, :].rearrange("p (b t) -> p b t", b=2)
        wide = ctx.enter_context(nc.sbuf_tensor("wide", [P, NE], mybir.dt.int32))
        mod = sb("mod", [P, 2, MODB])
        mod_all = mod[:, :, :].rearrange("p l b -> p (l b)")
        gs = sb("gs", [P, 6, KB])
        qkg = sb("qkg", [P, 8])
        hg = sb("hg", [P, 6, KB])
        silu_c = sb("silu_c", [P, KB])
        ones = sb("ones", [P, P])
        cst = sb("cst", [P, N_CONST])
        vec = sb("vec", [P, N_VEC])
        wp = proj[:, 16:20, :].rearrange("p (g h) (i f) -> p (g h i) f", g=4, i=2)
        wr = sb("wr", [P, KB, NE])

        def C(name):
            a, w = CONST[name]
            return cst[:, a:a + w]

        def V(name, i=0, n=None):
            a, w = VEC[name]
            return vec[:, a + i:a + i + (n or 1)]

        ps = ctx.enter_context(nc.psum_tensor("ps", [P, 8, 512], fp32))
        Y = ps[:, 0:4, :].rearrange("p b (h t) -> p (b h) t", h=2)
        SS = ps[:, 6, :]

        MOD_AT = 4 * CAP

        tile_in = [sem(f"tile_in{s}") for s in range(NS)]
        tile_used = sem("tile_used")
        hi_ready = sem("hi_ready")
        split_ready = sem("split_ready")
        split_used = sem("split_used")
        ah_ready = sem("ah_ready")
        as_ready = sem("as_ready")
        ada_in = [sem(f"ada_in{s}") for s in range(2)]
        ada_used = sem("ada_used")
        half_in = [sem(f"half_in{s}") for s in range(2)]
        half_used = sem("half_used")
        loaded = sem("loaded")
        stored = sem("stored")
        const_set = sem("const_set")
        x_ready = sem("x_ready")
        sq_ready = sem("sq_ready")
        sqsum_ready = sem("sqsum_ready")
        csqsum_ready = sem("csqsum_ready")
        ss_ready = sem("ss_ready")
        var_ready = sem("var_ready")
        std_ready = sem("std_ready")
        normed = sem("normed")
        h_ready = sem("h_ready")
        gu_ready = sem("gu_ready")
        sg_ready = sem("sg_ready")
        hid_ready = sem("hid_ready")
        in_ready = sem("in_ready")
        in_copied = sem("in_copied")
        d_ready = sem("d_ready")
        z_ready = sem("z_ready")
        z_copied = sem("z_copied")
        s_ready = sem("s_ready")
        s_used = sem("s_used")
        max_ready = sem("max_ready")
        sub_ready = sem("sub_ready")
        exp_ready = sem("exp_ready")
        rden_ready = sem("rden_ready")
        p_ready = sem("p_ready")
        pt_ready = sem("pt_ready")
        pt_copied = sem("pt_copied")
        o_ready = sem("o_ready")
        o_copied = sem("o_copied")
        csq_ready = sem("csq_ready")
        css_ready = sem("css_ready")
        cvar_ready = sem("cvar_ready")
        cstd_ready = sem("cstd_ready")
        cat_ready = sem("cat_ready")
        logit_ready = sem("logit_ready")
        route_exp_in = sem("route_exp_in")
        route_exp = sem("route_exp")
        diag_ready = sem("diag_ready")
        gate_ready = sem("gate_ready")
        mask_ready = sem("mask_ready")
        pos_ready = sem("pos_ready")
        wide_ready = sem("wide_ready")
        place_ready = sem("place_ready")
        ht_ready = sem("ht_ready")
        ht_copied = sem("ht_copied")
        gp_ready = sem("gp_ready")
        gp_copied = sem("gp_copied")
        he_gathered = sem("he_gathered")
        he_ready = sem("he_ready")
        ye_ready = sem("ye_ready")
        down_hi_ready = sem("down_hi_ready")
        down_lo_ready = sem("down_lo_ready")
        hid_top_x = sem("hid_top_x")
        y_ready = sem("y_ready")
        y_added = sem("y_added")
        gate_copied = sem("gate_copied")
        silu_c_ready = sem("silu_c_ready")
        acc_ready = sem("acc_ready")
        mod_ready = sem("mod_ready")
        acc_step = sem("acc_step")
        hid_raw = sem("hid_raw")
        hid_top = sem("hid_top")
        mod_done = sem("mod_done")
        qsq_ready = sem("qsq_ready")
        qss_ready = sem("qss_ready")
        qvar_ready = sem("qvar_ready")
        qstd_ready = sem("qstd_ready")
        qk_ready = sem("qk_ready")
        rot_ready = sem("rot_ready")
        root_ready = sem("root_ready")
        spread_ready = sem("spread_ready")
        cos_ready = sem("cos_ready")
        rope_ready = sem("rope_ready")
        il_ready = sem("il_ready")
        ir_ready = sem("ir_ready")
        ir_used = sem("ir_used")
        zt_ready = sem("zt_ready")
        l_ready = sem("l_ready")
        sp_ready = sem("sp_ready")
        spm_ready = sem("spm_ready")
        af_ready = sem("af_ready")
        arg_ready = sem("arg_ready")
        a_exp = sem("a_exp")
        a_ready = sem("a_ready")
        co_ready = sem("co_ready")
        co_copied = sem("co_copied")
        chain = {e: sem(f"chain_{e}") for e in ("dve", "act", "pool")}
        counts = {"dve": 0, "act": 0, "pool": 0}

        def after(engine, name, instruction):
            counts[name] += 1
            instruction.then_inc(chain[name], 1)
            engine.wait_ge(chain[name], counts[name])


        q0_ffn = [0, None, FF, 2 * FF, 3 * FF, 4 * FF]

        def chunks_before(f):
            return [0, FF, FF + NE * FX, 2 * FF + NE * FX, 3 * FF + NE * FX, 4 * FF + NE * FX][f]

        UP = 2 * KB * P

        def ffn_loop(n):
            lead = 2 + (n - 3) % NS
            return lead, (n - 1 - lead) // NS

        def in_units(m):
            f, v = (IN1_F * FB, len(IN1_V) * TT) if m < 2 else (IN2_F * FB, len(IN2_V) * TT)
            return f, v

        UNITS_BEFORE = [0]
        for m in range(4):
            UNITS_BEFORE.append(UNITS_BEFORE[-1] + sum(in_units(m)))

        def up_part(c):
            return 2 * c - 1 if c else 0

        def down_part(c, n):
            return 2 * n - 1 if c == n - 1 else 2 * c + 2

        def unit_tile(m, u):
            feats, _ = in_units(m)
            if u < feats:
                return SPLITS[IN_STAGE[m]] + u // FB, u % FB == FB - 1
            v = u - feats
            return SPLITS[IN_STAGE[m]] + feats // FB + v // TT, v % TT == TT - 1

        not_last = {}
        n_ready = 0
        for m in range(4):
            for u in range(sum(in_units(m))):
                n_ready += not unit_tile(m, u)[1]
                not_last[m, u] = n_ready

        def wait_unit(engine, m, u):
            i, last = unit_tile(m, u)
            if last:
                engine.wait_ge(split_used, i + 1)
            else:
                engine.wait_ge(in_ready, not_last[m, u])

        block = ctx.enter_context(nc.Block())

        @block.sync
        def _(sp):
            for dst, src in ((vec[:, :], vectors), (xT[:, :, :], x_in), (cst[:, :], consts),
                             (wp[:, :, :], wpool), (wr[:, :, :], wrouter)):
                sp.dma_start(dst, src).then_inc(loaded, 16)

            def load(s, i):
                sp.dma_start(ring[:, s, :], wstream[i]).then_inc(tile_in[s], 16)

            for s in range(NS):
                load(s, s)
            rounds = N_TILES // NS
            with nc.sync.Fori(1, rounds) as r:
                for s in range(NS):
                    sp.wait_ge(tile_used, r * NS + (s - NS + 1))
                    sp.dma_start(ring[:, s, :], wstream[bass.ds(r * NS + s, 1), :, :]
                                 .rearrange("a p n -> p (a n)")).then_inc(tile_in[s], 16)
            for i in range(rounds * NS, N_TILES):
                sp.wait_ge(tile_used, i - NS + 1)
                load(i % NS, i)
            sp.wait_ge(x_ready, KB * 11)
            sp.dma_start(out, xT[:, :, :]).then_inc(stored, 16)
            sp.wait_ge(stored, 16)

        @block.gpsimd
        def _(pool):
            nc.gpsimd.memset(ones[:, :], 1.0).then_inc(const_set, 1)
            nc.gpsimd.memset(win[0][:, :, 0:16], 0.0).then_inc(const_set, 1)
            nc.gpsimd.memset(win[1][:, :, 0:16], 0.0).then_inc(const_set, 1)
            nc.gpsimd.memset(upad[:, :, 0:16], 0.0).then_inc(const_set, 1)
            pool.wait_ge(const_set, 4)
            pool.wait_ge(loaded, 16 * 5)

            def ada_first():
                pool.wait_ge(as_ready, KB * (SPLIT_INPUTS.index("c0") + 1))
                for h in range(2):
                    pool.dma_start(ada_f[:, h, :], astream[0, :, h * TILE // 2:(h + 1) * TILE // 2])\
                        .then_inc(half_in[h], 16)
                with nc.gpsimd.Fori(1, ADA_F) as i:
                    for h in range(2):
                        pool.wait_ge(half_used, i * 2 + (h - 1))
                        pool.dma_start(ada_f[:, h, :],
                                       astream[bass.ds(i, 1), :, h * TILE // 2:(h + 1) * TILE // 2]
                                       .rearrange("a p n -> p (a n)")).then_inc(half_in[h], 16)

            def ada_stream():
                pool.wait_ge(place_ready, 2 * NE * TT)
                for s in range(2):
                    pool.dma_start(ada[:, s, :], astream[ADA_F + s]).then_inc(ada_in[s], 16)
                with nc.gpsimd.Fori(1, ADA_X * NE // 2) as r:
                    for s in range(2):
                        pool.wait_ge(ada_used, r * 2 + (s - 1))
                        pool.dma_start(ada[:, s, :], astream[bass.ds(r * 2 + (ADA_F + s), 1), :, :]
                                       .rearrange("a p n -> p (a n)")).then_inc(ada_in[s], 16)

            def windows(m):
                pool.wait_ge(in_copied, UNITS_BEFORE[m] + 4)
                src = upad
                for i, step in enumerate((1, 2, 4, 8)):
                    dst = win[i % 2]
                    after(pool, "pool", nc.gpsimd.tensor_tensor(
                        dst[:, i:4, 16:16 + T], src[:, i:4, 16:16 + T],
                        src[:, i:4, 16 - step:16 - step + T], ALU.add))
                    after(pool, "pool", nc.gpsimd.tensor_scalar(
                        sq[:, i, 16:T], dst[:, i, 32:16 + T], 0.5 / step, None, ALU.mult))
                    after(pool, "pool", nc.gpsimd.tensor_tensor(
                        sq[:, i, 0:16], dst[:, i, 16:32], C("invcnt")[:, i * 16:(i + 1) * 16], ALU.mult))
                    src = dst
                nc.gpsimd.tensor_tensor(sq[:, 0:4, :], sq[:, 0:4, :], upad[:, :, 16:16 + T],
                                        ALU.subtract).then_inc(d_ready, 1)

            def softmax_units(m):
                for i in range(5):
                    if i < 4:
                        u, nk = 4 * m + i, P * (i % 2 + 1)
                        pool.wait_ge(max_ready, u + 1)
                        at = 16 * (u % 2)
                        nc.gpsimd.tensor_tensor(sm2[u % 2][:, :, 0:nk], sm2[u % 2][:, :, 0:nk],
                                                small[:, at:at + 4].unsqueeze(2).broadcast_to([P, 4, nk]),
                                                ALU.subtract).then_inc(sub_ready, 1)
                    if i > 0:
                        u, nk = 4 * m + i - 1, P * ((i - 1) % 2 + 1)
                        pool.wait_ge(rden_ready, u + 1)
                        at = 16 * (u % 2) + 8
                        nc.gpsimd.tensor_tensor(sm2[u % 2][:, :, 0:nk], sm2[u % 2][:, :, 0:nk],
                                                small[:, at:at + 4].unsqueeze(2).broadcast_to([P, 4, nk]),
                                                ALU.mult).then_inc(p_ready, 1)

            def ropes(m):
                n = len(PAIRS) * (m - 2)
                for i, (b, w) in enumerate(PAIRS):
                    pool.wait_ge(rot_ready, n + i + 1)
                    nc.gpsimd.tensor_tensor(proj[:, b:b + w, :], proj[:, b:b + w, :],
                                            C("cos").unsqueeze(1).broadcast_to([P, w, T]), ALU.mult)\
                        .then_inc(cos_ready, 1)

            def sticks(m):
                n = 8 * (m - 2)
                for h in range(9):
                    if h < 8:
                        pool.wait_ge(sp_ready, n + h + 1)
                        nc.gpsimd.tensor_tensor(st_d[:, h % 2, 2, :], st_d[:, h % 2, 0, :],
                                                C("strict"), ALU.mult).then_inc(spm_ready, 1)
                    if h > 0:
                        g = h - 1
                        pool.wait_ge(a_exp, n + g + 1)
                        nc.gpsimd.tensor_tensor(st_d[:, g % 2, 3, :], st_d[:, g % 2, 3, :],
                                                C("strict"), ALU.mult).then_inc(a_ready, 1)

            for m in range(2):
                windows(m)
                softmax_units(m)
                if m == 0:
                    ada_first()
            ada_stream()
            for m in range(2, 4):
                ropes(m)
                sticks(m)
                softmax_units(m)

        @block.scalar
        def _(act):
            act.wait_ge(loaded, 16 * 5)
            act.wait_ge(const_set, 4)

            def norm(n, meanwhile=None):
                for i in range(4):
                    if n:
                        act.wait_ge(x_ready, KB * (n - 1) + 2 * i + 2)
                    nc.scalar.activation(sq[:, 2 * i:2 * i + 2, :], xT[:, 2 * i:2 * i + 2, :],
                                         ACT.Square).then_inc(sq_ready, 1)
                if meanwhile:
                    meanwhile()
                act.wait_ge(var_ready, n + 1)
                nc.scalar.activation(norm_s[:, 0, :], norm_s[:, 0, :], ACT.Sqrt).then_inc(std_ready, 1)
                if n < 5:
                    if n < 3:
                        split_input(f"n{n}", hT, h_ready, KB * n)
                else:
                    for k in range(KB):
                        act.wait_ge(normed, KB * (n - 5) + k + 1)
                        shift = mod[:, (n - 5) // 3, 3 * ((n - 5) % 3) * KB + k:
                                    3 * ((n - 5) % 3) * KB + k + 1]
                        nc.scalar.activation(a_hi[:, k, :], sq[:, k, :], ACT.Identity, bias=shift)\
                            .then_inc(ah_ready, 1)

            def split_input(name, src, ready, before):
                for k in range(KB):
                    act.wait_ge(ready, before + k + 1)
                    nc.scalar.activation(a_hi[:, k, :], src[:, k, :], ACT.Copy).then_inc(ah_ready, 1)

            def hi(stage, i, a, b):
                act.wait_ge(tile_in[(STARTS[stage] + i) % NS], 16 * ((STARTS[stage] + i) // NS + 1))
                q = SPLITS[stage] + i
                nc.scalar.activation(w_hi[:, q % 2, a:b], ring[:, (STARTS[stage] + i) % NS, a:b], ACT.Copy)\
                    .then_inc(hi_ready, 1)

            def hi_tile(stage, i):
                if i < STREAM[stage]:
                    q = SPLITS[stage] + i
                    if q >= 2:
                        act.wait_ge(split_used, q - 1)
                    for h in range(2):
                        hi(stage, i, h * TILE // 2, (h + 1) * TILE // 2)

            def hi_outproj(stage):
                for i in range(2, OUTP):
                    hi_tile(stage, i)

            def in_copies(m):
                feats, _ = in_units(m)
                u = UNITS_BEFORE[m]
                stage = IN_STAGE[m]
                for b in range(feats):
                    wait_unit(act, m, b)
                    src = ps[:, u % 4, 0:T]
                    if m < 2 and b < 4:
                        dst, scale = upad[:, b, 16:16 + T], 1.0
                    else:
                        isq = (4 <= b < 8) if m < 2 else (13 <= b < 17)
                        dst, scale = proj[:, b, :], (HD ** -0.5 if isq else 1.0)
                    nc.scalar.activation(dst, src, ACT.Copy, scale=scale).then_inc(in_copied, 1)
                    u += 1
                    if b % FB == FB - 1:
                        hi_tile(stage, b // FB + 2)
                    if m >= 2 and b == 8:
                        act.wait_ge(in_copied, UNITS_BEFORE[m] + 8)
                        nc.scalar.activation(sq[:, :, :], proj[:, 0:8, :], ACT.Square).then_inc(qsq_ready, 1)
                    if m >= 2 and b == 17:
                        act.wait_ge(qvar_ready, m - 1)
                        nc.scalar.activation(norm_s[0:16, 0, :], norm_s[0:16, 0, :], ACT.Sqrt)\
                            .then_inc(qstd_ready, 1)
                at = 0
                for w in (IN1_V if m < 2 else IN2_V):
                    for tt in range(TT):
                        wait_unit(act, m, u - UNITS_BEFORE[m])
                        nc.scalar.activation(vtok[:, tt, at:at + w], ps[:, u % 4, 0:w], ACT.Copy)\
                            .then_inc(in_copied, 1)
                        u += 1
                    at += w
                    hi_tile(stage, unit_tile(m, u - 1 - UNITS_BEFORE[m])[0] - SPLITS[stage] + 2)
                for i in range(2):
                    hi_tile(stage + 1, i)

            def softmax_units(m, block0):
                for i in range(5):
                    if i < 4:
                        u, nk = 4 * m + i, P * (i % 2 + 1)
                        act.wait_ge(sub_ready, u + 1)
                        nc.scalar.activation(sm2[u % 2][:, :, 0:nk], sm2[u % 2][:, :, 0:nk], ACT.Exp)\
                            .then_inc(exp_ready, 1)
                    if i > 0:
                        u, tt = 4 * m + i - 1, (i - 1) % 2
                        act.wait_ge(pt_ready, u + 1)
                        if u:
                            act.wait_ge(o_ready, u)
                        nc.scalar.activation(
                            pT[:, :, 0:tt + 1, :],
                            ps[:, 2:4, :].rearrange("p b (h k t) -> p (b h) k t", h=2, k=TT)[:, :, 0:tt + 1, :],
                            ACT.Copy).then_inc(pt_copied, 1)
                        act.wait_ge(o_ready, u + 1)
                        b = block0 + 2 * ((i - 1) // 2)
                        nc.scalar.activation(
                            cat[:, b:b + 2, tt * P:(tt + 1) * P],
                            ps[:, 4 + u % 2, 0:T].rearrange("p (b t) -> p b t", b=2), ACT.Copy)\
                            .then_inc(o_copied, 1)
                        if m >= 2 and tt == 1:
                            act.wait_ge(o_copied, u + 1)
                            nc.scalar.activation(cat_sq[:, b:b + 2, :], cat[:, b:b + 2, :], ACT.Square)\
                                .then_inc(csq_ready, 1)

            def cat_norm(m):
                if m < 2:
                    act.wait_ge(o_copied, 4 * (m + 1))
                    act.wait_ge(z_copied, 2 * (m + 1))
                    nc.scalar.activation(sq[:, :, :], cat[:, :, :], ACT.Square).then_inc(csq_ready, 1)
                act.wait_ge(cvar_ready, m + 1)
                if m < 2:
                    nc.scalar.activation(sq[:, 0:2, :], sq[:, 0:2, :], ACT.Sqrt).then_inc(cstd_ready, 1)
                else:
                    nc.scalar.activation(norm_s[0:16, 0, :], norm_s[0:16, 0, :], ACT.Sqrt)\
                        .then_inc(cstd_ready, 1)
                split_input(f"c{m}", cat, cat_ready, KB * m)
                hi_outproj(IN_STAGE[m] + 1)

            def mixer1(m):
                in_copies(m)
                for i in range(2):
                    act.wait_ge(z_ready, 2 * m + i + 1)
                    nc.scalar.activation(cat[:, 2 * i:2 * i + 2, :],
                                         ps[:, 6 + i, :].rearrange("p (b t) -> p b t", b=2),
                                         ACT.Copy).then_inc(z_copied, 1)
                softmax_units(m, 4)
                cat_norm(m)

            def mixer2(m):
                in_copies(m)
                for i in range(16):
                    n = 16 * (m - 2) + i
                    nk = P * (i // 8 + 1)
                    act.wait_ge(il_ready, n + 1)
                    if n >= 2:
                        act.wait_ge(ir_used, n - 1)
                    nc.scalar.activation(relu_l[:, n % 2, 0:nk], ps[:, 6 + n % 2, 0:nk], ACT.Relu)\
                        .then_inc(ir_ready, 1)
                for h in range(9):
                    n = 8 * (m - 2) + h
                    if h < 8:
                        act.wait_ge(zt_ready, n + 1)
                        if n >= 2:
                            act.wait_ge(sp_ready, n - 1)
                        z = ps[:, n % 2, 0:T + P]
                        term = st_l[:, n % 2, :]
                        after(act, "act", nc.scalar.activation(term, z, ACT.Abs))
                        after(act, "act", nc.scalar.activation(term, term, ACT.Exp, scale=-1.0))
                        nc.scalar.activation(term, term, ACT.Ln, bias=1.0).then_inc(l_ready, 1)
                    if h > 0:
                        g = n - 1
                        act.wait_ge(arg_ready, g + 1)
                        if g >= 2:
                            act.wait_ge(co_ready, g - 1)
                        nc.scalar.activation(st_d[:, g % 2, 3, :], st_d[:, g % 2, 1, :], ACT.Exp,
                                             scale=-1.0).then_inc(a_exp, 1)
                        if g % 2 and h >= 3:
                            copy_sticks(m, (h - 1) // 2 - 1)
                copy_sticks(m, 3)
                act.wait_ge(co_copied, 4 * (m - 1))
                nc.scalar.activation(cat_sq[:, 4:8, :], cat[:, 4:8, :], ACT.Square).then_inc(csq_ready, 1)
                softmax_units(m, 0)
                cat_norm(m)

            def copy_sticks(m, pair):
                act.wait_ge(co_ready, 8 * (m - 2) + 2 * pair + 2)
                nc.scalar.activation(cat[:, 4 + pair, :], ps[:, 4 + pair % 2, 0:T], ACT.Copy)\
                    .then_inc(co_copied, 1)

            def hi_first(f):
                stage = FFN_STAGE[f]
                for c in range(2):
                    act.wait_ge(split_used, SPLITS[stage] + c - 1)
                    hi(stage, c, 0, UP)

            def ffn(f, n):
                base, stage = chunks_before(f), FFN_STAGE[f]
                q0, i0 = SPLITS[stage], STARTS[stage]

                def chunk(c, r=0, last=False):
                    s, nx = (i0 + c) % NS, (i0 + c + 1) % NS
                    rt_ = 16 // NS
                    if c and not last:
                        act.wait_ge(gu_ready, r + (base + c))
                        act.wait_ge(tile_in[nx], r * rt_ + 16 * ((i0 + c + 1) // NS + 1))
                        nc.scalar.activation(w_hi[:, (q0 + c + 1) % 2, 0:UP], ring[:, nx, 0:UP], ACT.Copy)\
                            .then_inc(hi_ready, 1)
                    act.wait_ge(split_used, r + (q0 + c - 1))
                    act.wait_ge(tile_in[s], r * rt_ + 16 * ((i0 + c) // NS + 1))
                    nc.scalar.activation(w_hi[:, (q0 + c) % 2, UP:TILE], ring[:, s, UP:TILE], ACT.Copy)\
                        .then_inc(hi_ready, 1)
                    act.wait_ge(gu_ready, r + (base + c + 1))
                    if base + c >= 2:
                        act.wait_ge(hid_ready, r + (base + c - 1))
                    nc.scalar.activation(sg[:, c % 2, :], ps[:, 4 + c % 2, 0:T], ACT.Silu)\
                        .then_inc(sg_ready, 1)

                lead, rounds = ffn_loop(n)
                for c in range(lead):
                    chunk(c)
                with nc.scalar.Fori(0, rounds) as r:
                    for j in range(NS):
                        chunk(lead + j, r * NS)
                chunk(n - 1, last=True)

            def moe():
                base = chunks_before(1)

                def chunk(b, c, width):
                    act.wait_ge(gu_ready, c + 1)
                    act.wait_ge(hid_ready, c - 1)
                    nc.scalar.activation(sg[:, b, 0:width], ps[:, 4 + b, 0:width], ACT.Silu)\
                        .then_inc(sg_ready, 1)

                def tokens(n):
                    act.wait_ge(he_gathered, n)
                    nc.scalar.activation(
                        he.rearrange("p (h k) c -> p h (k c)", h=2), ps[:, 6:8, 0:4 * CAP], ACT.Copy)\
                        .then_inc(he_ready, 1)

                def down_hi(j, e, r, c):
                    i = STARTS[5] + j
                    act.wait_ge(tile_in[i % NS], e * (16 * FX // NS) + r * 16 + 16 * (i // NS + 1))
                    act.wait_ge(tile_used, c + (STARTS[5] - base - 1))
                    nc.scalar.activation(wd_hi[:, j % 2, :], ring[:, i % NS, UP:TILE], ACT.Copy)\
                        .then_inc(down_hi_ready, 1)

                act.wait_ge(wide_ready, 1)
                tokens(1)
                with nc.scalar.Fori(0, NE) as e:
                    is_wide = nc.scalar.value_load(wide[0:1, bass.ds(e, 1)], min_val=0, max_val=1)
                    with nc.scalar.If(is_wide == 1):
                        with nc.scalar.Fori(0, FX // NS) as r:
                            for j in range(NS):
                                chunk(j % 2, e * FX + r * NS + (base + j), T)
                        act.sem_inc(down_hi_ready, FX)
                        act.sem_inc(ye_ready, 1)
                        tokens(e + 2)
                    with nc.scalar.Else():
                        with nc.scalar.Fori(0, FX // NS) as r:
                            for j in range(NS):
                                c = e * FX + r * NS + (base + j)
                                down_hi(j, e, r, c)
                                chunk(j % 2, c, CAP)
                        act.wait_ge(tile_used, e * FX + (STARTS[5] + FX))
                        nc.scalar.activation(ye.rearrange("p (h n) -> p h n", h=2), ps[0:CAP, 0:2, :],
                                             ACT.Copy).then_inc(ye_ready, 1)
                        tokens(e + 2)

            nc.scalar.activation(silu_c[:, :], V("c", 0, KB), ACT.Silu).then_inc(silu_c_ready, 1)
            def tiles_first(stage):
                return lambda: [hi_tile(stage, i) for i in range(2)]

            norm(0, tiles_first(0))
            mixer1(0)
            norm(1, lambda: hi_first(0))
            ffn(0, FF)
            norm(2, tiles_first(IN_STAGE[1]))
            mixer1(1)
            norm(3)
            act.wait_ge(route_exp_in, 1)
            nc.scalar.activation(rt[:, 8, :, 0:1], rt[:, 7, :, 0:1], ACT.Exp).then_inc(route_exp, 1)
            for i in range(4):
                act.wait_ge(ht_ready, i + 1)
                nc.scalar.activation(htok[:, i // 2, (i % 2) * 512:(i % 2 + 1) * 512], ps[:, 4 + i % 2, :],
                                     ACT.Copy).then_inc(ht_copied, 1)
            for i in range(4):
                act.wait_ge(gp_ready, i + 1)
                nc.scalar.activation(scatter[:, 2 * i:2 * i + 2, :],
                                     ps[0:CAP, 4 + i % 2, :].rearrange("p (e t) -> p e t", e=2),
                                     ACT.Copy).then_inc(gp_copied, 1)
            moe()
            act.wait_ge(mod_done, 1)
            norm(4, lambda: hi_first(2))
            for l in range(2):
                norm(5 + 3 * l, (lambda: hi_first(4)) if l else None)
                ffn(2 + 2 * l, FF)
                norm(6 + 3 * l, tiles_first(IN_STAGE[2 + l]))
                mixer2(2 + l)
                norm(7 + 3 * l, lambda: hi_first(3 + 2 * l))
                ffn(3 + 2 * l, FF)

        @block.vector
        def _(dve):
            dve.wait_ge(loaded, 16 * 5)
            dve.wait_ge(const_set, 4)

            def mean_eps(dst, src, inv, signal):
                nc.vector.tensor_scalar(dst, src, inv, EPS, ALU.mult, ALU.add).then_inc(signal, 1)

            def norm(n, meanwhile=None, later=None):
                for i in range(1, 4):
                    dve.wait_ge(sq_ready, 4 * n + i + 1)
                    after(dve, "dve", nc.vector.tensor_tensor(sq[:, 0:2, :], sq[:, 0:2, :],
                                                              sq[:, 2 * i:2 * i + 2, :], ALU.add))
                nc.vector.tensor_tensor(sq[:, 0, :], sq[:, 0, :], sq[:, 1, :], ALU.add)\
                    .then_inc(sqsum_ready, 1)
                if meanwhile:
                    meanwhile()
                dve.wait_ge(ss_ready, n + 1)
                mean_eps(norm_s[:, 0, :], SS[:, 0:T], 1.0 / D, var_ready)
                dve.wait_ge(std_ready, n + 1)
                after(dve, "dve", nc.vector.reciprocal(norm_s[:, 1, :], norm_s[:, 0, :]))
                for k in range(KB):
                    if n < 4:
                        g = V("norm_ffn" if n % 2 else "norm_mix", (n // 2) * KB + k)
                        nc.vector.scalar_tensor_tensor(hT[:, k, :], xT[:, k, :], g, norm_s[:, 1, :],
                                                       ALU.mult, ALU.mult).then_inc(h_ready, 1)
                    elif n == 4:
                        nc.vector.scalar_tensor_tensor(xT[:, k, :], xT[:, k, :], V("final", k),
                                                       norm_s[:, 1, :], ALU.mult, ALU.mult)\
                            .then_inc(x_ready, 1)
                    else:
                        nc.vector.scalar_tensor_tensor(sq[:, k, :], xT[:, k, :],
                                                       gs[:, n - 5, k:k + 1], norm_s[:, 1, :],
                                                       ALU.mult, ALU.mult).then_inc(normed, 1)
                if n not in (3, 4):
                    split_input(f"n{n}", hT if n < 3 else sq)
                if later:
                    later()

            def split_input(name, src):
                e = SPLIT_INPUTS.index(name)
                n = int(name[1:])
                for k in range(KB):
                    dve.wait_ge(ah_ready, KB * e + k + 1)
                    if name[0] == "n" and n >= 5:
                        dve.wait_ge(normed, KB * (n - 5) + k + 1)
                        at = 3 * ((n - 5) % 3) * KB + k
                        ins = nc.vector.scalar_tensor_tensor(
                            a_lo[:, k, :], src[:, k, :], mod[:, (n - 5) // 3, at:at + 1], a_hi[:, k, :],
                            ALU.add, ALU.subtract)
                    else:
                        dve.wait_ge(h_ready if name[0] == "n" else cat_ready, KB * n + k + 1)
                        ins = nc.vector.tensor_tensor(a_lo[:, k, :], src[:, k, :], a_hi[:, k, :],
                                                      ALU.subtract)
                    ins.then_inc(as_ready, 1)

            def lo(stage, i, a, b, n, free):
                dve.wait_ge(hi_ready, n + 1)
                q = (SPLITS[stage] + i) % 2
                nc.vector.tensor_tensor(w_lo[:, q, a:b], ring[:, (STARTS[stage] + i) % NS, a:b],
                                        w_hi[:, q, a:b], ALU.subtract).then_inc(split_ready, 1)
                if free:
                    dve.wait_ge(split_ready, n + 1)
                    dve.sem_inc(tile_used, 1)

            def lo_tiles(stage, tiles):
                for i in tiles:
                    for h in range(2):
                        lo(stage, i, h * TILE // 2, (h + 1) * TILE // 2, 2 * (SPLITS[stage] + i) + h, h == 1)

            def lo_first(f, c):
                stage = FFN_STAGE[f]
                lo(stage, c, 0, UP, 2 * SPLITS[stage] + up_part(c), False)

            def residual(r, gate=None):
                dve.wait_ge(split_used, SPLITS[Y_STAGE[r] + 1])
                for k in range(KB):
                    if gate is None:
                        ins = nc.vector.tensor_tensor(xT[:, k, :], xT[:, k, :], Y[:, k, :], ALU.add)
                    else:
                        ins = nc.vector.scalar_tensor_tensor(xT[:, k, :], Y[:, k, :],
                                                             hg[:, gate, k:k + 1], xT[:, k, :],
                                                             ALU.mult, ALU.add)
                    ins.then_inc(x_ready, 1)

            def softmax_units(m, masks, mults, meanwhile=None):
                for i in range(5):
                    if i < 4:
                        u, nk, buf = 4 * m + i, P * (i % 2 + 1), sm2[i % 2]
                        s_ps = ps[:, 0:2, :].rearrange("p b (h t) -> p (b h) t", h=2)[:, :, 0:nk]
                        dve.wait_ge(s_ready, u + 1)
                        if u >= 2:
                            dve.wait_ge(pt_ready, u - 1)
                        nc.vector.tensor_tensor(buf[:, :, 0:nk], s_ps,
                                                masks[i].unsqueeze(1).broadcast_to([P, 4, nk]), ALU.add)\
                            .then_inc(s_used, 1)
                        dve.wait_ge(s_used, u + 1)
                        at = 16 * (u % 2)
                        nc.vector.tensor_reduce(small[:, at:at + 4], buf[:, :, 0:nk], AX, ALU.max)\
                            .then_inc(max_ready, 1)
                        if meanwhile and i == 0:
                            meanwhile(0)
                    if i > 0:
                        u, nk, buf = 4 * m + i - 1, P * ((i - 1) % 2 + 1), sm2[(i - 1) % 2]
                        at = 16 * (u % 2)
                        dve.wait_ge(exp_ready, u + 1)
                        if mults:
                            after(dve, "dve", nc.vector.tensor_tensor(
                                buf[:, :, 0:nk], buf[:, :, 0:nk],
                                mults[(i - 1) % 2].unsqueeze(1).broadcast_to([P, 4, nk]), ALU.mult))
                        after(dve, "dve", nc.vector.tensor_reduce(small[:, at + 4:at + 8], buf[:, :, 0:nk],
                                                                  AX, ALU.add))
                        nc.vector.reciprocal(small[:, at + 8:at + 12], small[:, at + 4:at + 8])\
                            .then_inc(rden_ready, 1)
                        if meanwhile and i < 4:
                            meanwhile(i)

            def head_roots(sums_ready, n, var_ready_, std_ready_, meanwhile=None):
                dve.wait_ge(sums_ready, n)
                mean_eps(norm_s[0:16, 0, :], SS[0:16, 0:T], 1.0 / HD, var_ready_)
                if meanwhile:
                    meanwhile()
                dve.wait_ge(std_ready_, n)
                nc.vector.reciprocal(norm_s[0:16, 1, :], norm_s[0:16, 0, :]).then_inc(root_ready, 1)

            def cat_norm(m):
                if m < 2:
                    two = sq.rearrange("p (g k) t -> p g k t", g=2)
                    dve.wait_ge(csq_ready, m + 1)
                    after(dve, "dve", nc.vector.tensor_tensor(two[:, :, 0:2, :], two[:, :, 0:2, :],
                                                              two[:, :, 2:4, :], ALU.add))
                    nc.vector.tensor_tensor(two[:, :, 0, :], two[:, :, 0, :], two[:, :, 1, :], ALU.add)\
                        .then_inc(csqsum_ready, 1)
                    dve.wait_ge(css_ready, m + 1)
                    mean_eps(sq[:, 0:2, :], SS.rearrange("p (b t) -> p b t", b=2), 1.0 / 512, cvar_ready)
                    dve.wait_ge(cstd_ready, m + 1)
                    after(dve, "dve", nc.vector.reciprocal(sq[:, 0:2, :], sq[:, 0:2, :]))
                else:
                    head_roots(css_ready, m + 1, cvar_ready, cstd_ready)
                for k in range(KB):
                    if m < 2:
                        g, root = V("cat_g", m * KB + k), sq[:, k // 4, :]
                    else:
                        g, root = V("out_g", (m - 2) * KB + k), Y[:, k, :]
                        dve.wait_ge(spread_ready, KB // 2 * (2 * (m - 2) + 1) + k // 2 + 1)
                    nc.vector.scalar_tensor_tensor(cat[:, k, :], cat[:, k, :], g, root,
                                                   ALU.mult, ALU.mult).then_inc(cat_ready, 1)
                split_input(f"c{m}", cat)
                lo_tiles(IN_STAGE[m] + 1, range(2, OUTP))

            def lo_outproj(m, j, h):
                stage = IN_STAGE[m] + 1
                lo(stage, j, h * TILE // 2, (h + 1) * TILE // 2, 2 * (SPLITS[stage] + j) + h, h == 1)

            def mixer1(m):
                lo_tiles(IN_STAGE[m], range(2, STREAM[IN_STAGE[m]]))
                softmax_units(m, [C(f"cmask{i % 2}") for i in range(4)], (C("mult0"), C("mult1")),
                              lambda i: lo_outproj(m, i // 2, i % 2))
                cat_norm(m)

            def mixer2(m):
                l = m - 2
                tiles = STREAM[IN_STAGE[m]]
                lo_tiles(IN_STAGE[m], range(2, 7))
                head_roots(qss_ready, l + 1, qvar_ready, qstd_ready, lambda: lo_tiles(IN_STAGE[m], [7]))
                lo_tiles(IN_STAGE[m], range(8, tiles))
                for b in range(8):
                    dve.wait_ge(spread_ready, KB * l + b // 2 + 1)
                    nc.vector.scalar_tensor_tensor(proj[:, b, :], proj[:, b, :],
                                                   qkg[:, 4 * l + b // 2:4 * l + b // 2 + 1],
                                                   Y[:, b, :], ALU.mult, ALU.mult)\
                        .then_inc(qk_ready, 1)
                for i, (b, w) in enumerate(PAIRS):
                    n = len(PAIRS) * l + i
                    dve.wait_ge(rot_ready, n + 1)
                    if n >= 2:
                        dve.wait_ge(rope_ready, n - 1)
                    term = rope_t[:, n % 2, 0:w, :]
                    after(dve, "dve", nc.vector.tensor_tensor(
                        term, ps[:, 6 + n % 2, 0:w * T].rearrange("p (b t) -> p b t", t=T),
                        C("sin").unsqueeze(1).broadcast_to([P, w, T]), ALU.mult))
                    dve.wait_ge(cos_ready, n + 1)
                    nc.vector.tensor_tensor(proj[:, b:b + w, :], proj[:, b:b + w, :], term, ALU.add)\
                        .then_inc(rope_ready, 1)
                dve.wait_ge(in_copied, UNITS_BEFORE[m + 1])
                for i in range(16):
                    n, tt = 16 * l + i, i // 8
                    nk = P * (tt + 1)
                    dve.wait_ge(ir_ready, n + 1)
                    if i % 8 == 0:
                        so_far = C(f"cmask{tt}")
                    else:
                        so_far = select[tt][:, 0:nk]
                        dve.wait_ge(ir_used, n)
                    nc.vector.scalar_tensor_tensor(select[tt][:, 0:nk], relu_l[:, n % 2, 0:nk],
                                                   vtok[:, tt, 1024 + i % 8:1025 + i % 8], so_far,
                                                   ALU.mult, ALU.add).then_inc(ir_used, 1)
                    if i % 4 == 3:
                        lo_outproj(m, i // 8, i // 4 % 2)
                dve.wait_ge(ir_used, 16 * (l + 1))

                def take_eight(i):
                    sc = select[i // 8][:, 0:P * (i // 8 + 1)]
                    after(dve, "dve", nc.vector.max(top8[:, :], sc))
                    after(dve, "dve", nc.vector.match_replace(sc, top8[:, :], sc, TAKEN))

                def softplus(h):
                    n = 8 * l + h
                    dve.wait_ge(l_ready, n + 1)
                    if n >= 2:
                        dve.wait_ge(spm_ready, n - 1)
                        dve.wait_ge(a_exp, n - 1)
                    z = ps[:, n % 2, 0:T + P]
                    after(dve, "dve", nc.vector.scalar_tensor_tensor(
                        st_d[:, n % 2, 0, :], z, 0.0, st_l[:, n % 2, :], ALU.max, ALU.add))
                    nc.vector.tensor_tensor(st_d[:, n % 2, 1, :], st_d[:, n % 2, 0, :], z,
                                            ALU.subtract).then_inc(sp_ready, 1)

                def exponent(h):
                    g = 8 * l + h
                    dve.wait_ge(af_ready, g + 1)
                    dve.wait_ge(sp_ready, g + 1)
                    nc.vector.tensor_tensor(st_d[:, g % 2, 1, :], st_d[:, g % 2, 1, :],
                                            ps[:, 2 + g % 2, 0:T + P], ALU.add).then_inc(arg_ready, 1)

                for h in range(9):
                    if h < 8:
                        take_eight(2 * h)
                        softplus(h)
                        take_eight(2 * h + 1)
                    if h > 0:
                        exponent(h - 1)
                for tt in range(TT):
                    sc = select[tt][:, 0:P * (tt + 1)]
                    after(dve, "dve", nc.vector.tensor_scalar(sc, sc, 2 * NEG * 1e7, -NEG,
                                                              ALU.is_le, ALU.mult))
                    after(dve, "dve", nc.vector.scalar_tensor_tensor(sc, sc, NEG, C(f"cmask{tt}"),
                                                                     ALU.add, ALU.add))
                softmax_units(m, [C("cmask0"), C("cmask1"), select[0][:, :], select[1]], None)
                cat_norm(m)

            def ffn(f, n):
                base, stage = chunks_before(f), FFN_STAGE[f]
                q0, i0 = SPLITS[stage], STARTS[stage]

                def ada_tile(i, r=0):
                    if i >= 3:
                        dve.wait_ge(mod_ready, r + i)
                    a = acc_f[:, i % 3, :]
                    for k in range(KB):
                        h, j = divmod(k, KB // 2)
                        if j == 0:
                            dve.wait_ge(half_in[h], r * 16 + 16 * (i + 1))
                        w, ck = ada_f[:, h, j * COLS:(j + 1) * COLS], silu_c[:, k:k + 1]
                        if k == 0:
                            ins = nc.vector.tensor_scalar(a, w, ck, None, ALU.mult)
                        else:
                            dve.wait_ge(acc_step, r * KB + (KB * i + k))
                            ins = nc.vector.scalar_tensor_tensor(a, w, ck, a, ALU.mult, ALU.add)
                        ins.then_inc(acc_step, 1)
                        if j == KB // 2 - 1:
                            dve.wait_ge(acc_step, r * KB + (KB * i + k + 1))
                            dve.sem_inc(half_used, 1)
                    dve.sem_inc(acc_ready, 1)

                def chunk(c, r=0, last=False, tile=None):
                    b = c % 2
                    if c and not last:
                        n_part = 2 * q0 + up_part(c + 1)
                        dve.wait_ge(hi_ready, r * 2 + (n_part + 1))
                        nc.vector.tensor_tensor(w_lo[:, (q0 + c + 1) % 2, 0:UP],
                                                ring[:, (i0 + c + 1) % NS, 0:UP],
                                                w_hi[:, (q0 + c + 1) % 2, 0:UP], ALU.subtract)\
                            .then_inc(split_ready, 1)
                    n_part = 2 * q0 + down_part(c, n)
                    dve.wait_ge(hi_ready, r * 2 + (n_part + 1))
                    nc.vector.tensor_tensor(w_lo[:, (q0 + c) % 2, UP:TILE], ring[:, (i0 + c) % NS, UP:TILE],
                                            w_hi[:, (q0 + c) % 2, UP:TILE], ALU.subtract)\
                        .then_inc(split_ready, 1)
                    dve.wait_ge(split_ready, r * 2 + (n_part + 1))
                    dve.sem_inc(tile_used, 1)
                    if tile is not None:
                        ada_tile(*tile)
                    dve.wait_ge(sg_ready, r + (base + c + 1))
                    dve.wait_ge(split_used, r + (q0 + c - 1))
                    nc.vector.tensor_tensor(hid[:, b, :], sg[:, b, :], ps[:, 4 + b, T:2 * T], ALU.mult)\
                        .then_inc(hid_raw, 1)
                    dve.wait_ge(hid_raw, r + (base + c + 1))
                    nc.vector.tensor_copy(hid_hi[:, b, :], hid[:, b, :]).then_inc(hid_top, 1)
                    dve.wait_ge(hid_top, r + (q0_ffn[f] + c + 1))
                    nc.vector.tensor_tensor(hid_lo[:, b, :], hid[:, b, :], hid_hi[:, b, :], ALU.subtract)\
                        .then_inc(hid_ready, 1)

                lead, rounds = ffn_loop(n)
                for c in range(lead):
                    chunk(c, tile=(c - 1,) if f == 0 and 1 <= c <= 3 else None)
                with nc.vector.Fori(0, rounds) as r:
                    for j in range(NS):
                        chunk(lead + j, r * NS, tile=(3 + j, r * 3) if f == 0 and j < 3 else None)
                chunk(n - 1, last=True, tile=(ADA_F - 1,) if f == 0 else None)
                if f == 0:
                    dve.wait_ge(mod_ready, ADA_F + 2)
                    nc.vector.tensor_tensor(mod_all[:, 0:ADA_F * FB], ps[:, 7, 0:ADA_F * FB],
                                            V("b_ada", 0, ADA_F * FB), ALU.add)

            def moe():
                base = chunks_before(1)

                def chunk(b, c, width, gate):
                    dve.wait_ge(sg_ready, c + 1)
                    dve.wait_ge(tile_used, c + (STARTS[5] - base - 1))
                    nc.vector.tensor_tensor(hid[:, b, 0:width], sg[:, b, 0:width],
                                            ps[:, 4 + b, width:2 * width], ALU.mult).then_inc(hid_raw, 1)
                    dve.wait_ge(hid_raw, c + 1)
                    if gate is not None:
                        ins = nc.vector.tensor_tensor(hid[:, b, :], hid[:, b, :], gate, ALU.mult)
                    else:
                        nc.vector.tensor_copy(hid_hi[:, b, 0:width], hid[:, b, 0:width])\
                            .then_inc(hid_top_x, 1)
                        dve.wait_ge(hid_top_x, c + (1 - base))
                        ins = nc.vector.tensor_tensor(hid_lo[:, b, 0:width], hid[:, b, 0:width],
                                                      hid_hi[:, b, 0:width], ALU.subtract)
                    ins.then_inc(hid_ready, 1)

                def down_lo(b, s, c):
                    dve.wait_ge(down_hi_ready, c + (1 - base))
                    nc.vector.tensor_tensor(wd_lo[:, b, :], ring[:, s, UP:TILE], wd_hi[:, b, :],
                                            ALU.subtract).then_inc(down_lo_ready, 1)

                def ada_part(e, r2, s, j):
                    i = e * ADA_X + r2 * 2 + (ADA_F + s)
                    step = e * (KB * ADA_X) + r2 * (2 * KB) + KB * (ADA_F + s)
                    if j == 0:
                        dve.wait_ge(ada_in[s], e * (ADA_X // 2 * 16) + r2 * 16 + 16)
                        dve.wait_ge(mod_ready, i + 1)
                    for k in range(j * KB // SPAN, (j + 1) * KB // SPAN):
                        src, c = ada[:, s, k * COLS:(k + 1) * COLS], silu_c[:, k:k + 1]
                        if k == 0:
                            ins = nc.vector.tensor_scalar(acc[:, s, :], src, c, None, ALU.mult)
                        else:
                            dve.wait_ge(acc_step, step + k)
                            ins = nc.vector.scalar_tensor_tensor(acc[:, s, :], src, c, acc[:, s, :],
                                                                 ALU.mult, ALU.add)
                        ins.then_inc(acc_step, 1)
                    if j == SPAN - 1:
                        dve.wait_ge(acc_step, step + KB)
                        dve.sem_inc(ada_used, 1)
                        dve.sem_inc(acc_ready, 1)

                def chunks(e, width, gate):
                    with nc.vector.Fori(0, ADA_X // 2) as r2:
                        for s in range(2):
                            for j in range(SPAN):
                                n = s * SPAN + j
                                c = e * FX + r2 * (2 * SPAN) + (base + n)
                                if gate is None:
                                    down_lo(n % 2, (STARTS[5] + n) % NS, c)
                                chunk(n % 2, c, width, gate)
                                ada_part(e, r2, s, j)
                    for j in range(FX - ADA_X * SPAN):
                        c = e * FX + (base + ADA_X * SPAN + j)
                        if gate is None:
                            down_lo(j % 2, (STARTS[5] + j) % NS, c)
                        chunk(j % 2, c, width, gate)

                dve.sem_inc(y_added, 1)
                with nc.vector.Fori(0, NE) as e:
                    is_wide = nc.vector.value_load(wide[0:1, bass.ds(e, 1)], min_val=0, max_val=1)
                    with nc.vector.If(is_wide == 1):
                        chunks(e, T, gates[:, bass.ds(e, 1), :].rearrange("p a t -> p (a t)"))
                        dve.sem_inc(hid_top_x, FX)
                        dve.sem_inc(down_lo_ready, FX)
                    with nc.vector.Else():
                        chunks(e, CAP, None)
                    dve.wait_ge(tile_used, e * FX + (STARTS[5] + FX))
                    for b in range(4):
                        dve.wait_ge(y_ready, e * 4 + (b + 1))
                        x2 = xT[:, 2 * b:2 * b + 2, :]
                        if b == 0:
                            dve.wait_ge(y_added, e * 4 + 1)
                        nc.vector.tensor_tensor(x2, x2, ps[:, b, :].rearrange("p (h t) -> p h t", h=2),
                                                ALU.add).then_inc(y_added, 1)

            def router():
                dve.wait_ge(logit_ready, 1)
                lg, t0, t1, oh1, oh2 = (rt[:, i, :, :] for i in range(5))
                m1, m2 = rt[:, 5, :, 0:1], rt[:, 6, :, 0:1]
                d, e2, g1, g2 = (rt[:, i, :, 0:1] for i in (7, 8, 9, 10))
                idx = rt[:, 11, :, 0:1]
                iota = C("iota").unsqueeze(1).broadcast_to([P, TT, NE])

                def bc(a):
                    return a.broadcast_to([P, TT, NE])

                def tt_(o, a, b, op):
                    after(dve, "dve", nc.vector.tensor_tensor(o, a, b, op))

                def first_max(mx, onehot):
                    after(dve, "dve", nc.vector.tensor_reduce(mx, lg, AX, ALU.max))
                    tt_(t0, lg, bc(mx), ALU.is_lt)
                    after(dve, "dve", nc.vector.tensor_scalar(t0, t0, 1000.0, None, ALU.mult))
                    tt_(t0, t0, iota, ALU.add)
                    after(dve, "dve", nc.vector.tensor_reduce(idx, t0, AX, ALU.min))
                    tt_(onehot, iota, bc(idx), ALU.is_equal)

                after(dve, "dve", nc.vector.tensor_copy(
                    lg, ps[:, 6, 0:TT * NE].rearrange("p (t e) -> p t e", t=TT)))
                first_max(m1, oh1)
                after(dve, "dve", nc.vector.tensor_scalar(t1, oh1, TAKEN, None, ALU.mult))
                tt_(lg, lg, t1, ALU.add)
                first_max(m2, oh2)
                nc.vector.tensor_tensor(d, m2, m1, ALU.subtract).then_inc(route_exp_in, 1)
                dve.wait_ge(route_exp, 1)
                after(dve, "dve", nc.vector.tensor_scalar(t0[:, :, 0:1], e2, 1.0, None, ALU.add))
                after(dve, "dve", nc.vector.reciprocal(g1, t0[:, :, 0:1]))
                tt_(g2, e2, g1, ALU.mult)
                nc.vector.tensor_tensor(lg, oh1, oh2, ALU.add).then_inc(mask_ready, 1)
                tt_(oh1, oh1, bc(g1), ALU.mult)
                tt_(oh2, oh2, bc(g2), ALU.mult)
                tt_(oh1, oh1, oh2, ALU.add)
                dve.wait_ge(mask_ready, 1)
                dve.wait_ge(pos_ready, 1)
                nc.vector.tensor_scalar(wide[:, :], ps[:, 7, TT * NE:(TT + 1) * NE], CAP + 0.5, None,
                                        ALU.is_gt).then_inc(wide_ready, 1)
                after(dve, "dve", nc.vector.tensor_copy(
                    t0, ps[:, 7, 0:TT * NE].rearrange("p (t e) -> p t e", t=TT)))
                for e in range(NE):
                    for tt in range(TT):
                        nc.vector.tensor_scalar(place[:, e, tt, :], C("slots"), rt[:, 1, tt, e:e + 1],
                                                rt[:, 0, tt, e:e + 1], ALU.is_equal, ALU.mult)\
                            .then_inc(place_ready, 1)
                        nc.vector.tensor_scalar(gplace[:, e, tt, :], C("slots"), rt[:, 1, tt, e:e + 1],
                                                rt[:, 3, tt, e:e + 1], ALU.is_equal, ALU.mult)\
                            .then_inc(place_ready, 1)
                for i in range(TT * NE):
                    e, tt = divmod(i, TT)
                    if i >= 2:
                        dve.wait_ge(gate_ready, i - 1)
                    nc.vector.tensor_scalar(diag[:, i % 2, :], C("ident"), rt[:, 3, tt, e:e + 1], None,
                                            ALU.mult).then_inc(diag_ready, 1)
                for b in range(4):
                    dve.wait_ge(gate_ready, 4 * b + 4)
                    after(dve, "dve", nc.vector.tensor_copy(
                        gates[:, 2 * b:2 * b + 2, :],
                        ps[:, b, :].rearrange("p (e t) -> p e t", e=2)))
                dve.sem_inc(gate_copied, 1)

            def modulation():
                dve.wait_ge(mod_ready, 2 * ADA + 2)
                dve.wait_ge(he_ready, NE + 1)
                rest = slice(ADA_F * FB, 2 * MODB)
                half = NE // 2 * ADA_X * FB
                after(dve, "dve", nc.vector.tensor_tensor(
                    mod_all[:, rest].rearrange("p (h b) -> p h b", h=2), ps[:, 6:8, MOD_AT:MOD_AT + half],
                    V("b_ada", ADA_F * FB, 2 * half).rearrange("p (h b) -> p h b", h=2), ALU.add))
                for n in range(6):
                    l, j = divmod(n, 3)
                    scale = mod[:, l, (3 * j + 1) * KB:(3 * j + 2) * KB]
                    after(dve, "dve", nc.vector.scalar_tensor_tensor(
                        gs[:, n, :], scale, 1.0, V("norm_g", n * KB, KB), ALU.add, ALU.mult))
                    after(dve, "dve", nc.vector.tensor_scalar(
                        hg[:, n, :], mod[:, l, (3 * j + 2) * KB:(3 * j + 3) * KB],
                        1.0 if j == 1 else 0.5, None, ALU.mult))
                for i in range(8):
                    after(dve, "dve", nc.vector.tensor_scalar(
                        qkg[:, i:i + 1], V("qk_g", i), HD ** -0.5 if i % 2 == 0 else 1.0, None, ALU.mult))
                dve.sem_inc(mod_done, 1)

            dve.wait_ge(silu_c_ready, 1)
            def tiles_first(stage):
                return [lambda i=i: lo_tiles(stage, [i]) for i in range(2)]

            def chunks_first(f):
                return [lambda c=c: lo_first(f, c) for c in range(2)]

            norm(0, *tiles_first(0))
            mixer1(0)
            residual(0)
            norm(1, *chunks_first(0))
            ffn(0, FF)
            residual(1)
            norm(2, *tiles_first(IN_STAGE[1]))
            mixer1(1)
            residual(2)
            norm(3)
            router()
            moe()
            dve.wait_ge(y_added, 4 * NE + 1)
            dve.sem_inc(x_ready, KB)
            modulation()
            norm(4, *chunks_first(2))
            for l in range(2):
                norm(5 + 3 * l, *(chunks_first(4) if l else ()))
                ffn(2 + 2 * l, FF)
                residual(4 + 3 * l, 3 * l)
                norm(6 + 3 * l, *tiles_first(IN_STAGE[2 + l]))
                mixer2(2 + l)
                residual(5 + 3 * l, 3 * l + 1)
                norm(7 + 3 * l, *chunks_first(3 + 2 * l))
                ffn(3 + 2 * l, FF)
                residual(6 + 3 * l, 3 * l + 2)

        @block.tensor
        def _(pe):
            mm = nc.tensor.matmul
            pe.wait_ge(loaded, 16 * 5)
            pe.wait_ge(const_set, 4)

            def mm3(o, stationary, moving, start, stop):
                mm(o, stationary[0], moving[0], start=start, stop=False, skip_group_check=True)
                mm(o, stationary[0], moving[1], start=False, stop=False, skip_group_check=True)
                return mm(o, stationary[1], moving[0], start=False, stop=stop, skip_group_check=True)

            def parts(stage, i, a, b):
                q = (SPLITS[stage] + i) % 2
                return w_hi[:, q, a:b], w_lo[:, q, a:b]

            def wait_half(stage, i, k):
                if k % (KB // 2) == 0:
                    pe.wait_ge(split_ready, 2 * (SPLITS[stage] + i) + k // (KB // 2) + 1)

            def wait_input(name, k):
                pe.wait_ge(as_ready, KB * SPLIT_INPUTS.index(name) + k + 1)

            def norm(n):
                pe.wait_ge(sqsum_ready, n + 1)
                mm(SS[:, 0:T], ones[:, :], sq[:, 0, :], start=True, stop=True).then_inc(ss_ready, 1)

            def wait_h(n, k):
                pe.wait_ge(h_ready, KB * n + k + 1)

            def inproj(m, n):
                u = UNITS_BEFORE[m]
                stage = IN_STAGE[m]
                feats = IN1_F if m < 2 else IN2_F
                for i in range(feats):
                    if m >= 2 and i == 5:
                        pe.wait_ge(qsq_ready, m - 1)
                        head_sums(qss_ready, sq, range(KB))
                    for b in range(FB):
                        if u >= 4:
                            pe.wait_ge(in_copied, u - 3)
                        for k in range(KB):
                            if b == 0:
                                wait_half(stage, i, k)
                                if i == 0:
                                    wait_input(f"n{n}", k)
                            at = k * COLS + b * P
                            ins = mm3(ps[:, u % 4, 0:T], parts(stage, i, at, at + P),
                                      (a_hi[:, k, :], a_lo[:, k, :]), k == 0, k == KB - 1)
                        last = unit_tile(m, u - UNITS_BEFORE[m])[1]
                        ins.then_inc(split_used if last else in_ready, 1)
                        u += 1
                for i, cols in enumerate(IN1_V if m < 2 else IN2_V, feats):
                    for tt in range(TT):
                        pe.wait_ge(in_copied, u - 3)
                        for k in range(KB):
                            if tt == 0:
                                wait_half(stage, i, k)
                            tokens = slice(tt * P, (tt + 1) * P)
                            ins = mm3(ps[:, u % 4, 0:cols], (a_hi[:, k, tokens], a_lo[:, k, tokens]),
                                      parts(stage, i, k * COLS, k * COLS + cols), k == 0, k == KB - 1)
                        last = unit_tile(m, u - UNITS_BEFORE[m])[1]
                        ins.then_inc(split_used if last else in_ready, 1)
                        u += 1

            def outproj(m):
                stage = IN_STAGE[m] + 1
                for i in range(OUTP):
                    for b in range(min(FB, KB - i * FB)):
                        for k in range(KB):
                            if b == 0:
                                wait_half(stage, i, k)
                                if i == 0:
                                    wait_input(f"c{m}", k)
                            at = k * COLS + b * P
                            ins = mm3(Y[:, i * FB + b, :], parts(stage, i, at, at + P),
                                      (a_hi[:, k, :], a_lo[:, k, :]), k == 0, k == KB - 1)
                    ins.then_inc(split_used, 1)

            def scores(u, tt, qb, kb):
                nk = P * (tt + 1)
                if u:
                    pe.wait_ge(s_used, u)
                for h in range(4):
                    r = (h % 2) * HD
                    ins = mm(ps[:, h % 2, (h // 2) * T:(h // 2) * T + nk],
                             proj[r:r + HD, qb + h // 2, tt * P:(tt + 1) * P],
                             proj[r:r + HD, kb + h // 2, 0:nk], start=True, stop=True)
                ins.then_inc(s_ready, 1)

            def values(u, tt, v0):
                pe.wait_ge(p_ready, u + 1)
                for i in range(4):
                    for kt in range(tt + 1):
                        at = (i % 2) * T + kt * P
                        ins = nc.tensor.transpose(ps[:, 2 + i // 2, at:at + P],
                                                  sm2[u % 2][:, i, kt * P:(kt + 1) * P], C("ident"))
                ins.then_inc(pt_ready, 1)
                pe.wait_ge(pt_copied, u + 1)
                if u >= 2:
                    pe.wait_ge(o_copied, u - 1)
                for h in range(4):
                    r = (h % 2) * HD
                    for kt in range(tt + 1):
                        ins = mm(ps[r:r + HD, 4 + u % 2, (h // 2) * P:(h // 2 + 1) * P],
                                 vtok[:, kt, v0 + h * HD:v0 + (h + 1) * HD], pT[:, 2 * (h % 2) + h // 2, kt, :],
                                 start=kt == 0, stop=kt == tt)
                ins.then_inc(o_ready, 1)

            def attend(m, q0, k0):
                step = 4 if m >= 2 else 2
                for u in range(-1, 4):
                    if u < 2:
                        v = u + 2
                        scores(4 * m + v, v % 2, q0 + step * (v // 2), k0 + step * (v // 2))
                    if u >= 0:
                        values(4 * m + u, u % 2, 256 * (u // 2))
                    if m >= 2 and u in (-1, 1, 3):
                        part = (u + 1) // 2
                        pe.wait_ge(csq_ready, 2 + 3 * (m - 2) + part + 1)
                        head_sums(css_ready, cat_sq, ((4, 5, 6, 7), (0, 1), (2, 3))[part],
                                  part == 0, part == 2)

            def mixer1(m, n):
                inproj(m, n)
                pe.wait_ge(in_copied, UNITS_BEFORE[m + 1])
                scores(4 * m, 0, 4, 8)
                pe.wait_ge(d_ready, m + 1)
                for g in range(4):
                    ins = mm(ps[:, 6 + g // 2, (g % 2) * T:(g % 2 + 1) * T], wp[:, 4 * m + g, :],
                             sq[:, g, :], start=True, stop=True)
                    if g % 2:
                        ins.then_inc(z_ready, 1)
                attend(m, 4, 8)
                pe.wait_ge(csqsum_ready, m + 1)
                for g in range(2):
                    ins = mm(SS[:, g * T:(g + 1) * T], ones[:, :], sq[:, 4 * g, :], start=True, stop=True)
                ins.then_inc(css_ready, 1)
                outproj(m)

            def head_sums(ready, squares, blocks, first=True, last=True):
                for i, b in enumerate(blocks):
                    ins = mm(SS[0:16, 0:T], C("headsel")[:, b * 16:(b + 1) * 16], squares[:, b, :],
                             start=first and i == 0, stop=last and i == len(blocks) - 1,
                             skip_group_check=True)
                if last:
                    ins.then_inc(ready, 1)

            def head_spread(n):
                pe.wait_ge(root_ready, n)
                for b in range(KB):
                    ins = mm(Y[:, b, :], C("spread")[0:16, b * P:(b + 1) * P], norm_s[0:16, 1, :],
                             start=True, stop=True)
                    if b % 2:
                        ins.then_inc(spread_ready, 1)

            def mixer2(m, n):
                l = m - 2
                inproj(m, n)
                pe.wait_ge(in_copied, UNITS_BEFORE[m + 1])
                head_spread(2 * l + 1)
                for j, (b, w) in enumerate(PAIRS):
                    i = len(PAIRS) * l + j
                    pe.wait_ge(qk_ready, 8 * l + min(b + w, 8))
                    if i >= 2:
                        pe.wait_ge(rope_ready, i - 1)
                    mm(ps[:, 6 + i % 2, 0:w * T], C("rot"), proj[:, b:b + w, :], start=True, stop=True)\
                        .then_inc(rot_ready, 1)
                pe.wait_ge(rope_ready, len(PAIRS) * (l + 1))
                for i in range(16):
                    nn = 16 * l + i
                    tt, j = divmod(i, 8)
                    r = (j % 2) * HD
                    if nn >= 2:
                        pe.wait_ge(ir_ready, nn - 1)
                    mm(ps[:, 6 + nn % 2, 0:P * (tt + 1)], proj[r:r + HD, 8 + j // 2, tt * P:(tt + 1) * P],
                       proj[r:r + HD, 12, 0:P * (tt + 1)], start=True, stop=True).then_inc(il_ready, 1)
                def logits(h):
                    nn = 8 * l + h
                    r, b = (h % 2) * HD, h // 2
                    if h >= 2:
                        pe.wait_ge(sp_ready, nn - 1)
                    z = ps[:, nn % 2, :]
                    mm(z[:, 0:T], proj[r:r + HD, 17 + b, 0:P], proj[r:r + HD, 13 + b, :],
                       start=True, stop=True)
                    mm(z[:, T:T + P], proj[r:r + HD, 17 + b, P:T], proj[r:r + HD, 13 + b, P:T],
                       start=True, stop=True).then_inc(zt_ready, 1)

                def weigh(h):
                    nn = 8 * l + h
                    r, b = (h % 2) * HD, h // 2
                    pe.wait_ge(a_ready, nn + 1)
                    if h % 2 == 0:
                        if b >= 2:
                            pe.wait_ge(co_copied, 4 * l + b - 1)
                    o = ps[r:r + HD, 4 + b % 2, :]
                    v0 = 512 + h * HD
                    mm(o[:, 0:T], vtok[:, 0, v0:v0 + HD], st_d[:, nn % 2, 3, 0:T], start=True, stop=False)
                    mm(o[:, P:T], vtok[:, 1, v0:v0 + HD], st_d[:, nn % 2, 3, T:T + P], start=False,
                       stop=True).then_inc(co_ready, 1)

                logits(0)
                for h in range(9):
                    nn = 8 * l + h
                    if h < 7:
                        logits(h + 1)
                    if h < 8:
                        pe.wait_ge(spm_ready, nn + 1)
                        if h >= 2:
                            pe.wait_ge(arg_ready, nn - 1)
                        a = ps[:, 2 + nn % 2, :]
                        spm = st_d[:, nn % 2, 2, :]
                        mm(a[:, 0:T], C("after"), spm[:, 0:T], start=True, stop=False)
                        mm(a[:, P:T], ones[:, :], spm[:, T:T + P], start=False, stop=True)
                        mm(a[:, T:T + P], C("after"), spm[:, T:T + P], start=True, stop=True)\
                            .then_inc(af_ready, 1)
                    if h > 0:
                        weigh(h - 1)
                pe.wait_ge(sp_ready, 8 * (l + 1))
                pe.wait_ge(arg_ready, 8 * (l + 1))
                scores(4 * m, 0, 0, 2)
                pe.wait_ge(co_copied, 4 * (l + 1))
                attend(m, 0, 2)
                head_spread(2 * l + 2)
                outproj(m)

            def ffn(f, n, norm_n):
                base, stage = chunks_before(f), FFN_STAGE[f]
                q0 = SPLITS[stage]

                def up(c, r=0):
                    pe.wait_ge(split_ready, r * 2 + (2 * q0 + up_part(c) + 1))
                    if base + c >= 2:
                        pe.wait_ge(hid_ready, r + (base + c - 1))
                    for g in range(2):
                        for k in range(KB):
                            if c == 0 and g == 0:
                                wait_input(f"n{norm_n}", k)
                            at = (g * KB + k) * P
                            ins = mm3(ps[:, 4 + c % 2, g * T:(g + 1) * T], parts(stage, c, at, at + P),
                                      (a_hi[:, k, :], a_lo[:, k, :]), k == 0, k == KB - 1)
                    ins.then_inc(gu_ready, 1)

                def down(c, r=0):
                    pe.wait_ge(hid_ready, r + (base + c + 1))
                    pe.wait_ge(split_ready, r * 2 + (2 * q0 + down_part(c, n) + 1))
                    for d in range(KB):
                        at = UP + d * P
                        ins = mm3(Y[:, d, :], parts(stage, c, at, at + P),
                                  (hid_hi[:, c % 2, :], hid_lo[:, c % 2, :]),
                                  c == 0 and d % 2 == 0, c == n - 1)
                    ins.then_inc(split_used, 1)

                def ada_sums(i, r=0):
                    if f:
                        return
                    pe.wait_ge(acc_ready, r + (i + 1))
                    for j in range(FB):
                        ins = mm(ps[:, 7, bass.ds(r * FB + (i * FB + j), 1)] if i >= 3 else
                                 ps[:, 7, i * FB + j:i * FB + j + 1],
                                 acc_f[:, i % 3, j * P:(j + 1) * P], ones[:, 0:1], start=True, stop=True)
                    ins.then_inc(mod_ready, 1)

                lead, rounds = ffn_loop(n)
                assert f or (lead == 5 and ADA_F == 3 + 3 * rounds + 1)
                if f == 0:
                    pe.sem_inc(mod_ready, 2)
                up(0)
                for c in range(1, lead):
                    up(c)
                    down(c - 1)
                    if c >= 2:
                        ada_sums(c - 2)
                with nc.tensor.Fori(0, rounds) as r:
                    for j in range(NS):
                        up(lead + j, r * NS)
                        down(lead + j - 1, r * NS)
                        if j:
                            ada_sums(3 + j - 1, r * 3)
                up(n - 1)
                down(n - 2)
                down(n - 1)
                ada_sums(ADA_F - 1)

            def router():
                for tt in range(TT):
                    for k in range(KB):
                        if tt == 0:
                            wait_h(3, k)
                        ins = mm(ps[:, 6, tt * NE:(tt + 1) * NE], hT[:, k, tt * P:(tt + 1) * P],
                                 wr[:, k, :], start=k == 0, stop=k == KB - 1)
                ins.then_inc(logit_ready, 1)
                for i in range(4):
                    if i >= 2:
                        pe.wait_ge(ht_copied, i - 1)
                    for j in range(4):
                        ins = nc.tensor.transpose(ps[:, 4 + i % 2, j * P:(j + 1) * P],
                                                  hT[:, 4 * (i % 2) + j, (i // 2) * P:(i // 2 + 1) * P],
                                                  C("ident"))
                    ins.then_inc(ht_ready, 1)
                pe.wait_ge(mask_ready, 1)
                m0, m1 = rt[:, 0, 0, :], rt[:, 0, 1, :]
                before = C("strict")[:, 0:P]
                mm(ps[:, 7, 0:NE], before, m0, start=True, stop=True)
                mm(ps[:, 7, NE:2 * NE], before, m1, start=True, stop=False)
                mm(ps[:, 7, NE:2 * NE], ones[:, :], m0, start=False, stop=True)
                mm(ps[:, 7, 2 * NE:3 * NE], ones[:, :], m0, start=True, stop=False)
                mm(ps[:, 7, 2 * NE:3 * NE], ones[:, :], m1, start=False, stop=True).then_inc(pos_ready, 1)
                for i in range(4):
                    pe.wait_ge(ht_copied, min(4, 3 + i))
                    if i >= 2:
                        pe.wait_ge(gp_copied, i - 1)
                    for j in range(4):
                        e, tt = 2 * i + j // 2, j % 2
                        pe.wait_ge(place_ready, 4 * e + 2 * tt + 2)
                        ins = nc.tensor.transpose(ps[0:CAP, 4 + i % 2, j * P:(j + 1) * P],
                                                  gplace[:, e, tt, :], C("ident"))
                    ins.then_inc(gp_ready, 1)
                for i in range(TT * NE):
                    e, tt = divmod(i, TT)
                    pe.wait_ge(diag_ready, i + 1)
                    at = (e % 2) * T + tt * P
                    mm(ps[:, e // 2, at:at + P], ones[:, :], diag[:, i % 2, :], start=True, stop=True)\
                        .then_inc(gate_ready, 1)
                pe.wait_ge(gate_copied, 1)
                pe.wait_ge(gp_copied, 4)

            def moe():
                base = chunks_before(1)
                t0 = STARTS[5]
                assert FX % NS == 0
                def up(s, c, n_in, act_in, width):
                    pe.wait_ge(tile_in[s], n_in)
                    w = ring[:, s, 0:2 * KB * P].rearrange("p (g k f) -> p g k f", g=2, k=KB)
                    b = (s - t0) % 2
                    pe.wait_ge(hid_ready, c - 1)
                    for g in range(2):
                        for k in range(KB):
                            ins = mm(ps[:, 4 + b, g * width:(g + 1) * width], w[:, g, k, :], act_in[:, k, :],
                                     start=k == 0, stop=k == KB - 1)
                    ins.then_inc(gu_ready, 1)

                def down(s, c, wide_path, first=False):
                    pe.wait_ge(hid_ready, c + 1)
                    b = (s - t0) % 2
                    if wide_path:
                        w = ring[:, s, UP:].rearrange("p (d f) -> p d f", d=KB)
                        for d in range(KB):
                            ins = mm(Y[:, d, :], w[:, d, :], hid[:, b, :], start=first and d % 2 == 0,
                                     stop=False, skip_group_check=True)
                    else:
                        pe.wait_ge(down_lo_ready, c + (1 - base))
                        for n, (h, w) in enumerate(((hid_hi, wd_hi), (hid_hi, wd_lo), (hid_lo, wd_hi))):
                            for half in range(2):
                                ins = mm(ps[0:CAP, half, :], h[:, b, 0:CAP],
                                         w[:, b, half * D // 2:(half + 1) * D // 2],
                                         start=first and n == 0, stop=False, skip_group_check=True)
                    ins.then_inc(tile_used, 1)

                def ada_sums(e, half, e4, r2, b):
                    pe.wait_ge(acc_ready, e * ADA_X + r2 * 2 + (ADA_F + b + 1))
                    for f in range(FB):
                        column = e4 * (ADA_X * FB) + r2 * (2 * FB) + (MOD_AT + b * FB + f)
                        ins = mm(ps[:, bass.ds(half + 6, 1), bass.ds(column, 1)]
                                 .rearrange("p a c -> p (a c)"),
                                 acc[:, b, f * P:(f + 1) * P], ones[:, 0:1], start=True, stop=True)
                    ins.then_inc(mod_ready, 1)

                def expert(e, half, e4, wide_path):
                    act_in, width = (hT, T) if wide_path else (he, CAP)

                    def at(c):
                        i = t0 + c
                        return i % NS, e * FX + (base + c), e * (16 * FX // NS) + 16 * (i // NS + 1)

                    lead = NS
                    for c in range(lead):
                        s, n, n_in = at(c)
                        up(s, n, n_in, act_in, width)
                        if c:
                            if c == 1:
                                pe.wait_ge(y_added, e * 4 + 1)
                            s, n, _ = at(c - 1)
                            down(s, n, wide_path, first=c == 1)
                    with nc.tensor.Fori(0, ADA_X // 2) as r:
                        for j in range(2 * SPAN):
                            s, n, n_in = at(lead + j)
                            up(s, r * (2 * SPAN) + n, r * (16 * 2 * SPAN // NS) + n_in, act_in, width)
                            s, n, _ = at(lead + j - 1)
                            down(s, r * (2 * SPAN) + n, wide_path)
                            if j % SPAN == SPAN - 1:
                                ada_sums(e, half, e4, r, j // SPAN)
                    s, n, _ = at(FX - 1)
                    down(s, n, wide_path)

                assert 2 * SPAN % NS == 0 and FX == NS + ADA_X * SPAN
                pe.wait_ge(wide_ready, 1)
                pe.wait_ge(place_ready, 2 * NE * TT)

                def gather(n):
                    for k in range(KB):
                        for tt in range(TT):
                            ins = mm(ps[:, 6 + k // 4, (k % 4) * CAP:(k % 4 + 1) * CAP],
                                     htok[:, tt, k * P:(k + 1) * P],
                                     place_next[:, bass.ds(n, 1), tt, :].rearrange("p a c -> p (a c)"),
                                     start=tt == 0, stop=tt == TT - 1)
                    ins.then_inc(he_gathered, 1)

                gather(0)
                with nc.tensor.Fori(0, 2) as half, nc.tensor.Fori(0, NE // 2) as e4:
                    e = half * (NE // 2) + e4
                    is_wide = nc.tensor.value_load(wide[0:1, bass.ds(e, 1)], min_val=0, max_val=1)
                    pe.wait_ge(he_ready, e + 1)
                    with nc.tensor.If(is_wide == 1):
                        expert(e, half, e4, True)
                        nc.tensor.sem_inc(y_ready, 4)
                        gather(e + 1)
                    with nc.tensor.Else():
                        expert(e, half, e4, False)
                        gather(e + 1)
                        pe.wait_ge(ye_ready, e + 1)
                        for d in range(KB):
                            ins = mm(Y[:, d, :], ye[:, d * P:(d + 1) * P],
                                     scatter[:, bass.ds(e, 1), :].rearrange("p a t -> p (a t)"),
                                     start=d % 2 == 0, stop=True, skip_group_check=True)
                            if d % 2:
                                ins.then_inc(y_ready, 1)

            norm(0)
            mixer1(0, 0)
            norm(1)
            ffn(0, FF, 1)
            norm(2)
            mixer1(1, 2)
            norm(3)
            router()
            moe()
            norm(4)
            for l in range(2):
                norm(5 + 3 * l)
                ffn(2 + 2 * l, FF, 5 + 3 * l)
                norm(6 + 3 * l)
                mixer2(2 + l, 6 + 3 * l)
                norm(7 + 3 * l)
                ffn(3 + 2 * l, FF, 7 + 3 * l)


def _proj_tiles(w):
    f = w.shape[1]
    n = -(-f // COLS)
    w = np.pad(w, ((0, 0), (0, n * COLS - f)))
    return w.reshape(KB, P, n, COLS).transpose(2, 1, 0, 3).reshape(n, P, TILE)


def _ffn_tiles(wg, wu, wd):
    n = wg.shape[1] // P
    g = wg.reshape(KB, P, n, P).transpose(2, 1, 0, 3).reshape(n, P, D)
    u = wu.reshape(KB, P, n, P).transpose(2, 1, 0, 3).reshape(n, P, D)
    return np.concatenate([g, u, wd.reshape(n, P, D)], axis=2)


def _col(v):
    return np.asarray(v).reshape(-1, P).T


def _constants():
    c = np.zeros((P, N_CONST), np.float32)

    def put(name, a):
        at, w = CONST[name]
        c[:, at:at + w] = a.reshape(P, w)

    i = np.arange(P)
    t = np.arange(T)
    put("ident", np.eye(P))
    sel = np.zeros((P, KB, 16))
    for b in range(KB):
        sel[i, b, 2 * b + i // HD] = 1.0
    put("headsel", sel)
    spread = np.zeros((P, KB, P))
    spread[0:16] = sel.transpose(2, 1, 0)
    put("spread", spread)
    rot = np.zeros((P, P))
    for h in range(0, P, HD):
        for a in range(8):
            rot[h + a + 8, h + a] = -1.0
            rot[h + a, h + a + 8] = 1.0
    put("rot", rot)
    put("after", (i[:, None] > i[None, :]).astype(np.float32))
    for tt in range(TT):
        q = tt * P + i[:, None]
        k = np.arange(P * (tt + 1))[None, :]
        d = q - k
        put(f"cmask{tt}", np.where(d >= 0, 0.0, NEG))
        put(f"mult{tt}", sum(((d >= 0) & (d <= w) & (d % s == 0)).astype(np.float32)
                             for w, s in ((128, 1), (512, 4), (2048, 16))))
    put("strict", np.concatenate([(i[:, None] < t[None, :]), (P + i[:, None] < t[None, P:])], axis=1)
        .astype(np.float32))
    inv = np.float32(500000.0) ** (-np.arange(0, 16, 2, dtype=np.float32) / np.float32(16))
    ang = t.astype(np.float32)[:, None] * inv.astype(np.float32)[None, :]
    cos, sin = np.ones((P, T), np.float32), np.zeros((P, T), np.float32)
    for h in range(0, P, HD):
        for a in range(16):
            cos[h + a], sin[h + a] = np.cos(ang[:, a % 8]), np.sin(ang[:, a % 8])
    put("cos", cos)
    put("sin", sin)
    put("invcnt", np.broadcast_to(np.concatenate([1.0 / np.minimum(t[:16] + 1, w) for w in (2, 4, 8, 16)]),
                                  (P, 4 * 16)))
    put("iota", np.broadcast_to(np.arange(NE), (P, NE)))
    put("slots", np.broadcast_to(np.arange(CAP), (P, CAP)))
    return c


def kernel(**inputs):
    import concourse.bacc as bacc
    from concourse.bass_utils import run_bass_kernel_spmd

    a = {k: np.asarray(v) for k, v in inputs.items()}

    stream = np.empty((N_TILES, P, TILE), np.float32)
    at = 0

    def add(tiles):
        nonlocal at
        stream[at:at + len(tiles)] = tiles
        at += len(tiles)

    for l in range(2):
        add(_proj_tiles(a["w_in"][l]))
        add(_proj_tiles(a["w_out"][l]))
        if l == 0:
            add(_ffn_tiles(a["ffn_wg"][0], a["ffn_wu"][0], a["ffn_wd"][0]))
        else:
            for e in range(NE):
                add(_ffn_tiles(a["moe_wg"][0, e], a["moe_wu"][0, e], a["moe_wd"][0, e]))
    for l in range(2):
        w = a["w_in_2"][l]
        qa, ka, va, qb, kb, vb, qi, ki, wi, qc, kc, vc = np.split(
            w, np.cumsum([256, 256, 256, 256, 256, 256, 512, 64, 8, 512, 512]), axis=1)
        w = np.concatenate([qa, ka, qb, kb, qi, ki, ki, qc, kc, va, vb, vc, wi], axis=1)
        f = (a["ffn_w1_2"][l], a["ffn_w3_2"][l], a["ffn_w2_2"][l])
        add(_ffn_tiles(*(x[0] for x in f)))
        add(_proj_tiles(w))
        add(_proj_tiles(a["w_out_2"][l]))
        add(_ffn_tiles(*(x[1] for x in f)))
    assert at == N_TILES
    astream = np.concatenate([_proj_tiles(a["w_ada_2"][l]) for l in range(2)])

    cat_g = np.concatenate([np.concatenate([a["pool_scale"][l], a["attn_gain"][l]]) for l in range(2)])
    qk = np.concatenate([np.tile(a["qk_g_2"], (1, 1, 2)).reshape(-1)])
    vectors = np.concatenate([_col(v) for v in (
        a["norm_mix"], a["norm_ffn"], a["final_norm"], cat_g, a["norm_g_2"], a["out_g_2"], qk,
        a["b_ada_2"], a["c_2"])], axis=1)
    host = {
        "x_in": a["x"][0].T.reshape(KB, P, T).transpose(1, 0, 2),
        "wstream": stream,
        "astream": astream,
        "wpool": a["w_pool"].reshape(8, P, P).transpose(1, 0, 2),
        "wrouter": a["w_router"][0].reshape(KB, P, NE).transpose(1, 0, 2),
        "vectors": vectors,
        "consts": _constants(),
    }
    host = {k: np.ascontiguousarray(v) for k, v in host.items()}
    nc = bacc.Bacc("TRN2", target_bir_lowering=False, num_devices=1)
    args = {k: nc.dram_tensor(k, v.shape, mybir.dt.float32, kind="ExternalInput").ap()
            for k, v in host.items()}
    out = nc.dram_tensor("out", (P, KB, T), mybir.dt.float32, kind="ExternalOutput").ap()
    build(nc, out=out, **args)
    r = run_bass_kernel_spmd(nc, [host], core_ids=[0])
    y = r.results[0]["out"]
    return y.transpose(1, 0, 2).reshape(1, D, T).transpose(0, 2, 1)
```
